# Optimizing a Trainium2 kernel written in Bass

```python
import jax, jax.numpy as jnp
from jax import lax
import numpy as np

D_MODEL = 1024
BATCH = 1
SEQ = 256
DEPTH = 1
DEC_BATCH = 1
DEC_SEQ = 1024
PAST_LEN = 128

GRID_W = 64
Q_BLOCK = 128
ROPE_THETA = 10000.0
NORM_EPS = 1e-6
GQA_HEADS = 8
GQA_KV_HEADS = 2
GQA_HEAD_DIM = 64
MLA_HEADS = 8
MLA_Q_RANK = 256
MLA_KV_RANK = 128
MLA_NOPE_DIM = 64
MLA_ROPE_DIM = 32
MLA_V_DIM = 64
GQA_WIDTH = GQA_HEADS * GQA_HEAD_DIM
MLA_WIDTH = MLA_HEADS * MLA_V_DIM
MIX_WIDTH = GQA_WIDTH + MLA_WIDTH
IN_SPLITS = (GQA_WIDTH, GQA_KV_HEADS * GQA_HEAD_DIM, GQA_KV_HEADS * GQA_HEAD_DIM, MLA_Q_RANK, MLA_KV_RANK, MLA_ROPE_DIM)
IN_WIDTH = sum(IN_SPLITS)
D_FF = -(-8 * D_MODEL // (3 * 256)) * 256

kernel_name = 'hymba_gqa_mla_deepnorm_adaln_encoder'

def _rms_norm(x, g):
    xf = x.astype(jnp.float32)
    y = xf * lax.rsqrt(jnp.mean(xf * xf, axis=-1, keepdims=True) + NORM_EPS)
    return (y * g.astype(jnp.float32)).astype(x.dtype)

def _layer_norm(x, g=None, b=None):
    xf = x.astype(jnp.float32)
    xc = xf - jnp.mean(xf, axis=-1, keepdims=True)
    y = xc * lax.rsqrt(jnp.mean(xc * xc, axis=-1, keepdims=True) + NORM_EPS)
    if g is not None:
        y = y * g.astype(jnp.float32) + b.astype(jnp.float32)
    return y.astype(x.dtype)

def _axial_rope(seq_len, rot_dim):
    rows = seq_len // GRID_W
    row = jnp.repeat(jnp.arange(rows, dtype=jnp.float32), GRID_W)
    col = jnp.tile(jnp.arange(GRID_W, dtype=jnp.float32), rows)
    n = rot_dim // 4
    inv_freq = 1.0 / jnp.power(ROPE_THETA, jnp.arange(n, dtype=jnp.float32) / n)
    ang = jnp.concatenate([row[:, None] * inv_freq, col[:, None] * inv_freq], axis=-1)
    return jnp.cos(ang), jnp.sin(ang)

def _apply_rope(x, cos, sin):
    xf = x.astype(jnp.float32)
    half = x.shape[-1] // 2
    x1, x2 = xf[..., :half], xf[..., half:]
    c = cos[None, :, None, :]
    s = sin[None, :, None, :]
    return jnp.concatenate([x1 * c - x2 * s, x1 * s + x2 * c], axis=-1).astype(x.dtype)

def _block_attention(q, k, v, scale):
    B, S, KV, G, dq = q.shape
    dv = v.shape[-1]
    nb = S // Q_BLOCK
    qb = q.reshape(B, nb, Q_BLOCK, KV, G, dq).transpose(1, 0, 2, 3, 4, 5)

    def one_block(q_blk):
        s = jnp.einsum('bqkgd,bskd->bkgqs', q_blk, k).astype(jnp.float32) * scale
        p = jax.nn.softmax(s, axis=-1).astype(v.dtype)
        return jnp.einsum('bkgqs,bskd->bqkgd', p, v)

    o = lax.map(one_block, qb)
    return o.transpose(1, 0, 2, 3, 4, 5).reshape(B, S, KV * G * dv)

def _encoder_layer(x, c, rope_a, rope_b, w_ada, b_ada, w_in, gqa_q_norm, gqa_k_norm,
                   mla_q_norm, w_uq, mla_kv_norm, w_ukv, grp_norm_a, grp_norm_b, w_out,
                   ln1_g, ln1_b, w_gate, w_up, w_down, ln2_g, ln2_b):
    B, S, _ = x.shape
    alpha = (2.0 * DEPTH) ** 0.25
    mod = jax.nn.silu(c) @ w_ada + b_ada
    sh1, sc1, g1, sh2, sc2, g2 = [m[:, None, :] for m in jnp.split(mod, 6, axis=-1)]

    u = _layer_norm(x) * (1 + sc1) + sh1
    h = u @ w_in
    offs = [int(o) for o in np.cumsum(IN_SPLITS)[:-1]]
    q_a, k_a, v_a, q_lat, kv_lat, k_rope = jnp.split(h, offs, axis=-1)

    q_a = _apply_rope(_rms_norm(q_a.reshape(B, S, GQA_HEADS, GQA_HEAD_DIM), gqa_q_norm), *rope_a)
    k_a = _apply_rope(_rms_norm(k_a.reshape(B, S, GQA_KV_HEADS, GQA_HEAD_DIM), gqa_k_norm), *rope_a)
    v_a = v_a.reshape(B, S, GQA_KV_HEADS, GQA_HEAD_DIM)
    q_a = q_a.reshape(B, S, GQA_KV_HEADS, GQA_HEADS // GQA_KV_HEADS, GQA_HEAD_DIM)
    o_a = _block_attention(q_a, k_a, v_a, GQA_HEAD_DIM ** -0.5)

    q_m = (_rms_norm(q_lat, mla_q_norm) @ w_uq).reshape(B, S, MLA_HEADS, MLA_NOPE_DIM + MLA_ROPE_DIM)
    q_nope = q_m[..., :MLA_NOPE_DIM]
    q_pe = _apply_rope(q_m[..., MLA_NOPE_DIM:], *rope_b)
    kv = (_rms_norm(kv_lat, mla_kv_norm) @ w_ukv).reshape(B, S, MLA_HEADS, MLA_NOPE_DIM + MLA_V_DIM)
    k_nope, v_m = kv[..., :MLA_NOPE_DIM], kv[..., MLA_NOPE_DIM:]
    k_pe = _apply_rope(k_rope[:, :, None, :], *rope_b)
    k_m = jnp.concatenate([k_nope, jnp.broadcast_to(k_pe, (B, S, MLA_HEADS, MLA_ROPE_DIM))], axis=-1)
    q_m = jnp.concatenate([q_nope, q_pe], axis=-1)[:, :, :, None, :]
    o_m = _block_attention(q_m, k_m, v_m, (MLA_NOPE_DIM + MLA_ROPE_DIM) ** -0.5)

    mix = jnp.concatenate([_rms_norm(o_a, grp_norm_a), _rms_norm(o_m, grp_norm_b)], axis=-1) @ w_out
    x = _layer_norm(alpha * x + g1 * mix, ln1_g, ln1_b)

    u2 = _layer_norm(x) * (1 + sc2) + sh2
    f = (jax.nn.silu(u2 @ w_gate) * (u2 @ w_up)) @ w_down
    return _layer_norm(alpha * x + g2 * f, ln2_g, ln2_b)

def _trunk(x, c, params):
    S = x.shape[1]
    rope_a = _axial_rope(S, GQA_HEAD_DIM)
    rope_b = _axial_rope(S, MLA_ROPE_DIM)
    for l in range(DEPTH):
        x = _encoder_layer(x, c, rope_a, rope_b, *[p[l] for p in params])
    return x

def setup_inputs(seed: int = 0) -> dict:
    key = jax.random.key(seed)
    ks = jax.random.split(key, 24)
    beta = (8.0 * DEPTH) ** -0.25

    def dense(k, shape, fan_in, mult=1.0):
        return jax.random.normal(k, shape, jnp.float32) * (fan_in ** -0.5) * mult

    def gain(k, n):
        return 1.0 + 0.1 * jax.random.normal(k, (DEPTH, n), jnp.float32)

    def bias(k, n):
        return 0.02 * jax.random.normal(k, (DEPTH, n), jnp.float32)

    return {
        'x_prompt': jax.random.normal(ks[0], (BATCH, SEQ, D_MODEL), jnp.float32),
        'x_sample': jax.random.normal(ks[1], (DEC_BATCH, DEC_SEQ, D_MODEL), jnp.float32),
        'c_prompt': jax.random.normal(ks[2], (BATCH, D_MODEL), jnp.float32),
        'c_sample': jax.random.normal(ks[3], (DEC_BATCH, D_MODEL), jnp.float32),
        'w_ada': dense(ks[4], (DEPTH, D_MODEL, 6 * D_MODEL), D_MODEL, 0.5),
        'b_ada': bias(ks[5], 6 * D_MODEL),
        'w_in': dense(ks[6], (DEPTH, D_MODEL, IN_WIDTH), D_MODEL),
        'gqa_q_norm': gain(ks[7], GQA_HEAD_DIM),
        'gqa_k_norm': gain(ks[8], GQA_HEAD_DIM),
        'mla_q_norm': gain(ks[9], MLA_Q_RANK),
        'w_uq': dense(ks[10], (DEPTH, MLA_Q_RANK, MLA_HEADS * (MLA_NOPE_DIM + MLA_ROPE_DIM)), MLA_Q_RANK),
        'mla_kv_norm': gain(ks[11], MLA_KV_RANK),
        'w_ukv': dense(ks[12], (DEPTH, MLA_KV_RANK, MLA_HEADS * (MLA_NOPE_DIM + MLA_V_DIM)), MLA_KV_RANK),
        'grp_norm_a': gain(ks[13], GQA_WIDTH),
        'grp_norm_b': gain(ks[14], MLA_WIDTH),
        'w_out': dense(ks[15], (DEPTH, MIX_WIDTH, D_MODEL), MIX_WIDTH, beta),
        'ln1_g': gain(ks[16], D_MODEL),
        'ln1_b': bias(ks[17], D_MODEL),
        'w_gate': dense(ks[18], (DEPTH, D_MODEL, D_FF), D_MODEL),
        'w_up': dense(ks[19], (DEPTH, D_MODEL, D_FF), D_MODEL),
        'w_down': dense(ks[20], (DEPTH, D_FF, D_MODEL), D_FF, beta),
        'ln2_g': gain(ks[21], D_MODEL),
        'ln2_b': bias(ks[22], D_MODEL),
    }

def reference(x_prompt, x_sample, c_prompt, c_sample, w_ada, b_ada, w_in, gqa_q_norm, gqa_k_norm,
              mla_q_norm, w_uq, mla_kv_norm, w_ukv, grp_norm_a, grp_norm_b, w_out,
              ln1_g, ln1_b, w_gate, w_up, w_down, ln2_g, ln2_b):
    params = (w_ada, b_ada, w_in, gqa_q_norm, gqa_k_norm, mla_q_norm, w_uq, mla_kv_norm, w_ukv,
              grp_norm_a, grp_norm_b, w_out, ln1_g, ln1_b, w_gate, w_up, w_down, ln2_g, ln2_b)
    y_prompt = _trunk(x_prompt, c_prompt, params)
    y_sample = _trunk(x_sample, c_sample, params)
    return (y_prompt, y_sample)


_drawn_inputs = setup_inputs


def setup_inputs(seed=0):
    import zlib

    import numpy as np

    out = dict(_drawn_inputs(seed))
    spreads = {}
    factors = {'b_ada': 3.548,
     'gqa_q_norm': 8.0,
     'gqa_k_norm': 8.0,
     'mla_q_norm': 8.0,
     'mla_kv_norm': 4.025,
     'grp_norm_a': 5.232,
     'grp_norm_b': 5.749,
     'ln1_b': 2.883,
     'ln2_b': 2.851}
    for name, (base, spread) in spreads.items():
        noise = np.random.default_rng([zlib.crc32(name.encode()), seed]).standard_normal(out[name].shape)
        drawn = base * np.exp(spread * noise) if base else spread * noise
        out[name] = __import__('jax').numpy.asarray(drawn.astype(out[name].dtype))
    for name, factor in factors.items():
        out[name] = (out[name] * factor).astype(out[name].dtype)
    return out
```

```python
import concourse.bass as bass
from concourse import mybir
from contextlib import ExitStack

F32 = mybir.dt.float32
F32R = mybir.dt.float32r
ALU = mybir.AluOpType
ACT = mybir.ActivationFunctionType
AX = mybir.AxisListType

P = 128
D = 1024
KT = D // P
S_PROMPT, S_SAMPLE = 256, 1024
TOK = S_PROMPT + S_SAMPLE
NT = TOK // P
NTP = S_PROMPT // P
EPS = 1e-6
HA, KVA, DA = 8, 2, 64
HM, NOPE, ROPE, VD = 8, 64, 32, 64
DM = NOPE + ROPE
RQ, RKV = 256, 128
QK_A = (HA + KVA) * DA
C_VA = QK_A
C_QL = C_VA + KVA * DA
C_KVL = C_QL + RQ
C_KR = C_KVL + RKV
W_IN = C_KR + ROPE
BANKS_H = [(0, 384), (384, 768), (768, W_IN)]
FF = 2816
NF = FF // P
ALPHA = 2.0 ** 0.25
STOP = 0
CHUNKS = [(0, 256), (256, 768), (768, 1280)]


def rows(ap, n=P):
    return ap.rearrange("(t p) m -> p t m", p=n)


class Link:

    def __init__(self, eng, sem, start=0):
        self.eng, self.sem, self.n = eng, sem, start

    def __call__(self, ins):
        self.n += 1
        ins.then_inc(self.sem, 1)
        self.eng.wait_ge(self.sem, self.n)


class Kernel:
    def __init__(self, nc, ctx, ins, outs):
        self.nc, self.ctx = nc, ctx
        self.i, self.o = ins, outs
        self.names = set()

    def sem(self, name):
        return self.ctx.enter_context(self.nc.semaphore(name))

    def sb(self, stage, name, shape, dt=F32):
        return stage.enter_context(self.nc.sbuf_tensor(name, shape, dt))

    def dram(self, name, shape):
        return self.nc.dram_tensor(name, shape, F32, kind="Internal").ap()


def encoder_layer(nc, ins, outs):
    ctx = ExitStack()
    with ctx:
        k = Kernel(nc, ctx, ins, outs)
        k.bank = [ctx.enter_context(nc.psum_tensor(f"pair{b}", [P, 2, 512], F32)) for b in range(4)]
        k.ident = k.sb(ctx, "ident", [P, P])
        k.eps = k.sb(ctx, "eps", [P, 1])
        k.mod = k.dram("mod_rows", [2, 6 * D])
        k.qa_t = k.dram("qa_t", [HA * DA, TOK])
        k.ka_t = k.dram("ka_t", [KVA * DA, TOK])
        k.va = k.dram("va", [TOK, KVA * DA])
        k.qm_t = k.dram("qm_t", [HM * DM, TOK])
        k.kn_t = k.dram("kn_t", [HM * NOPE, TOK])
        k.kr_t = k.dram("kr_t", [ROPE, TOK])
        k.vm = k.dram("vm", [TOK, HM * VD])
        k.o = k.dram("o", [TOK, D])
        k.x1 = k.dram("x1", [TOK, D])
        k.o_prompt = lambda t: outs["y_prompt"][0, t * P:(t + 1) * P, :]
        k.o_sample = lambda t: outs["y_sample"][0, t * P:(t + 1) * P, :]
        with ExitStack() as weights:
            k.win = [k.sb(weights, f"w_in_{s}", [P, KT, W_IN], F32R) for s in ("hi", "lo")]
            k.wuq = [k.sb(weights, f"w_uq_{s}", [P, RQ // P, HM * DM], F32R) for s in ("hi", "lo")]
            k.wukv = [k.sb(weights, f"w_ukv_{s}", [P, HM * (NOPE + VD)], F32R) for s in ("hi", "lo")]
            with ExitStack() as stage:
                modulation(k, stage)
            if STOP == 1:
                return
            with ExitStack() as stage:
                projections(k, stage)
        if STOP == 2:
            return
        with ExitStack() as stage:
            attention(k, stage)
        if STOP == 3:
            return
        with ExitStack() as stage:
            k.u2 = [k.sb(stage, f"u2_{s}", [P, KT, TOK], F32R) for s in ("hi", "lo")]
            with ExitStack() as inner:
                output(k, inner)
            if STOP == 4:
                return
            channel(k, stage)


def bank(k, n):
    return k.bank[n // 2][:, n % 2, :]


def xrow(k, t):
    if t < NTP:
        return k.i["x_prompt"][0, t * P:(t + 1) * P, :]
    return k.i["x_sample"][0, (t - NTP) * P:(t - NTP + 1) * P, :]


def three(pe, out, a, b, start, stop):
    pe.matmul(out, a[0], b[0], start=start, stop=False)
    pe.matmul(out, a[0], b[1], start=False, stop=False)
    return pe.matmul(out, a[1], b[0], start=False, stop=stop)


def modulation(k, stage):
    nc = k.nc
    NC = 6 * D // 512
    RING = 3
    c_t = k.sb(stage, "c_t", [P, KT, 2])
    silu_c = k.sb(stage, "silu_c", [P, KT, 2])
    wa = k.sb(stage, "w_ada_ring", [P, RING, KT, 512])
    bias = k.sb(stage, "b_ada_rows", [2, 2, 512])
    mrow = k.sb(stage, "mod_chunk", [2, 2, 512])
    raw = k.sb(stage, "w_raw", [P, 2, W_IN])
    c_in, ident_in = k.sem("c_in"), k.sem("ident_in")
    wa_in = [k.sem(f"wa_in{s}") for s in range(RING)]
    b_in = [k.sem(f"b_ada_in{s}") for s in range(2)]
    raw_in = [k.sem(f"raw_in{s}") for s in range(2)]
    c_ready, mod_done, mod_sum = k.sem("c_ready"), k.sem("mod_done"), k.sem("mod_sum")
    mod_out = [k.sem(f"mod_out{s}") for s in range(2)]
    hi_done, lo_done = k.sem("w_hi_done"), k.sem("w_lo_done")

    pieces = [(rows(k.i["w_in"][0])[:, j, :], k.win[0][:, j, :], k.win[1][:, j, :]) for j in range(KT)]
    pieces += [(rows(k.i["w_uq"][0])[:, j, :], k.wuq[0][:, j, :], k.wuq[1][:, j, :]) for j in range(RQ // P)]
    pieces += [(k.i["w_ukv"][0], k.wukv[0][:, :], k.wukv[1][:, :])]

    with nc.Block() as block:
        @block.sync
        def _(sp):
            for s, c in enumerate(("c_prompt", "c_sample")):
                with nc.allow_non_contiguous_dma(reason="two short vectors"):
                    sp.dma_start(c_t[:, :, s:s + 1], k.i[c][0:1, :].rearrange("a (p j) -> p j a", j=KT)).then_inc(c_in, 16)
            wsrc = k.i["w_ada"][0].rearrange("(p j) n -> p j n", j=KT)
            for n in range(NC):
                if n >= RING:
                    sp.wait_ge(mod_done, n - RING + 1)
                sp.dma_start(wa[:, n % RING, :, :], wsrc[:, :, n * 512:(n + 1) * 512]).then_inc(wa_in[n % RING], 16)

        @block.gpsimd
        def _(pool):
            pool.memset(k.eps[:, :], EPS)
            pool.dma_start(k.ident[:, :], k.i["ident"]).then_inc(ident_in, 16)
            for m, (src, hi, lo) in enumerate(pieces):
                if m >= 2:
                    pool.wait_ge(lo_done, m - 1)
                pool.dma_start(raw[:, m % 2, :hi.shape[-1]], src).then_inc(raw_in[m % 2], 16)
            pool.wait_ge(ident_in, 16)

        @block.tensor
        def _(pe):
            pe.wait_ge(c_ready, 1)
            for n in range(NC):
                pe.wait_ge(wa_in[n % RING], 16 * (n // RING + 1))
                if n >= 8:
                    pe.wait_ge(mod_sum, n - 7)
                for j in range(KT):
                    mm = pe.matmul(bank(k, n % 8)[0:2, :], silu_c[:, j, :], wa[:, n % RING, j, :],
                                   start=j == 0, stop=j == KT - 1)
                mm.then_inc(mod_done, 1)

        @block.scalar
        def _(act):
            act.wait_ge(c_in, 32)
            act.activation(silu_c[:, :, :], c_t[:, :, :], ACT.Silu).then_inc(c_ready, 1)
            assert len(pieces) <= NC
            for n in range(NC):
                if n < len(pieces):
                    act.wait_ge(raw_in[n % 2], 16 * (n // 2 + 1))
                    hi = pieces[n][1]
                    act.activation(hi, raw[:, n % 2, :hi.shape[-1]], ACT.Copy).then_inc(hi_done, 1)
                if n >= 2:
                    act.wait_ge(mod_sum, n - 1)
                src = k.i["b_ada"][0:1, n * 512:(n + 1) * 512]
                for s in range(2):
                    act.dma_start(bias[s:s + 1, n % 2, :], src).then_inc(b_in[n % 2], 16)
                if n >= 1:
                    act.wait_ge(mod_sum, n)
                    act.dma_start(k.mod[:, (n - 1) * 512:n * 512], mrow[:, (n - 1) % 2, :]).then_inc(mod_out[(n - 1) % 2], 16)
            act.wait_ge(mod_sum, NC)
            act.dma_start(k.mod[:, (NC - 1) * 512:], mrow[:, (NC - 1) % 2, :]).then_inc(mod_out[(NC - 1) % 2], 16)
            for s in range(2):
                act.wait_ge(mod_out[s], 16 * (NC // 2))

        @block.vector
        def _(dve):
            def split(m):
                src, hi, lo = pieces[m]
                dve.wait_ge(hi_done, m + 1)
                dve.tensor_tensor(lo, raw[:, m % 2, :hi.shape[-1]], hi, ALU.subtract).then_inc(lo_done, 1)

            for n in range(NC):
                if n < len(pieces):
                    split(n)
                dve.wait_ge(mod_done, n + 1)
                dve.wait_ge(b_in[n % 2], 32 * (n // 2 + 1))
                if n >= 2:
                    dve.wait_ge(mod_out[n % 2], 16 * (n // 2))
                dve.tensor_tensor(mrow[:, n % 2, :], bank(k, n % 8)[0:2, :], bias[:, n % 2, :], ALU.add).then_inc(mod_sum, 1)
            for m in range(NC, len(pieces)):
                split(m)


def projections(k, stage):
    nc = k.nc
    sb = lambda name, shape, dt=F32: k.sb(stage, name, shape, dt)
    xt = sb("x_tile", [P, 2, D])
    stats = sb("x_stats", [P, 2, 12])
    mv = sb("x_mean_var", [P, 2, 2])
    std = sb("x_std", [P, 2, 1])
    xh = sb("x_hat", [P, 2, D])
    uf = sb("u_t", [P, KT, P])
    u = [sb(f"u_{s}", [P, 2, KT, P], F32R) for s in ("hi", "lo")]
    modt = sb("mod_in_t", [P, 2, 2, KT])
    hs = sb("h", [P, 2, W_IN])
    sq = sb("squares", [P, C_KR])
    ssq = sb("norm_sums", [P, 12])
    inv_n = sb("inv_n", [P, 12])
    rn = sb("norm_factors", [P, 12])
    gain_qk = sb("gain_qk", [P, 2, DA])
    gain_lat = sb("gain_lat", [P, RQ + RKV])
    tab = sb("rope_tables", [P, S_SAMPLE // P, 96])
    qk = sb("qk", [P, QK_A])
    rot = sb("qk_rotated", [P, QK_A])
    qkr = sb("qk_out", [P, 2, QK_A + ROPE])
    lat = sb("latents", [P, 2, RQ + RKV])
    latf = sb("latents_t", [P, 3, P])
    lath = [sb(f"latents_t_{s}", [P, 3, P], F32R) for s in ("hi", "lo")]
    qms = sb("q_mla", [P, 2, HM * DM])
    mrot = sb("q_mla_rotated", [P, HM, ROPE])
    kvs = sb("kv_mla", [P, 2, 2, HM * NOPE])
    q_tr = sb("qa_tr", [P, 4, P])
    k_tr = sb("ka_tr", [P, 2, P])
    qm_tr = sb("qm_tr", [DM, HM, P])
    kn_tr = sb("kn_tr", [P, 4, P])

    x_in = [k.sem(f"pj_x_in{s}") for s in range(2)]
    tabs_in, mod_in, modp = k.sem("tabs_in"), k.sem("mod_in"), k.sem("mod_plus_one")
    var_ready, std_ready, xhat_ready = k.sem("pj_var"), k.sem("pj_std"), k.sem("pj_xhat")
    t_ready, t_free = k.sem("pj_t_ready"), k.sem("pj_t_free")
    uf_ready, u_ready = k.sem("uf_ready"), k.sem("pj_u_ready")
    h_ready, h_free = k.sem("h_ready"), k.sem("h_free")
    qm_ready, qm_free, kv_ready, kv_free = (k.sem(n) for n in ("qm_ready", "qm_free", "kv_ready", "kv_free"))
    sums_ready, root_ready = k.sem("sums_ready"), k.sem("root_ready")
    qk_ready, lat_ready, latf_ready, lath_ready = (k.sem(n) for n in ("qk_ready", "lat_ready", "latf_ready", "lath_ready"))
    qm_roped = k.sem("qm_roped")
    sq_done = k.sem("sq_done")
    out_v, out_q, out_k, out_qm, out_kn, out_vm = ([k.sem(f"{n}{s}") for s in range(2)] for n in ("out_va", "out_qa", "out_ka", "out_qm", "out_kn", "out_vm"))
    dv, pl = k.sem("pj_dve_link"), k.sem("pj_pool_link")

    def tcols(t):
        return slice(t * P, (t + 1) * P)

    def groups(n):
        return ([0, 1] if n < NT else []) + ([2, 3, 4] if 0 <= n - 2 < NT else []) + ([5, 6, 7] if 0 <= n - 3 < NT else [])

    order = [(n, g) for n in range(NT + 3) for g in groups(n)]
    number = {ng: m for m, ng in enumerate(order)}

    with nc.Block() as block:
        @block.sync
        def _(sp):
            with nc.allow_non_contiguous_dma(reason="modulation columns, once"):
                for s in range(2):
                    for m, part in enumerate((1, 0)):
                        sp.dma_start(modt[:, s, m, :], k.mod[s, part * D:(part + 1) * D].rearrange("(j p) -> p j", p=P)).then_inc(mod_in, 16)
            for t in range(2):
                sp.dma_start(xt[:, t, :], xrow(k, t)).then_inc(x_in[t], 16)
            sp.dma_start(tab[:, :, :], rows(k.i["rope"])).then_inc(tabs_in, 16)
            sp.dma_start(inv_n[:, :], k.i["inv_n"].partition_broadcast(P)).then_inc(tabs_in, 16)
            for m, g in enumerate(("gqa_q_norm", "gqa_k_norm")):
                sp.dma_start(gain_qk[:, m, :], k.i[g][0, :].partition_broadcast(P)).then_inc(tabs_in, 16)
            sp.dma_start(gain_lat[:, 0:RQ], k.i["mla_q_norm"][0, :].partition_broadcast(P)).then_inc(tabs_in, 16)
            sp.dma_start(gain_lat[:, RQ:], k.i["mla_kv_norm"][0, :].partition_broadcast(P)).then_inc(tabs_in, 16)
            for n in range(NT + 3):
                if n + 2 < NT:
                    sp.wait_ge(xhat_ready, n + 1)
                    sp.dma_start(xt[:, n % 2, :], xrow(k, n + 2)).then_inc(x_in[n % 2], 16)
                t = n - 1
                if 0 <= t < NT:
                    sp.wait_ge(h_free, 3 * (t + 1))
                    sp.dma_start(k.va[tcols(t), :], hs[:, t % 2, C_VA:C_QL]).then_inc(out_v[t % 2], 16)
                t = n - 2
                if 0 <= t < NT:
                    sp.wait_ge(t_free, number[n, 3] + 1)
                    sp.dma_start(rows(k.qa_t)[:, :, tcols(t)], q_tr[:, :, :]).then_inc(out_q[0], 16)
                    sp.wait_ge(t_free, number[n, 4] + 1)
                    sp.dma_start(k.ka_t[:, tcols(t)], k_tr[:, 0, :]).then_inc(out_k[0], 16)
                    sp.dma_start(k.kr_t[:, tcols(t)], k_tr[0:ROPE, 1, :]).then_inc(out_k[0], 16)
                t = n - 3
                if 0 <= t < NT:
                    sp.wait_ge(t_free, number[n, 6] + 1)
                    sp.dma_start(rows(k.qm_t, DM)[:, :, tcols(t)], qm_tr[:, :, :]).then_inc(out_qm[0], 16)
                    sp.wait_ge(t_free, number[n, 7] + 1)
                    sp.dma_start(rows(k.kn_t)[:, :, tcols(t)], kn_tr[:, :, :]).then_inc(out_kn[0], 16)
                t = n - 2
                if 0 <= t < NT:
                    sp.wait_ge(kv_free, 2 * (t + 1))
                    sp.dma_start(k.vm[tcols(t), :], kvs[:, t % 2, 1, :]).then_inc(out_vm[t % 2], 16)
            for s in range(2):
                sp.wait_ge(out_v[s], 16 * (NT // 2))
                sp.wait_ge(out_vm[s], 16 * (NT // 2))
            sp.wait_ge(out_q[0], 16 * NT)
            sp.wait_ge(out_k[0], 32 * NT)
            sp.wait_ge(out_qm[0], 16 * NT)
            sp.wait_ge(out_kn[0], 16 * NT)

        @block.tensor
        def _(pe):
            def transposes(n, g, blocks):
                m = number[n, g]
                if m >= 2:
                    pe.wait_ge(t_free, m - 1)
                for q, src in enumerate(blocks):
                    mm = pe.transpose(bank(k, m % 2)[0:cols_of(src), q * P:(q + 1) * P], src, k.ident[:, :])
                mm.then_inc(t_ready, 1)

            def h_bank(t, b):
                lo, hi = BANKS_H[b]
                if t >= 1:
                    pe.wait_ge(h_free, 3 * (t - 1) + b + 1)
                out = bank(k, 2 + b)[:, 0:hi - lo]
                for j in range(KT):
                    mm = three(pe, out, [u[0][:, t % 2, j, :], u[1][:, t % 2, j, :]],
                               [w[:, j, lo:hi] for w in k.win], j == 0, j == KT - 1)
                mm.then_inc(h_ready, 1)

            for n in range(NT + 3):
                a, b, c = n - 1, n - 2, n - 3
                if n < NT:
                    pe.wait_ge(xhat_ready, n + 1)
                    for g in range(2):
                        transposes(n, g, [xh[:, n % 2, (4 * g + q) * P:(4 * g + q + 1) * P] for q in range(4)])
                if 0 <= a < NT:
                    pe.wait_ge(u_ready, a + 1)
                    h_bank(a, 0)
                if 0 <= b < NT:
                    pe.wait_ge(lat_ready, b + 1)
                    transposes(n, 2, [lat[:, b % 2, q * P:(q + 1) * P] for q in range(3)])
                if 0 <= a < NT:
                    h_bank(a, 1)
                if 0 <= b < NT:
                    pe.wait_ge(qk_ready, b + 1)
                    transposes(n, 3, [qkr[:, b % 2, q * P:(q + 1) * P] for q in range(4)])
                    transposes(n, 4, [qkr[:, b % 2, 4 * P:5 * P], qkr[:, b % 2, QK_A:QK_A + ROPE]])
                if 0 <= a < NT:
                    h_bank(a, 2)
                if 0 <= b < NT:
                    pe.wait_ge(lath_ready, b + 1)
                    for half in range(2):
                        if b >= 1:
                            pe.wait_ge(kv_free, 2 * (b - 1) + half + 1)
                        out = bank(k, 6 + half)[:, 0:4 * DM]
                        for j in range(RQ // P):
                            mm = three(pe, out, [w[:, j, :] for w in lath],
                                       [w[:, j, half * 4 * DM:(half + 1) * 4 * DM] for w in k.wuq], j == 0, j == RQ // P - 1)
                        mm.then_inc(qm_ready, 1)
                if 0 <= c < NT:
                    pe.wait_ge(qm_roped, c + 1)
                    for g in range(2):
                        transposes(n, 5 + g, [qms[:, c % 2, (4 * g + q) * DM:(4 * g + q + 1) * DM] for q in range(4)])
                    transposes(n, 7, [kvs[:, c % 2, 0, q * P:(q + 1) * P] for q in range(4)])
                if 0 <= b < NT:
                    for half in range(2):
                        pe.wait_ge(qm_free, 2 * b + half + 1)
                        mm = three(pe, bank(k, 6 + half), [w[:, 2, :] for w in lath],
                                   [w[:, :].rearrange("p (h c) -> p h c", h=HM)[:, :, half * NOPE:(half + 1) * NOPE] for w in k.wukv],
                                   True, True)
                        mm.then_inc(kv_ready, 1)

        @block.scalar
        def _(act):
            def take(n, g):
                act.wait_ge(t_ready, number[n, g] + 1)
                return bank(k, number[n, g] % 2)

            for n in range(NT + 3):
                a, b, c = n - 1, n - 2, n - 3
                if n < NT:
                    act.wait_ge(var_ready, n + 1)
                    act.activation(std[:, n % 2, :], mv[:, n % 2, 1:2], ACT.Sqrt, bias=k.eps[:, 0:1]).then_inc(std_ready, 1)
                    if n == 0:
                        act.wait_ge(modp, 1)
                    if n >= 1:
                        act.wait_ge(u_ready, n)
                    seq = 0 if n < NTP else 1
                    for g in range(2):
                        src = take(n, g)
                        for q in range(4):
                            j = 4 * g + q
                            mm = act.activation(uf[:, j, :], src[:, q * P:(q + 1) * P], ACT.Identity,
                                                bias=modt[:, seq, 1, j:j + 1], scale=modt[:, seq, 0, j:j + 1])
                            if q < 3:
                                mm.then_inc(uf_ready, 1)
                        mm.then_inc(t_free, 1)
                if 0 <= b < NT:
                    src = take(n, 2)
                    if b >= 1:
                        act.wait_ge(lath_ready, b)
                    act.activation(latf[:, :, :], src[:, 0:3 * P].rearrange("p (q c) -> p q c", c=P), ACT.Copy).then_inc(t_free, 1)

                def h_copy(m):
                    lo, hi = BANKS_H[m]
                    act.wait_ge(h_ready, 3 * a + m + 1)
                    if m == 0 and a >= 2:
                        act.wait_ge(out_v[a % 2], 16 * (a // 2))
                        act.wait_ge(qk_ready, a - 1)
                        act.wait_ge(lat_ready, a - 1)
                    act.activation(hs[:, a % 2, lo:hi], bank(k, 2 + m)[:, 0:hi - lo], ACT.Copy).then_inc(h_free, 1)

                if 0 <= a < NT:
                    h_copy(0)
                    h_copy(1)
                if 0 <= b < NT:
                    src = take(n, 3)
                    if b >= 1:
                        act.wait_ge(out_q[0], 16 * b)
                    act.activation(q_tr[:, :, :], src.rearrange("p (q c) -> p q c", c=P), ACT.Copy).then_inc(t_free, 1)
                    src = take(n, 4)
                    if b >= 1:
                        act.wait_ge(out_k[0], 32 * b)
                    act.activation(k_tr[:, 0, :], src[:, 0:P], ACT.Copy).then_inc(uf_ready, 1)
                    act.activation(k_tr[0:ROPE, 1, :], src[0:ROPE, P:2 * P], ACT.Copy).then_inc(t_free, 1)
                if 0 <= a < NT:
                    h_copy(2)
                    act.wait_ge(sums_ready, a + 1)
                    act.activation(rn[:, :], ssq[:, :], ACT.Sqrt, bias=k.eps[:, 0:1]).then_inc(root_ready, 1)
                if 0 <= b < NT:
                    for half in range(2):
                        act.wait_ge(qm_ready, 2 * b + half + 1)
                        if half == 0 and b >= 2:
                            act.wait_ge(t_free, number[b - 2 + 3, 6] + 1)
                            act.wait_ge(t_ready, number[b - 2 + 3, 6] + 1)
                        act.activation(qms[:, b % 2, half * 4 * DM:(half + 1) * 4 * DM], bank(k, 6 + half)[:, 0:4 * DM], ACT.Copy).then_inc(qm_free, 1)
                if 0 <= c < NT:
                    if c >= 1:
                        act.wait_ge(out_qm[0], 16 * c)
                    for g in range(2):
                        src = take(n, 5 + g)
                        act.activation(qm_tr[:, 4 * g:4 * g + 4, :], src[0:DM, :].rearrange("p (q c) -> p q c", c=P), ACT.Copy).then_inc(t_free, 1)
                    src = take(n, 7)
                    if c >= 1:
                        act.wait_ge(out_kn[0], 16 * c)
                    act.activation(kn_tr[:, :, :], src.rearrange("p (q c) -> p q c", c=P), ACT.Copy).then_inc(t_free, 1)
                if 0 <= b < NT:
                    for half in range(2):
                        act.wait_ge(kv_ready, 2 * b + half + 1)
                        if half == 1 and b >= 2:
                            act.wait_ge(out_vm[b % 2], 16 * (b // 2))
                        act.activation(kvs[:, b % 2, half, :], bank(k, 6 + half)[:, :], ACT.Copy).then_inc(kv_free, 1)

        @block.gpsimd
        def _(pool):
            for t in range(NT):
                pool.wait_ge(h_free, 3 * (t + 1))
                if t >= 1:
                    pool.wait_ge(sums_ready, t)
                pool.tensor_tensor(sq[:, 0:QK_A], hs[:, t % 2, 0:QK_A], hs[:, t % 2, 0:QK_A], ALU.mult).then_inc(pl, 1)
                pool.tensor_tensor(sq[:, C_QL:C_KR], hs[:, t % 2, C_QL:C_KR], hs[:, t % 2, C_QL:C_KR], ALU.mult).then_inc(sq_done, 1)

        @block.vector
        def _(dve):
            link = Link(dve, dv)

            def rope(out, x, cos, sin, heads, w, tmp):
                c2 = cos[:, None, None, :].to_broadcast([P, heads, 2, w])
                s1 = sin[:, None, :].to_broadcast([P, heads, w])
                link(dve.tensor_tensor(tmp[:, :, 0:w], x[:, :, w:2 * w], s1, ALU.mult))
                link(dve.tensor_tensor(tmp[:, :, w:2 * w], x[:, :, 0:w], s1, ALU.mult))
                link(dve.tensor_tensor(x.rearrange("p h (a c) -> p h a c", a=2), x.rearrange("p h (a c) -> p h a c", a=2), c2, ALU.mult))
                link(dve.tensor_tensor(out[:, :, 0:w], x[:, :, 0:w], tmp[:, :, 0:w], ALU.subtract))
                return dve.tensor_tensor(out[:, :, w:2 * w], x[:, :, w:2 * w], tmp[:, :, w:2 * w], ALU.add)

            dve.wait_ge(mod_in, 64)
            for s in range(2):
                m = dve.tensor_scalar(modt[:, s, 0, :], modt[:, s, 0, :], 1.0, None, ALU.add)
                if s == 0:
                    link(m)
            m.then_inc(modp, 1)
            for n in range(NT + 3):
                a, b = n - 1, n - 2
                if n < NT:
                    dve.wait_ge(x_in[n % 2], 16 * (n // 2 + 1))
                    for q in range(2):
                        link(dve.bn_stats(stats[:, n % 2, 6 * q:6 * q + 6], xt[:, n % 2, q * 512:(q + 1) * 512]))
                    dve.bn_aggr(mv[:, n % 2, :], stats[:, n % 2, :]).then_inc(var_ready, 1)
                    dve.wait_ge(std_ready, n + 1)
                    dve.wait_ge(var_ready, n + 1)
                    link(dve.reciprocal(std[:, n % 2, :], std[:, n % 2, :]))
                    if n >= 2:
                        dve.wait_ge(t_ready, number[n - 2, 1] + 1)
                    dve.tensor_scalar(xh[:, n % 2, :], xt[:, n % 2, :], mv[:, n % 2, 0:1], std[:, n % 2, :], ALU.subtract, ALU.mult).then_inc(xhat_ready, 1)
                    dve.wait_ge(t_free, number[n, 1] + 1)
                    if n >= 2:
                        dve.wait_ge(h_ready, 3 * (n - 1))
                    link(dve.tensor_copy(u[0][:, n % 2, :, :], uf[:, :, :]))
                    dve.tensor_tensor(u[1][:, n % 2, :, :], uf[:, :, :], u[0][:, n % 2, :, :], ALU.subtract).then_inc(u_ready, 1)
                if 0 <= b < NT:
                    dve.wait_ge(t_free, number[n, 2] + 1)
                    if b >= 1:
                        dve.wait_ge(kv_ready, 2 * b)
                    link(dve.tensor_copy(lath[0][:, :, :], latf[:, :, :]))
                    dve.tensor_tensor(lath[1][:, :, :], latf[:, :, :], lath[0][:, :, :], ALU.subtract).then_inc(lath_ready, 1)
                if n == 1:
                    dve.wait_ge(tabs_in, 96)
                if 0 <= a < NT:
                    h = hs[:, a % 2, :]
                    pos = a if a < NTP else a - NTP
                    dve.wait_ge(sq_done, a + 1)
                    dve.wait_ge(pl, a + 1)
                    if a >= 1:
                        dve.wait_ge(root_ready, a)
                    heads = HA + KVA
                    link(dve.reduce_sum(ssq[:, 0:heads], sq[:, 0:QK_A].rearrange("p (h c) -> p h c", c=DA), AX.X))
                    link(dve.reduce_sum(ssq[:, heads:heads + 1], sq[:, C_QL:C_KVL], AX.X))
                    link(dve.reduce_sum(ssq[:, heads + 1:heads + 2], sq[:, C_KVL:C_KR], AX.X))
                    dve.tensor_tensor(ssq[:, :], ssq[:, :], inv_n[:, :], ALU.mult).then_inc(sums_ready, 1)
                    dve.wait_ge(root_ready, a + 1)
                    link(dve.reciprocal(rn[:, :], rn[:, :]))
                    if a >= 2:
                        dve.wait_ge(t_ready, number[a - 2 + 2, 2] + 1)
                    link(dve.scalar_tensor_tensor(lat[:, a % 2, 0:RQ], h[:, C_QL:C_KVL], rn[:, heads:heads + 1], gain_lat[:, 0:RQ], ALU.mult, ALU.mult))
                    dve.scalar_tensor_tensor(lat[:, a % 2, RQ:], h[:, C_KVL:C_KR], rn[:, heads + 1:heads + 2], gain_lat[:, RQ:], ALU.mult, ALU.mult).then_inc(lat_ready, 1)
                    qk3 = qk[:, :].rearrange("p (h c) -> p h c", c=DA)
                    link(dve.tensor_tensor(qk3, h[:, 0:QK_A].rearrange("p (h c) -> p h c", c=DA), rn[:, 0:heads, None].to_broadcast([P, heads, DA]), ALU.mult))
                    link(dve.tensor_tensor(qk3[:, 0:HA, :], qk3[:, 0:HA, :], gain_qk[:, 0:1, :].to_broadcast([P, HA, DA]), ALU.mult))
                    link(dve.tensor_tensor(qk3[:, HA:, :], qk3[:, HA:, :], gain_qk[:, 1:2, :].to_broadcast([P, KVA, DA]), ALU.mult))
                    if a >= 2:
                        dve.wait_ge(t_ready, number[a, 4] + 1)
                    link(rope(qkr[:, a % 2, 0:QK_A].rearrange("p (h c) -> p h c", c=DA), qk3, tab[:, pos, 0:32], tab[:, pos, 32:64],
                              heads, DA // 2, rot[:, :].rearrange("p (h c) -> p h c", c=DA)))
                    rope(qkr[:, a % 2, QK_A:].rearrange("p (h c) -> p h c", h=1), h[:, C_KR:].rearrange("p (h c) -> p h c", h=1),
                         tab[:, pos, 64:80], tab[:, pos, 80:96], 1, ROPE // 2, mrot[:, 0:1, :]).then_inc(qk_ready, 1)
                if 0 <= b < NT:
                    pos = b if b < NTP else b - NTP
                    dve.wait_ge(qm_free, 2 * (b + 1))
                    if a < NT:
                        dve.wait_ge(qk_ready, a + 1)
                    x = qms[:, b % 2, :].rearrange("p (h c) -> p h c", c=DM)[:, :, NOPE:]
                    rope(x, x, tab[:, pos, 64:80], tab[:, pos, 80:96], HM, ROPE // 2, mrot[:, :, :]).then_inc(qm_roped, 1)



def cols_of(src):
    n = 1
    for s in src.shape[1:]:
        n *= s
    return n


def attention(k, stage):
    nc = k.nc
    sb = lambda name, shape, dt=F32: k.sb(stage, name, shape, dt)
    H = HA + HM
    RING = 3
    UNITS = 1 + S_SAMPLE // P
    PS = 3
    LAG = 2
    qf = sb("q_f32", [P, TOK])
    kf = sb("k_f32", [P, TOK])
    vf = sb("v_f32", [P, NT, VD])
    qs = [sb(f"q_{s}", [P, RING, TOK], F32R) for s in ("a", "b")]
    ks = [sb(f"k_{s}", [P, RING, TOK], F32R) for s in ("a", "b")]
    VC = VD + 2
    vs = [sb(f"v_{s}", [P, RING, NT, VC], F32R) for s in ("hi", "lo")]
    pf = sb("p_f32", [P, PS, 1024])
    ph = [sb(f"p_{s}", [P, PS, 1024], F32R) for s in ("hi", "lo")]
    mcol = sb("max_col", [P, NT])
    mrow = sb("neg_max_row", [NT, P], F32R)
    oc = sb("o_t", [VD + 1, TOK])
    rec = sb("recip_sum", [P, NT])
    on = sb("o_head", [P, 2, NT, VD])

    q_in, k_in, v_in = k.sem("q_in"), k.sem("k_in"), k.sem("v_in")
    q_hi, k_hi, v_hi, q_lo, k_lo, v_lo = (k.sem(n) for n in ("q_hi_ready", "k_hi_ready", "v_hi_ready", "q_lo_ready", "k_lo_ready", "v_lo_ready"))
    ones, pool_link = k.sem("ones_rows"), k.sem("at_pool_link")
    s_ready, e_done, p_hi, p_lo, pv_done = (k.sem(n) for n in ("s_ready", "exp_done", "p_hi_ready", "p_lo_ready", "pv_done"))
    a_ready, a_free = k.sem("approx_ready"), k.sem("approx_free")
    m_tr, m_row, m_in = k.sem("max_tr"), k.sem("max_row"), k.sem("max_in")
    o_free, ot_ready, ot_free = k.sem("o_free"), k.sem("ot_ready"), k.sem("ot_free")
    rec_done = k.sem("rec_done")
    o_out = [k.sem(f"o_out{s}") for s in range(2)]

    gqa = lambda g: g < HA
    GROUP = HA // KVA

    def kv(g):
        return g // GROUP if gqa(g) else KVA + g - HA

    def first_head(n):
        return n * GROUP if n < KVA else HA + n - KVA

    def last_head(n):
        return first_head(n) + (GROUP - 1 if n < KVA else 0)

    S_BANKS = [k.bank[0], k.bank[1]]
    A_PAIR, O_PAIR = k.bank[2], k.bank[3]
    ITEMS = UNITS
    SPREAD = {(0, "x"): 0, (0, "y"): 1, (1, "x"): 2, (1, "y"): 3, (2, "x"): 4, (3, "x"): 5, (3, "y"): 6, (4, "x"): 7, (5, "x"): 8}
    ROWS_AT = 6
    OUT_AT = sum(u < 2 or (u, z) == (2, "x") for u, z in SPREAD)

    def first_use(g):
        return (ITEMS + 1) * min(g + 1, 2) + (ITEMS + 2) * max(g - 1, 0)

    def item_use(g, i):
        return i if g == 0 else first_use(g - 1) + (g > 1 and i >= OUT_AT) + i

    def out_use(g):
        return first_use(g + 1) + OUT_AT if g < H - 2 else first_use(H - 1) + g - (H - 2)

    def use_before(eng, m):
        if m >= 1:
            eng.wait_ge(a_free, m)

    with nc.Block() as block:
        @block.sync
        def _(sp):
            for g in range(H):
                sp.wait_ge(m_row, g + 1)
                row = qs[1][DA:DA + 1, g % RING, :] if gqa(g) else qs[0][DM:DM + 1, g % RING, :]
                sp.dma_start(row.bitcast(F32), mrow[:, :].bitcast(F32)).then_inc(m_in, 16)

        @block.gpsimd
        def _(pool):
            def load(g):
                n = kv(g)
                if g >= 1:
                    pool.wait_ge(q_lo, g)
                if gqa(g):
                    for half in range(2):
                        pool.dma_start(qf[64 * half:64 * half + 64, :], k.qa_t[g * DA:(g + 1) * DA, :]).then_inc(q_in, 16)
                else:
                    h = g - HA
                    pool.dma_start(qf[0:48, :], k.qm_t[h * DM:h * DM + 48, :]).then_inc(q_in, 16)
                    pool.dma_start(qf[48:DM, :], k.qm_t[h * DM + 48:(h + 1) * DM, :]).then_inc(q_in, 16)
                if g != first_head(n):
                    return
                if n >= 1:
                    pool.wait_ge(k_lo, n)
                    pool.wait_ge(v_lo, n)
                if gqa(g):
                    for half in range(2):
                        pool.dma_start(kf[64 * half:64 * half + 64, :], k.ka_t[n * DA:(n + 1) * DA, :]).then_inc(k_in, 16)
                    pool.dma_start(vf[:, :, :], rows(k.va)[:, :, n * VD:(n + 1) * VD]).then_inc(v_in, 16)
                else:
                    pool.dma_start(kf[0:NOPE, :], k.kn_t[h * NOPE:(h + 1) * NOPE, :]).then_inc(k_in, 16)
                    pool.dma_start(kf[NOPE:DM, :], k.kr_t[:, :]).then_inc(k_in, 16)
                    pool.dma_start(vf[:, :, :], rows(k.vm)[:, :, h * VD:(h + 1) * VD]).then_inc(v_in, 16)

            def store(g):
                pool.wait_ge(a_free, out_use(g) + 1)
                pool.dma_start(rows(k.o)[:, :, g * VD:(g + 1) * VD], on[:, g % 2, :, :]).then_inc(o_out[g % 2], 16)

            load(0)
            link = Link(pool, pool_link)
            for s in range(RING):
                link(pool.memset(vs[0][:, s, :, VD:VC].bitcast(F32), 1.0))
                link(pool.memset(vs[1][:, s, :, VD:VC].bitcast(F32), 0.0))
                ins = pool.memset(ks[1][DA:DA + 1, s, :].bitcast(F32), 1.0)
                if s < RING - 1:
                    link(ins)
            ins.then_inc(ones, 1)
            load(1)
            load(2)
            for g in range(H):
                if g + 3 < H:
                    load(g + 3)
                store(g)
            for s in range(2):
                pool.wait_ge(o_out[s], 16 * (H // 2))

        @block.tensor
        def _(pe):
            def scores(g, u):
                c = g * UNITS + u
                if u == 0:
                    pe.wait_ge(m_in, 16 * (g + 1))
                if c >= 2:
                    pe.wait_ge(e_done, c - 1)
                out = S_BANKS[c % 2]
                s, n = g % RING, kv(g) % RING
                if u == 0:
                    jobs = [(out[:, 0, m * 256:(m + 1) * 256], m * P, slice(0, S_PROMPT)) for m in range(NTP)]
                else:
                    key = S_PROMPT + (u - 1) * P
                    jobs = [(out[:, m, :], key, slice(S_PROMPT + m * 512, S_PROMPT + (m + 1) * 512)) for m in range(2)]
                for dst, key, q in jobs:
                    kk = slice(key, key + P)
                    if gqa(g):
                        pe.matmul(dst, ks[0][:, n, kk], qs[0][:, s, q], start=True, stop=False)
                        mm = pe.matmul(dst, ks[1][0:DA + 1, n, kk], qs[1][0:DA + 1, s, q], start=False, stop=True)
                    else:
                        pe.matmul(dst, ks[0][0:DM + 1, n, kk], qs[0][0:DM + 1, s, q], start=True, stop=False)
                        pe.matmul(dst, ks[1][0:DM, n, kk], qs[0][0:DM, s, q], start=False, stop=False)
                        mm = pe.matmul(dst, ks[0][0:DM, n, kk], qs[1][0:DM, s, q], start=False, stop=True)
                mm.then_inc(s_ready, 1)

            def values(g, u):
                c = g * UNITS + u
                pe.wait_ge(p_lo, c + 1)
                if u == 0:
                    pe.wait_ge(v_lo, kv(g) + 1)
                    if g >= 1:
                        pe.wait_ge(o_free, 2 * g)
                if u == 1:
                    pe.wait_ge(o_free, 2 * g + 1)
                s = kv(g) % RING
                if u == 0:
                    jobs = [(O_PAIR[0:VD + 1, 0, 0:256], m, slice(m * 256, (m + 1) * 256), m == 0, m == NTP - 1) for m in range(NTP)]
                else:
                    jobs = [(O_PAIR[0:VD + 1, m, :], NTP + u - 1, slice(m * 512, (m + 1) * 512), u == 1, u == UNITS - 1) for m in range(2)]
                for dst, t, q, first, last in jobs:
                    v = [x[:, s, t, 0:VD + 1] for x in vs]
                    mm = three(pe, dst, v, [x[:, c % PS, q] for x in ph], first, last)
                mm.then_inc(pv_done, 1)

            def maxima(g, i):
                m = item_use(g, i)
                use_before(pe, m)
                if i == 0:
                    pe.wait_ge(q_lo, g + 1)
                    pe.wait_ge(k_lo, kv(g) + 1)
                    pe.wait_ge(ones, 1 + min(max(g - HA + 1, 0), RING))
                s, n = g % RING, kv(g) % RING
                w = P if gqa(g) else DM
                if i < ITEMS - 1:
                    q = slice(S_PROMPT + i * P, S_PROMPT + (i + 1) * P)
                    jobs = [(A_PAIR[:, c, :], q, slice(S_PROMPT + c * 512, S_PROMPT + (c + 1) * 512)) for c in range(2)]
                else:
                    jobs = [(A_PAIR[:, 0, c * 256:(c + 1) * 256], slice(c * P, (c + 1) * P), slice(0, S_PROMPT)) for c in range(NTP)]
                for dst, q, key in jobs:
                    mm = pe.matmul(dst, qs[0][0:w, s, q], ks[0][0:w, n, key], start=True, stop=True)
                mm.then_inc(a_ready, 1)

            def max_rows(g):
                m = item_use(g, ITEMS)
                use_before(pe, m)
                pe.transpose(A_PAIR[0:NT, 0, 0:P], mcol[:, :], k.ident[:, :]).then_inc(a_ready, 1)

            def outputs(g):
                use_before(pe, out_use(g))
                pe.wait_ge(o_free, 2 * (g + 1))
                for t in range(NT):
                    mm = pe.transpose(A_PAIR[:, t // 5, t % 5 * VC:t % 5 * VC + VD + 1], oc[:, t * P:(t + 1) * P], k.ident[0:VD + 1, 0:VD + 1])
                mm.then_inc(a_ready, 1)

            for i in range(ITEMS):
                maxima(0, i)
            max_rows(0)
            for g in range(H):
                for u in range(UNITS):
                    scores(g, u)
                    if g + 1 < H and (u, "x") in SPREAD:
                        maxima(g + 1, SPREAD[u, "x"])
                    if g + 1 < H and u == ROWS_AT:
                        max_rows(g + 1)
                    c = g * UNITS + u - LAG
                    if c >= 0:
                        values(c // UNITS, c % UNITS)
                    if u == 2 and g >= 1:
                        outputs(g - 1)
                    if g + 1 < H and (u, "y") in SPREAD:
                        maxima(g + 1, SPREAD[u, "y"])
            for u in range(UNITS - LAG, UNITS):
                values(H - 1, u)
            outputs(H - 1)

        @block.scalar
        def _(act):
            def round_q(g):
                act.wait_ge(q_in, 32 * (g + 1))
                if g >= RING:
                    act.wait_ge(s_ready, UNITS * (g - RING + 1))
                s = g % RING
                if gqa(g):
                    act.activation(qs[1][0:DA, s, :], qf[0:DA, :], ACT.Copy)
                    act.activation(qs[0][:, s, :], qf[:, :], ACT.Copy).then_inc(q_hi, 1)
                else:
                    act.activation(qs[0][0:DM, s, :], qf[0:DM, :], ACT.Copy).then_inc(q_hi, 1)

            def round_k(n):
                act.wait_ge(k_in, 32 * (n + 1))
                if n >= RING:
                    act.wait_ge(s_ready, UNITS * (last_head(n - RING) + 1))
                w = P if n < KVA else DM
                act.activation(ks[0][0:w, n % RING, :], kf[0:w, :], ACT.Copy).then_inc(k_hi, 1)

            def round_v(n):
                act.wait_ge(v_in, 16 * (n + 1))
                if n >= RING:
                    act.wait_ge(pv_done, UNITS * (last_head(n - RING) + 1))
                act.activation(vs[0][:, n % RING, :, 0:VD], vf[:, :, :], ACT.Copy).then_inc(v_hi, 1)

            def exp(g, u):
                c = g * UNITS + u
                scale = DA ** -0.5 if gqa(g) else DM ** -0.5
                act.wait_ge(s_ready, c + 1)
                if c >= PS:
                    act.wait_ge(p_lo, c - PS + 1)
                w = 512 if u == 0 else 1024
                src = S_BANKS[c % 2][:, :, :].rearrange("p a b -> p (a b)")[:, 0:w]
                act.activation(pf[:, c % PS, 0:w], src, ACT.Exp, scale=scale).then_inc(e_done, 1)
                act.wait_ge(e_done, c + 1)
                if c >= PS:
                    act.wait_ge(pv_done, c - PS + 1)
                act.activation(ph[0][:, c % PS, 0:w], pf[:, c % PS, 0:w], ACT.Copy).then_inc(p_hi, 1)

            def take_outputs(g, part):
                act.wait_ge(pv_done, g * UNITS + (1 if part == 0 else UNITS))
                if part == 0:
                    if g >= 1:
                        act.wait_ge(a_ready, out_use(g - 1) + 1)
                    act.activation(oc[:, 0:S_PROMPT], O_PAIR[0:VD + 1, 0, 0:S_PROMPT], ACT.Copy).then_inc(o_free, 1)
                else:
                    act.activation(oc[:, S_PROMPT:], O_PAIR[0:VD + 1, :, :].rearrange("p a b -> p (a b)"), ACT.Copy).then_inc(o_free, 1)

            round_q(0)
            round_k(0)
            round_v(0)
            round_q(1)
            for g in range(H):
                for u in range(UNITS):
                    exp(g, u)
                    if u == 1 and g >= 1:
                        take_outputs(g - 1, 1)
                    if g + 2 < H and u == 4:
                        round_q(g + 2)
                    if g + 2 < H and first_head(kv(g + 2)) == g + 2:
                        if u == 5:
                            round_k(kv(g + 2))
                        if u == 6:
                            round_v(kv(g + 2))
                    if u == 2:
                        take_outputs(g, 0)
            take_outputs(H - 1, 1)

        @block.vector
        def _(dve):
            def low_q(g):
                dve.wait_ge(q_hi, g + 1)
                s = g % RING
                if gqa(g):
                    ins = dve.tensor_tensor(qs[0][DA:P, s, :], qf[DA:P, :], qs[0][DA:P, s, :], ALU.subtract)
                else:
                    if g < HA + RING:
                        dve.memset(ks[0][DM:DM + 1, kv(g) % RING, :].bitcast(F32), 1.0).then_inc(ones, 1)
                    ins = dve.tensor_tensor(qs[1][0:DM, s, :], qf[0:DM, :], qs[0][0:DM, s, :], ALU.subtract)
                ins.then_inc(q_lo, 1)

            def low_k(n):
                dve.wait_ge(k_hi, n + 1)
                s, w = n % RING, DA if n < KVA else DM
                dve.tensor_tensor(ks[1][0:w, s, :], kf[0:w, :], ks[0][0:w, s, :], ALU.subtract).then_inc(k_lo, 1)

            def low_v(n):
                dve.wait_ge(v_hi, n + 1)
                dve.tensor_tensor(vs[1][:, n % RING, :, 0:VD], vf[:, :, :], vs[0][:, n % RING, :, 0:VD], ALU.subtract).then_inc(v_lo, 1)

            def p_low(g, u):
                c = g * UNITS + u
                w = 512 if u == 0 else 1024
                dve.wait_ge(p_hi, c + 1)
                dve.tensor_tensor(ph[1][:, c % PS, 0:w], pf[:, c % PS, 0:w], ph[0][:, c % PS, 0:w], ALU.subtract).then_inc(p_lo, 1)

            def maximum(g, i):
                m = item_use(g, i)
                dve.wait_ge(a_ready, m + 1)
                if i == 0 and g >= 1:
                    dve.wait_ge(a_ready, item_use(g - 1, ITEMS) + 1)
                if i < ITEMS - 1:
                    dve.reduce_max(mcol[:, NTP + i:NTP + i + 1], A_PAIR[:, :, :].rearrange("p a b -> p (a b)"), AX.X).then_inc(a_free, 1)
                else:
                    dve.reduce_max(mcol[:, 0:NTP], A_PAIR[:, 0, :].rearrange("p (a b) -> p a b", a=NTP), AX.X).then_inc(a_free, 1)

            def max_row(g):
                dve.wait_ge(a_ready, item_use(g, ITEMS) + 1)
                if g >= 1:
                    dve.wait_ge(m_in, 16 * g)
                dve.tensor_scalar(mrow[:, :], A_PAIR[0:NT, 0, 0:P], -1.0, None, ALU.mult).then_inc(m_row, 1)
                dve.wait_ge(m_row, g + 1)
                dve.engine_nop().then_inc(a_free, 1)

            def normalise(g):
                dve.wait_ge(a_ready, out_use(g) + 1)
                if g >= 2:
                    dve.wait_ge(o_out[g % 2], 16 * (g // 2))
                for m in range(2):
                    tr = A_PAIR[:, m, 0:5 * VC].rearrange("p (t c) -> p t c", c=VC)
                    dve.reciprocal(rec[:, 5 * m:5 * m + 5, None], tr[:, :, VD:VD + 1]).then_inc(rec_done, 1)
                    dve.wait_ge(rec_done, 2 * g + m + 1)
                    ins = dve.tensor_tensor(on[:, g % 2, 5 * m:5 * m + 5, :], tr[:, :, 0:VD],
                                            rec[:, 5 * m:5 * m + 5, None].to_broadcast([P, 5, VD]), ALU.mult)
                ins.then_inc(a_free, 1)

            low_q(0)
            low_k(0)
            for i in range(ITEMS):
                maximum(0, i)
            max_row(0)
            low_v(0)
            low_q(1)
            for g in range(H):
                for u in range(UNITS):
                    if g + 1 < H and (u, "x") in SPREAD:
                        maximum(g + 1, SPREAD[u, "x"])
                    if g + 1 < H and u == ROWS_AT:
                        max_row(g + 1)
                    c = g * UNITS + u - 1
                    if c >= 0:
                        p_low(c // UNITS, c % UNITS)
                    if u == 2 and g >= 1:
                        normalise(g - 1)
                    if g + 2 < H and u == 5:
                        low_q(g + 2)
                    if g + 2 < H and first_head(kv(g + 2)) == g + 2:
                        if u == 6:
                            low_k(kv(g + 2))
                        if u == 7:
                            low_v(kv(g + 2))
                    if g + 1 < H and (u, "y") in SPREAD:
                        maximum(g + 1, SPREAD[u, "y"])
            p_low(H - 1, UNITS - 1)
            normalise(H - 1)


def output(k, stage):
    nc = k.nc
    sb = lambda name, shape, dt=F32: k.sb(stage, name, shape, dt)
    wo = [sb(f"w_out_{s}", [P, KT, D], F32R) for s in ("hi", "lo")]
    raw = sb("w_out_raw", [P, D])
    gain = sb("grp_gain", [P, KT])
    modt = sb("mod_mid_t", [P, 2, 2, KT])
    g1 = sb("gate_1", [P, 2, D])
    ln1 = sb("ln1_gain_bias", [P, 2, D])
    ot = sb("o_tile", [P, 2, D])
    junk = sb("squares_c", [P, 512])
    ss = sb("grp_sums", [P, 2, 2])
    mt = [sb(f"mix_t_{s}", [P, 2, KT, P], F32R) for s in ("hi", "lo")]
    y = sb("y", [P, 2, D])
    r = sb("gated", [P, D])
    uf = sb("u2_f32", [P, KT, P])
    stats = sb("stats_c", [P, 12])
    mv = sb("mean_var_c", [P, 2, 2])
    std = sb("std_c", [P, 2, 1])

    raw_in, raw_scaled, hi_done, lo_done = (k.sem(n) for n in ("wo_in", "wo_scaled", "wo_hi", "wo_lo"))
    tabs_in, modp = k.sem("oc_tabs_in"), k.sem("oc_mod_plus_one")
    o_in, x_in = [k.sem(f"oc_o_in{s}") for s in range(2)], [k.sem(f"oc_x_in{s}") for s in range(2)]
    ss_ready, on_ready = k.sem("ss_ready"), k.sem("on_ready")
    mt_tr, mt_hi, mt_lo = k.sem("mt_tr"), k.sem("mt_hi"), k.sem("mt_lo")
    mix_ready, mix_free = k.sem("mix_ready"), k.sem("mix_free")
    var_ready, std_ready = k.sem("oc_var"), k.sem("oc_std")
    x1_ready, x1_out = k.sem("x1_ready"), [k.sem(f"x1_out{s}") for s in range(2)]
    xh_ready, u_tr, uf_ready, u2_ready = k.sem("oc_xhat"), k.sem("oc_u_tr"), k.sem("oc_uf"), k.sem("u2_ready")
    dv, ac = k.sem("oc_dve_link"), k.sem("oc_act_link")

    with nc.Block() as block:
        @block.sync
        def _(sp):
            with nc.allow_non_contiguous_dma(reason="columns of gains and modulation, once"):
                for m, g in enumerate(("grp_norm_a", "grp_norm_b")):
                    sp.dma_start(gain[:, 4 * m:4 * m + 4], k.i[g][0, :].rearrange("(j p) -> p j", p=P)).then_inc(tabs_in, 16)
                for s in range(2):
                    for m, part in enumerate((4, 3)):
                        sp.dma_start(modt[:, s, m, :], k.mod[s, part * D:(part + 1) * D].rearrange("(j p) -> p j", p=P)).then_inc(tabs_in, 16)
            for s in range(2):
                sp.dma_start(g1[:, s, :], k.mod[s, 2 * D:3 * D].partition_broadcast(P)).then_inc(tabs_in, 16)
            for m, g in enumerate(("ln1_g", "ln1_b")):
                sp.dma_start(ln1[:, m, :], k.i[g][0, :].partition_broadcast(P)).then_inc(tabs_in, 16)

            def load(t):
                sp.dma_start(ot[:, t % 2, :], k.o[t * P:(t + 1) * P, :]).then_inc(o_in[t % 2], 16)
                if t >= 2:
                    sp.wait_ge(x1_out[t % 2], 16 * (t // 2))
                    sp.wait_ge(xh_ready, t - 1)
                sp.dma_start(y[:, t % 2, :], xrow(k, t)).then_inc(x_in[t % 2], 16)

            def store(t):
                sp.wait_ge(x1_ready, t + 1)
                sp.dma_start(k.x1[t * P:(t + 1) * P, :], y[:, t % 2, :]).then_inc(x1_out[t % 2], 16)

            load(0)
            load(1)
            for t in range(NT):
                store(t)
                if t + 2 < NT:
                    sp.wait_ge(mt_tr, 2 * (t + 1))
                    load(t + 2)
            for s in range(2):
                sp.wait_ge(x1_out[s], 16 * (NT // 2))

        @block.gpsimd
        def _(pool):
            for j in range(KT):
                if j >= 1:
                    pool.wait_ge(lo_done, j)
                pool.dma_start(raw[:, :], rows(k.i["w_out"][0])[:, j, :]).then_inc(raw_in, 16)

        @block.tensor
        def _(pe):
            def mix_t(t):
                pe.wait_ge(on_ready, t + 1)
                for m in range(2):
                    if t >= 1:
                        pe.wait_ge(mt_lo, 2 * (t - 1) + m + 1)
                    for q in range(4):
                        j = 4 * m + q
                        mm = pe.transpose(bank(k, m)[:, q * P:(q + 1) * P], ot[:, t % 2, j * P:(j + 1) * P], k.ident[:, :])
                    mm.then_inc(mt_tr, 1)

            def mix(t):
                pe.wait_ge(mt_lo, 2 * (t + 1))
                if t == 0:
                    pe.wait_ge(lo_done, KT)
                if t >= 2:
                    pe.wait_ge(mix_free, t - 1)
                out = k.bank[1 + t % 2]
                for m in range(2):
                    for j in range(KT):
                        mm = three(pe, out[:, m, :], [x[:, t % 2, j, :] for x in mt],
                                   [w[:, j, m * 512:(m + 1) * 512] for w in wo], j == 0, j == KT - 1)
                mm.then_inc(mix_ready, 1)

            def u_t(t):
                pe.wait_ge(xh_ready, t + 1)
                if t >= 1:
                    pe.wait_ge(uf_ready, t)
                for j in range(KT):
                    mm = pe.transpose(k.bank[3][:, j // 4, j % 4 * P:(j % 4 + 1) * P], r[:, j * P:(j + 1) * P], k.ident[:, :])
                mm.then_inc(u_tr, 1)

            for n in range(NT + 2):
                if n < NT:
                    mix_t(n)
                if 0 <= n - 1 < NT:
                    mix(n - 1)
                if 0 <= n - 2 < NT:
                    u_t(n - 2)

        @block.scalar
        def _(act):
            def w_hi(j):
                act.wait_ge(raw_scaled, j + 1)
                act.activation(wo[0][:, j, :], raw[:, :], ACT.Copy).then_inc(hi_done, 1)

            def squares(t):
                act.wait_ge(o_in[t % 2], 16 * (t // 2 + 1))
                for m in range(2):
                    ins = act.activation(junk[:, :], ot[:, t % 2, m * 512:(m + 1) * 512], ACT.Square, accum_out=ss[:, t % 2, m:m + 1])
                    ins.then_inc(ac, 1)
                    act.wait_ge(ac, 2 * t + m + 1)
                act.activation(ss[:, t % 2, :], ss[:, t % 2, :], ACT.Sqrt, scale=1.0 / 512, bias=k.eps[:, 0:1]).then_inc(ss_ready, 1)

            def mix_hi(t):
                for m in range(2):
                    act.wait_ge(mt_tr, 2 * t + m + 1)
                    if m == 0 and t >= 2:
                        act.wait_ge(mix_ready, t - 1)
                    act.activation(mt[0][:, t % 2, 4 * m:4 * m + 4, :], bank(k, m).rearrange("p (q c) -> p q c", c=P), ACT.Copy).then_inc(mt_hi, 1)

            def roots(t, which):
                act.wait_ge(var_ready, 2 * t + which + 1)
                act.activation(std[:, which, :], mv[:, which, 1:2], ACT.Sqrt, bias=k.eps[:, 0:1]).then_inc(std_ready, 1)

            def modulate(t):
                act.wait_ge(u_tr, t + 1)
                if t >= 1:
                    act.wait_ge(u2_ready, t)
                seq = 0 if t < NTP else 1
                for j in range(KT):
                    ins = act.activation(uf[:, j, :], k.bank[3][:, j // 4, j % 4 * P:(j % 4 + 1) * P], ACT.Identity,
                                         bias=modt[:, seq, 1, j:j + 1], scale=modt[:, seq, 0, j:j + 1])
                ins.then_inc(uf_ready, 1)

            for j in range(KT):
                w_hi(j)
            act.wait_ge(modp, 1)
            for n in range(NT + 2):
                if n < NT:
                    squares(n)
                    mix_hi(n)
                if 0 <= n - 1 < NT:
                    roots(n - 1, 0)
                    roots(n - 1, 1)
                if 0 <= n - 2 < NT:
                    modulate(n - 2)

        @block.vector
        def _(dve):
            link = Link(dve, dv)

            def w_lo(j):
                if j == 0:
                    dve.wait_ge(tabs_in, 160)
                dve.wait_ge(raw_in, 16 * (j + 1))
                dve.tensor_scalar(raw[:, :], raw[:, :], gain[:, j:j + 1], None, ALU.mult).then_inc(raw_scaled, 1)
                dve.wait_ge(hi_done, j + 1)
                dve.tensor_tensor(wo[1][:, j, :], raw[:, :], wo[0][:, j, :], ALU.subtract).then_inc(lo_done, 1)

            def group_norm(t):
                dve.wait_ge(ss_ready, t + 1)
                link(dve.reciprocal(ss[:, t % 2, :], ss[:, t % 2, :]))
                for m in range(2):
                    ins = dve.tensor_scalar(ot[:, t % 2, m * 512:(m + 1) * 512], ot[:, t % 2, m * 512:(m + 1) * 512],
                                            ss[:, t % 2, m:m + 1], None, ALU.mult)
                ins.then_inc(on_ready, 1)

            def mix_lo(t):
                for m in range(2):
                    dve.wait_ge(mt_hi, 2 * t + m + 1)
                    dve.tensor_tensor(mt[1][:, t % 2, 4 * m:4 * m + 4, :], bank(k, m).rearrange("p (q c) -> p q c", c=P),
                                      mt[0][:, t % 2, 4 * m:4 * m + 4, :], ALU.subtract).then_inc(mt_lo, 1)

            def norm(t, which, out):
                src = y[:, t % 2, :]
                for m in range(2):
                    link(dve.bn_stats(stats[:, 6 * m:6 * m + 6], src[:, m * 512:(m + 1) * 512]))
                dve.bn_aggr(mv[:, which, :], stats[:, :]).then_inc(var_ready, 1)
                dve.wait_ge(std_ready, 2 * t + which + 1)
                dve.wait_ge(var_ready, 2 * t + which + 1)
                link(dve.reciprocal(std[:, which, :], std[:, which, :]))
                return dve.tensor_scalar(out, src, mv[:, which, 0:1], std[:, which, :], ALU.subtract, ALU.mult)

            def residual(t):
                seq = 0 if t < NTP else 1
                dve.wait_ge(mix_ready, t + 1)
                if t >= 1:
                    dve.wait_ge(u_tr, t)
                dve.tensor_tensor(r[:, :], k.bank[1 + t % 2][:, :, :].rearrange("p a b -> p (a b)"), g1[:, seq, :], ALU.mult).then_inc(mix_free, 1)
                dve.wait_ge(mix_free, t + 1)
                dve.wait_ge(x_in[t % 2], 16 * (t // 2 + 1))
                yt = y[:, t % 2, :]
                link(dve.scalar_tensor_tensor(yt, yt, ALPHA, r[:, :], ALU.mult, ALU.add))
                link(norm(t, 0, yt))
                link(dve.tensor_tensor(yt, yt, ln1[:, 0, :], ALU.mult))
                dve.tensor_tensor(yt, yt, ln1[:, 1, :], ALU.add).then_inc(x1_ready, 1)
                dve.wait_ge(x1_ready, t + 1)
                norm(t, 1, r[:, :]).then_inc(xh_ready, 1)

            def u_split(t):
                cols = slice(t * P, (t + 1) * P)
                dve.wait_ge(uf_ready, t + 1)
                link(dve.tensor_copy(k.u2[0][:, :, cols], uf[:, :, :]))
                dve.tensor_tensor(k.u2[1][:, :, cols], uf[:, :, :], k.u2[0][:, :, cols], ALU.subtract).then_inc(u2_ready, 1)

            for j in range(KT):
                w_lo(j)
            for s in range(2):
                ins = dve.tensor_scalar(modt[:, s, 0, :], modt[:, s, 0, :], 1.0, None, ALU.add)
            ins.then_inc(modp, 1)
            for n in range(NT + 2):
                if n < NT:
                    group_norm(n)
                    mix_lo(n)
                if 0 <= n - 1 < NT:
                    residual(n - 1)
                if 0 <= n - 2 < NT:
                    u_split(n - 2)


def channel(k, stage):
    nc = k.nc
    sumf = k.sb(stage, "sum_f", [P, NT, D])
    with ExitStack() as inner:
        sb = lambda name, shape, dt=F32: k.sb(inner, name, shape, dt)
        raw_gu = sb("gate_up_raw", [P, 2, KT, P])
        raw_d = sb("down_raw", [P, D])
        wgu = [sb(f"gate_up_{s}", [P, 2, 2, KT, P], F32R) for s in ("hi", "lo")]
        wd = [sb(f"down_{s}", [P, 2, D], F32R) for s in ("hi", "lo")]
        sg = sb("silu_gate", [P, 512])
        hf = sb("hidden_f32", [P, 512])
        hid = [sb(f"hidden_{s}", [P, TOK], F32R) for s in ("hi", "lo")]
        gu_in, d_in = k.sem("gu_in"), k.sem("down_in")
        gu_hi, gu_lo, d_hi, d_lo = (k.sem(n) for n in ("gu_hi", "gu_lo", "down_hi", "down_lo"))
        gu_ready, silu_done, h_ready, hid_hi, hid_lo = (k.sem(n) for n in ("gu_ready", "silu_done", "ff_h", "hid_hi", "hid_lo"))
        dn_ready, dn_added = k.sem("down_ready"), k.sem("down_added")
        TILES = [range(c[0] // P, c[1] // P) for c in CHUNKS]
        NCH = len(CHUNKS)

        def run(eng, body):
            body(0, 0, True)
            body(1, 1, False)
            with eng.Fori(2, NF, 2) as i:
                body(i, 0, False)
                body(i + 1, 1, False)
            body(NF, 0, False, last=True)

        def prev(f, c):
            return (c - 1) % NCH, NCH * f + c

        with nc.Block() as block:
            @block.sync
            def _(sp):
                wg, wu, w_dn = rows(k.i["w_gate"][0]), rows(k.i["w_up"][0]), rows(k.i["w_down"][0])

                def load(f, wait=True):
                    if wait:
                        sp.wait_ge(gu_lo, f)
                    for m, w in enumerate((k.i["w_gate"][0], k.i["w_up"][0])):
                        sp.dma_start(raw_gu[:, m, :, :], rows(w)[:, :, bass.ds(f * P, P)]).then_inc(gu_in, 16)
                    if wait:
                        sp.wait_ge(d_lo, f)
                    sp.dma_start(raw_d[:, :], k.i["w_down"][0][bass.ds(f * P, P), :]).then_inc(d_in, 16)

                load(0, wait=False)
                load(1)
                with sp.Fori(2, NF) as f:
                    load(f)

            @block.tensor
            def _(pe):
                def down(f, t, slot):
                    if t < 2 and isinstance(f, int) and f == 1:
                        pass
                    else:
                        pe.wait_ge(dn_added, NT * (f - 1) + t - 1)
                    for m in range(2):
                        mm = three(pe, k.bank[2 + t % 2][:, m, :], [x[:, t * P:(t + 1) * P] for x in hid],
                                   [w[:, 1 - slot, m * 512:(m + 1) * 512] for w in wd], True, True)
                    mm.then_inc(dn_ready, 1)

                def body(f, slot, first, last=False):
                    for c, (lo, hi) in enumerate(CHUNKS):
                        if not first:
                            pe.wait_ge(hid_lo, NCH * (f - 1) + c + 1)
                            if c == 0:
                                pe.wait_ge(d_lo, f)
                            for t in TILES[c]:
                                down(f, t, slot)
                        if last:
                            continue
                        if c == 0:
                            pe.wait_ge(gu_lo, f + 1)
                        out = k.bank[(slot + c) % 2]
                        if not (first and c < 2):
                            pe.wait_ge(h_ready, NCH * f + c - 1)
                        for m in range(2):
                            for j in range(KT):
                                mm = three(pe, out[:, m, 0:hi - lo], [w[:, slot, m, j, :] for w in wgu],
                                           [x[:, j, lo:hi] for x in k.u2], j == 0, j == KT - 1)
                        mm.then_inc(gu_ready, 1)

                run(pe, body)

            @block.scalar
            def _(act):
                def gu_round(f, slot, first):
                    act.wait_ge(gu_in, 32 * (f + 1))
                    if not first:
                        act.wait_ge(gu_ready, NCH * (f - 1))
                    act.activation(wgu[0][:, slot, :, :, :], raw_gu[:, :, :, :], ACT.Copy).then_inc(gu_hi, 1)

                def d_round(f, slot, first):
                    act.wait_ge(d_in, 16 * (f + 1))
                    if not first:
                        act.wait_ge(dn_ready, NT * (f - 1))
                    act.activation(wd[0][:, slot, :], raw_d[:, :], ACT.Copy).then_inc(d_hi, 1)

                def silu(f, c, slot):
                    pc, m = prev(f, c)
                    lo, hi = CHUNKS[pc]
                    act.wait_ge(gu_ready, m)
                    if not (isinstance(m, int) and m == 1):
                        act.wait_ge(h_ready, m - 1)
                    act.activation(sg[:, 0:hi - lo], k.bank[(slot + c + 1) % 2][:, 0, 0:hi - lo], ACT.Silu).then_inc(silu_done, 1)
                    act.wait_ge(h_ready, m)
                    if not (isinstance(f, int) and (f == 0 or (f == 1 and c == 0))):
                        act.wait_ge(dn_ready, NT * (f - 1 - (c == 0)) + TILES[pc][-1] + 1)
                    act.activation(hid[0][:, lo:hi], hf[:, 0:hi - lo], ACT.Copy).then_inc(hid_hi, 1)

                gu_round(0, 0, True)

                def body(f, slot, first, last=False):
                    for c in range(NCH):
                        if not (first and c == 0) and not (last and c > 0):
                            silu(f, c, slot)
                        if last:
                            continue
                        if c == 1:
                            d_round(f, slot, isinstance(f, int) and f < 2)
                        if c == 2:
                            if isinstance(f, int):
                                gu_round(f + 1, 1 - slot, f == 0)
                            elif slot == 0:
                                gu_round(f + 1, 1, False)
                            else:
                                with act.If(f + 1 < NF):
                                    gu_round(f + 1, 0, False)

                run(act, body)

            @block.vector
            def _(dve):
                def gu_low(f, slot):
                    dve.wait_ge(gu_hi, f + 1)
                    dve.tensor_tensor(wgu[1][:, slot, :, :, :], raw_gu[:, :, :, :], wgu[0][:, slot, :, :, :], ALU.subtract).then_inc(gu_lo, 1)

                def d_low(f, slot):
                    dve.wait_ge(d_hi, f + 1)
                    dve.tensor_tensor(wd[1][:, slot, :], raw_d[:, :], wd[0][:, slot, :], ALU.subtract).then_inc(d_lo, 1)

                def product(f, c, slot):
                    pc, m = prev(f, c)
                    lo, hi = CHUNKS[pc]
                    dve.wait_ge(silu_done, m)
                    if not (isinstance(m, int) and m == 1):
                        dve.wait_ge(hid_lo, m - 1)
                    dve.tensor_tensor(hf[:, 0:hi - lo], k.bank[(slot + c + 1) % 2][:, 1, 0:hi - lo], sg[:, 0:hi - lo], ALU.mult).then_inc(h_ready, 1)

                def hidden_low(f, c):
                    pc, m = prev(f, c)
                    lo, hi = CHUNKS[pc]
                    dve.wait_ge(hid_hi, m)
                    dve.tensor_tensor(hid[1][:, lo:hi], hf[:, 0:hi - lo], hid[0][:, lo:hi], ALU.subtract).then_inc(hid_lo, 1)

                def add(f, t):
                    dve.wait_ge(dn_ready, NT * (f - 1) + t + 1)
                    src = k.bank[2 + t % 2][:, :, :].rearrange("p a b -> p (a b)")
                    if isinstance(f, int) and f == 1:
                        dve.tensor_copy(sumf[:, t, :], src).then_inc(dn_added, 1)
                    else:
                        dve.wait_ge(dn_added, NT * (f - 2) + t + 1)
                        dve.tensor_tensor(sumf[:, t, :], src, sumf[:, t, :], ALU.add).then_inc(dn_added, 1)

                gu_low(0, 0)

                def body(f, slot, first, last=False):
                    for c in range(NCH):
                        before = not (first and c == 0) and not (last and c > 0)
                        tiles = [] if first else list(TILES[c])
                        for q in range(max(len(tiles), 2)):
                            if q < len(tiles):
                                add(f, tiles[q])
                            if before and q == 0:
                                product(f, c, slot)
                            if before and q == 1:
                                hidden_low(f, c)
                        if last:
                            continue
                        if c == 1:
                            d_low(f, slot)
                        if c == 2:
                            if isinstance(f, int) or slot == 0:
                                gu_low(f + 1, 1 - slot)
                            else:
                                with dve.If(f + 1 < NF):
                                    gu_low(f + 1, 0)

                run(dve, body)

    with ExitStack() as inner:
        last_norm(k, inner, sumf)


def last_norm(k, stage, sumf):
    nc = k.nc
    sb = lambda name, shape, dt=F32: k.sb(stage, name, shape, dt)
    g2 = sb("gate_2", [P, 2, D])
    ln2 = sb("ln2_gain_bias", [P, 2, D])
    xt = sb("x1_tile", [P, 2, D])
    z = sb("z", [P, 3, D])
    stats = sb("stats_e", [P, 2, 12])
    mv = sb("mean_var_e", [P, 2, 2])
    std = sb("std_e", [P, 2, 1])
    tabs_in, x_in = k.sem("e_tabs_in"), [k.sem(f"e_x_in{s}") for s in range(2)]
    y_ready, var_ready, std_ready, hat_ready, gained, out_ready = (k.sem(n) for n in ("e_y", "e_var", "e_std", "e_hat", "e_gained", "e_out"))
    y_out = [k.sem(f"e_stored{s}") for s in range(3)]
    dv = k.sem("e_dve_link")

    with nc.Block() as block:
        @block.sync
        def _(sp):
            for s in range(2):
                sp.dma_start(g2[:, s, :], k.mod[s, 5 * D:6 * D].partition_broadcast(P)).then_inc(tabs_in, 16)
            for t in range(2):
                sp.dma_start(xt[:, t, :], k.x1[t * P:(t + 1) * P, :]).then_inc(x_in[t], 16)
            for m, g in enumerate(("ln2_g", "ln2_b")):
                sp.dma_start(ln2[:, m, :], k.i[g][0, :].partition_broadcast(P)).then_inc(tabs_in, 16)
            for t in range(NT):
                if t + 2 < NT:
                    sp.wait_ge(y_ready, t + 1)
                    sp.dma_start(xt[:, t % 2, :], k.x1[(t + 2) * P:(t + 3) * P, :]).then_inc(x_in[t % 2], 16)
                sp.wait_ge(out_ready, t + 1)
                dst = k.o_prompt(t) if t < NTP else k.o_sample(t - NTP)
                sp.dma_start(dst, z[:, t % 3, :]).then_inc(y_out[t % 3], 16)
            for s in range(3):
                sp.wait_ge(y_out[s], 16 * len(range(s, NT, 3)))

        @block.scalar
        def _(act):
            for t in range(NT):
                act.wait_ge(var_ready, t + 1)
                act.activation(std[:, t % 2, :], mv[:, t % 2, 1:2], ACT.Sqrt, bias=k.eps[:, 0:1]).then_inc(std_ready, 1)

        @block.gpsimd
        def _(pool):
            for t in range(NT):
                pool.wait_ge(gained, t + 1)
                pool.tensor_tensor(z[:, t % 3, :], z[:, t % 3, :], ln2[:, 1, :], ALU.add).then_inc(out_ready, 1)

        @block.vector
        def _(dve):
            link = Link(dve, dv)
            dve.wait_ge(tabs_in, 64)
            for n in range(NT + 1):
                if n < NT:
                    zt, seq = z[:, n % 3, :], 0 if n < NTP else 1
                    dve.wait_ge(x_in[n % 2], 16 * (n // 2 + 1))
                    if n >= 3:
                        dve.wait_ge(y_out[n % 3], 16 * (n // 3))
                    link(dve.tensor_tensor(zt, sumf[:, n, :], g2[:, seq, :], ALU.mult))
                    dve.scalar_tensor_tensor(zt, xt[:, n % 2, :], ALPHA, zt, ALU.mult, ALU.add).then_inc(y_ready, 1)
                    dve.wait_ge(y_ready, n + 1)
                    for m in range(2):
                        link(dve.bn_stats(stats[:, n % 2, 6 * m:6 * m + 6], zt[:, m * 512:(m + 1) * 512]))
                    dve.bn_aggr(mv[:, n % 2, :], stats[:, n % 2, :]).then_inc(var_ready, 1)
                t = n - 1
                if t >= 0:
                    zt = z[:, t % 3, :]
                    dve.wait_ge(std_ready, t + 1)
                    dve.wait_ge(var_ready, t + 1)
                    link(dve.reciprocal(std[:, t % 2, :], std[:, t % 2, :]))
                    link(dve.tensor_scalar(zt, zt, mv[:, t % 2, 0:1], std[:, t % 2, :], ALU.subtract, ALU.mult))
                    dve.tensor_tensor(zt, zt, ln2[:, 0, :], ALU.mult).then_inc(gained, 1)


_INS = ["x_prompt", "x_sample", "c_prompt", "c_sample", "w_ada", "b_ada", "w_in", "gqa_q_norm", "gqa_k_norm",
        "mla_q_norm", "w_uq", "mla_kv_norm", "w_ukv", "grp_norm_a", "grp_norm_b", "w_out", "ln1_g", "ln1_b",
        "w_gate", "w_up", "w_down", "ln2_g", "ln2_b"]
_OUTS = [("y_prompt", (1, 256, 1024)), ("y_sample", (1, 1024, 1024))]


def _tables():
    import numpy as np

    row = np.repeat(np.arange(1024 // 64, dtype=np.float32), 64)
    col = np.tile(np.arange(64, dtype=np.float32), 1024 // 64)
    parts = []
    for dim in (64, 32):
        n = dim // 4
        freq = (1.0 / np.power(np.float32(10000.0), np.arange(n, dtype=np.float32) / np.float32(n))).astype(np.float32)
        ang = np.concatenate([row[:, None] * freq, col[:, None] * freq], axis=-1).astype(np.float32)
        parts += [np.cos(ang), np.sin(ang)]
    inv_n = np.array([1 / 64] * 10 + [1 / 256, 1 / 128], np.float32)
    return {"ident": np.eye(128, dtype=np.float32), "rope": np.concatenate(parts, 1).astype(np.float32), "inv_n": inv_n}


def kernel(**inputs):
    import numpy as _np
    import concourse.bacc as _bacc
    from concourse import mybir as _mybir
    from concourse.bass_utils import run_bass_kernel_spmd as _run

    nc = _bacc.Bacc("TRN2", target_bir_lowering=False, num_devices=1)
    arrays = {name: _np.ascontiguousarray(inputs[name]) for name in _INS}
    arrays.update(_tables())
    ins = {n: nc.dram_tensor(f"in_{n}", a.shape, _mybir.dt.from_np(a.dtype), kind="ExternalInput").ap() for n, a in arrays.items()}
    outs = {n: nc.dram_tensor(f"out_{n}", s, _mybir.dt.float32, kind="ExternalOutput").ap() for n, s in _OUTS}
    encoder_layer(nc, ins, outs)
    r = _run(nc, [{f"in_{n}": a for n, a in arrays.items()}], core_ids=[0])
    return tuple(r.results[0][f"out_{n}"] for n, _ in _OUTS)
```

```python
import concourse.bass as bass
from concourse import mybir
from contextlib import ExitStack

F32 = mybir.dt.float32
F32R = mybir.dt.float32r
ALU = mybir.AluOpType
ACT = mybir.ActivationFunctionType
AX = mybir.AxisListType

P = 128
D = 1024
KT = D // P
S_PROMPT, S_SAMPLE = 256, 1024
TOK = S_PROMPT + S_SAMPLE
NT = TOK // P
NTP = S_PROMPT // P
EPS = 1e-6
HA, KVA, DA = 8, 2, 64
HM, NOPE, ROPE, VD = 8, 64, 32, 64
DM = NOPE + ROPE
RQ, RKV = 256, 128
QK_A = (HA + KVA) * DA
C_VA = QK_A
C_QL = C_VA + KVA * DA
C_KVL = C_QL + RQ
C_KR = C_KVL + RKV
W_IN = C_KR + ROPE
BANKS_H = [(0, 384), (384, 768), (768, W_IN)]
FF = 2816
NF = FF // P
ALPHA = 2.0 ** 0.25
STOP = 0
CHUNKS = [(0, 256), (256, 768), (768, 1280)]


def rows(ap, n=P):
    return ap.rearrange("(t p) m -> p t m", p=n)


class Link:

    def __init__(self, eng, sem, start=0):
        self.eng, self.sem, self.n = eng, sem, start

    def __call__(self, ins):
        self.n += 1
        ins.then_inc(self.sem, 1)
        self.eng.wait_ge(self.sem, self.n)


class Kernel:
    def __init__(self, nc, ctx, ins, outs):
        self.nc, self.ctx = nc, ctx
        self.i, self.o = ins, outs
        self.names = set()

    def sem(self, name):
        return self.ctx.enter_context(self.nc.semaphore(name))

    def sb(self, stage, name, shape, dt=F32, side=None):
        return stage.enter_context(self.nc.sbuf_tensor(name, shape, dt, side=side))

    def dram(self, name, shape):
        return self.nc.dram_tensor(name, shape, F32, kind="Internal").ap()


def encoder_layer(nc, ins, outs):
    ctx = ExitStack()
    with ctx:
        k = Kernel(nc, ctx, ins, outs)
        k.bank = [ctx.enter_context(nc.psum_tensor(f"pair{b}", [P, 2, 512], F32)) for b in range(4)]
        k.ident = k.sb(ctx, "ident", [P, P])
        k.eps = k.sb(ctx, "eps", [P, 1])
        k.mod = k.dram("mod_rows", [2, 6 * D])
        k.qa_t = k.dram("qa_t", [HA * DA, TOK])
        k.ka_t = k.dram("ka_t", [KVA * DA, TOK])
        k.va = k.dram("va", [TOK, KVA * DA])
        k.qm_t = k.dram("qm_t", [HM * DM, TOK])
        k.kn_t = k.dram("kn_t", [HM * NOPE, TOK])
        k.kr_t = k.dram("kr_t", [ROPE, TOK])
        k.vm = k.dram("vm", [TOK, HM * VD])
        k.o = k.dram("o", [TOK, D])
        k.x1 = k.dram("x1", [TOK, D])
        k.o_prompt = lambda t: outs["y_prompt"][0, t * P:(t + 1) * P, :]
        k.o_sample = lambda t: outs["y_sample"][0, t * P:(t + 1) * P, :]
        with ExitStack() as weights:
            k.win = [k.sb(weights, f"w_in_{s}", [P, KT, W_IN], F32R) for s in ("hi", "lo")]
            k.wuq = [k.sb(weights, f"w_uq_{s}", [P, RQ // P, HM * DM], F32R) for s in ("hi", "lo")]
            k.wukv = [k.sb(weights, f"w_ukv_{s}", [P, HM * (NOPE + VD)], F32R) for s in ("hi", "lo")]
            with ExitStack() as stage:
                modulation(k, stage)
            if STOP == 1:
                return
            with ExitStack() as stage:
                projections(k, stage)
        if STOP == 2:
            return
        with ExitStack() as stage:
            with ExitStack() as weights:
                k.wo = [k.sb(weights, f"w_out_{s}", [P, KT, D], F32R, side="right") for s in ("hi", "lo")]
                with ExitStack() as inner:
                    attention(k, inner)
                if STOP == 3:
                    return
                k.u2 = [k.sb(stage, f"u2_{s}", [P, KT, TOK], F32R) for s in ("hi", "lo")]
                with ExitStack() as inner:
                    output(k, inner)
            if STOP == 4:
                return
            channel(k, stage)


def bank(k, n):
    return k.bank[n // 2][:, n % 2, :]


def xrow(k, t):
    if t < NTP:
        return k.i["x_prompt"][0, t * P:(t + 1) * P, :]
    return k.i["x_sample"][0, (t - NTP) * P:(t - NTP + 1) * P, :]


def three(pe, out, a, b, start, stop):
    pe.matmul(out, a[0], b[0], start=start, stop=False)
    pe.matmul(out, a[0], b[1], start=False, stop=False)
    return pe.matmul(out, a[1], b[0], start=False, stop=stop)


def modulation(k, stage):
    nc = k.nc
    NC = 6 * D // 512
    RING = 3
    c_t = k.sb(stage, "c_t", [P, KT, 2])
    silu_c = k.sb(stage, "silu_c", [P, KT, 2])
    wa = k.sb(stage, "w_ada_ring", [P, RING, KT, 512])
    bias = k.sb(stage, "b_ada_rows", [2, 2, 512])
    mrow = k.sb(stage, "mod_chunk", [2, 2, 512])
    raw = k.sb(stage, "w_raw", [P, 2, W_IN])
    c_in, ident_in = k.sem("c_in"), k.sem("ident_in")
    wa_in = [k.sem(f"wa_in{s}") for s in range(RING)]
    b_in = [k.sem(f"b_ada_in{s}") for s in range(2)]
    raw_in = [k.sem(f"raw_in{s}") for s in range(2)]
    c_ready, mod_done, mod_sum = k.sem("c_ready"), k.sem("mod_done"), k.sem("mod_sum")
    mod_out = [k.sem(f"mod_out{s}") for s in range(2)]
    hi_done, lo_done = k.sem("w_hi_done"), k.sem("w_lo_done")

    pieces = [(rows(k.i["w_in"][0])[:, j, :], k.win[0][:, j, :], k.win[1][:, j, :]) for j in range(KT)]
    pieces += [(rows(k.i["w_uq"][0])[:, j, :], k.wuq[0][:, j, :], k.wuq[1][:, j, :]) for j in range(RQ // P)]
    pieces += [(k.i["w_ukv"][0], k.wukv[0][:, :], k.wukv[1][:, :])]

    with nc.Block() as block:
        @block.sync
        def _(sp):
            for s, c in enumerate(("c_prompt", "c_sample")):
                with nc.allow_non_contiguous_dma(reason="two short vectors"):
                    sp.dma_start(c_t[:, :, s:s + 1], k.i[c][0:1, :].rearrange("a (p j) -> p j a", j=KT)).then_inc(c_in, 16)
            wsrc = k.i["w_ada"][0].rearrange("(p j) n -> p j n", j=KT)
            for n in range(NC):
                if n >= RING:
                    sp.wait_ge(mod_done, n - RING + 1)
                sp.dma_start(wa[:, n % RING, :, :], wsrc[:, :, n * 512:(n + 1) * 512]).then_inc(wa_in[n % RING], 16)

        @block.gpsimd
        def _(pool):
            pool.memset(k.eps[:, :], EPS)
            pool.dma_start(k.ident[:, :], k.i["ident"]).then_inc(ident_in, 16)
            for m, (src, hi, lo) in enumerate(pieces):
                if m >= 2:
                    pool.wait_ge(lo_done, m - 1)
                pool.dma_start(raw[:, m % 2, :hi.shape[-1]], src).then_inc(raw_in[m % 2], 16)
            pool.wait_ge(ident_in, 16)

        @block.tensor
        def _(pe):
            pe.wait_ge(c_ready, 1)
            for n in range(NC):
                pe.wait_ge(wa_in[n % RING], 16 * (n // RING + 1))
                if n >= 8:
                    pe.wait_ge(mod_sum, n - 7)
                for j in range(KT):
                    mm = pe.matmul(bank(k, n % 8)[0:2, :], silu_c[:, j, :], wa[:, n % RING, j, :],
                                   start=j == 0, stop=j == KT - 1)
                mm.then_inc(mod_done, 1)

        @block.scalar
        def _(act):
            act.wait_ge(c_in, 32)
            act.activation(silu_c[:, :, :], c_t[:, :, :], ACT.Silu).then_inc(c_ready, 1)
            assert len(pieces) <= NC
            for n in range(NC):
                if n < len(pieces):
                    act.wait_ge(raw_in[n % 2], 16 * (n // 2 + 1))
                    hi = pieces[n][1]
                    act.activation(hi, raw[:, n % 2, :hi.shape[-1]], ACT.Copy).then_inc(hi_done, 1)
                if n >= 2:
                    act.wait_ge(mod_sum, n - 1)
                src = k.i["b_ada"][0:1, n * 512:(n + 1) * 512]
                for s in range(2):
                    act.dma_start(bias[s:s + 1, n % 2, :], src).then_inc(b_in[n % 2], 16)
                if n >= 1:
                    act.wait_ge(mod_sum, n)
                    act.dma_start(k.mod[:, (n - 1) * 512:n * 512], mrow[:, (n - 1) % 2, :]).then_inc(mod_out[(n - 1) % 2], 16)
            act.wait_ge(mod_sum, NC)
            act.dma_start(k.mod[:, (NC - 1) * 512:], mrow[:, (NC - 1) % 2, :]).then_inc(mod_out[(NC - 1) % 2], 16)
            for s in range(2):
                act.wait_ge(mod_out[s], 16 * (NC // 2))

        @block.vector
        def _(dve):
            def split(m):
                src, hi, lo = pieces[m]
                dve.wait_ge(hi_done, m + 1)
                dve.tensor_tensor(lo, raw[:, m % 2, :hi.shape[-1]], hi, ALU.subtract).then_inc(lo_done, 1)

            for n in range(NC):
                if n < len(pieces):
                    split(n)
                dve.wait_ge(mod_done, n + 1)
                dve.wait_ge(b_in[n % 2], 32 * (n // 2 + 1))
                if n >= 2:
                    dve.wait_ge(mod_out[n % 2], 16 * (n // 2))
                dve.tensor_tensor(mrow[:, n % 2, :], bank(k, n % 8)[0:2, :], bias[:, n % 2, :], ALU.add).then_inc(mod_sum, 1)
            for m in range(NC, len(pieces)):
                split(m)


def projections(k, stage):
    nc = k.nc
    sb = lambda name, shape, dt=F32: k.sb(stage, name, shape, dt)
    xt = sb("x_tile", [P, 2, D])
    stats = sb("x_stats", [P, 2, 12])
    mv = sb("x_mean_var", [P, 2, 2])
    std = sb("x_std", [P, 2, 1])
    xh = sb("x_hat", [P, 2, D])
    uf = sb("u_t", [P, KT, P])
    u = [sb(f"u_{s}", [P, 2, KT, P], F32R) for s in ("hi", "lo")]
    modt = sb("mod_in_t", [P, 2, 2, KT])
    hs = sb("h", [P, 2, W_IN])
    sq = sb("squares", [P, C_KR])
    ssq = sb("norm_sums", [P, 12])
    inv_n = sb("inv_n", [P, 12])
    rn = sb("norm_factors", [P, 12])
    gain_qk = sb("gain_qk", [P, 2, DA])
    gain_lat = sb("gain_lat", [P, RQ + RKV])
    tab = sb("rope_tables", [P, S_SAMPLE // P, 96])
    qk = sb("qk", [P, QK_A])
    rot = sb("qk_rotated", [P, QK_A])
    qkr = sb("qk_out", [P, 2, QK_A + ROPE])
    lat = sb("latents", [P, 2, RQ + RKV])
    latf = sb("latents_t", [P, 3, P])
    lath = [sb(f"latents_t_{s}", [P, 3, P], F32R) for s in ("hi", "lo")]
    qms = sb("q_mla", [P, 2, HM * DM])
    mrot = sb("q_mla_rotated", [P, HM, ROPE])
    kvs = sb("kv_mla", [P, 2, 2, HM * NOPE])
    q_tr = sb("qa_tr", [P, 4, P])
    k_tr = sb("ka_tr", [P, 2, P])
    qm_tr = sb("qm_tr", [DM, HM, P])
    kn_tr = sb("kn_tr", [P, 4, P])

    x_in = [k.sem(f"pj_x_in{s}") for s in range(2)]
    tabs_in, mod_in, modp = k.sem("tabs_in"), k.sem("mod_in"), k.sem("mod_plus_one")
    var_ready, std_ready, xhat_ready = k.sem("pj_var"), k.sem("pj_std"), k.sem("pj_xhat")
    t_ready, t_free = k.sem("pj_t_ready"), k.sem("pj_t_free")
    uf_ready, u_hi, u_ready = k.sem("uf_ready"), k.sem("pj_u_hi"), k.sem("pj_u_ready")
    h_ready, h_free = k.sem("h_ready"), k.sem("h_free")
    qm_ready, qm_free, kv_ready, kv_free = (k.sem(n) for n in ("qm_ready", "qm_free", "kv_ready", "kv_free"))
    sums_ready, root_ready = k.sem("sums_ready"), k.sem("root_ready")
    qk_ready, lat_ready, latf_ready, lath_ready = (k.sem(n) for n in ("qk_ready", "lat_ready", "latf_ready", "lath_ready"))
    qm_roped = k.sem("qm_roped")
    sq_done = k.sem("sq_done")
    out_v, out_q, out_k, out_qm, out_kn, out_vm = ([k.sem(f"{n}{s}") for s in range(2)] for n in ("out_va", "out_qa", "out_ka", "out_qm", "out_kn", "out_vm"))
    dv, pl = k.sem("pj_dve_link"), k.sem("pj_pool_link")

    def tcols(t):
        return slice(t * P, (t + 1) * P)

    def groups(n):
        return ([0, 1] if n < NT else []) + ([2, 3, 4] if 0 <= n - 3 < NT else []) + ([5, 6, 7] if 0 <= n - 4 < NT else [])

    TURNS = range(NT + 4)
    order = [(n, g) for n in TURNS for g in groups(n)]
    number = {ng: m for m, ng in enumerate(order)}

    with nc.Block() as block:
        @block.sync
        def _(sp):
            with nc.allow_non_contiguous_dma(reason="modulation columns, once"):
                for s in range(2):
                    for m, part in enumerate((1, 0)):
                        sp.dma_start(modt[:, s, m, :], k.mod[s, part * D:(part + 1) * D].rearrange("(j p) -> p j", p=P)).then_inc(mod_in, 16)
            for t in range(2):
                sp.dma_start(xt[:, t, :], xrow(k, t)).then_inc(x_in[t], 16)
            sp.dma_start(tab[:, :, :], rows(k.i["rope"])).then_inc(tabs_in, 16)
            sp.dma_start(inv_n[:, :], k.i["inv_n"].partition_broadcast(P)).then_inc(tabs_in, 16)
            for m, g in enumerate(("gqa_q_norm", "gqa_k_norm")):
                sp.dma_start(gain_qk[:, m, :], k.i[g][0, :].partition_broadcast(P)).then_inc(tabs_in, 16)
            sp.dma_start(gain_lat[:, 0:RQ], k.i["mla_q_norm"][0, :].partition_broadcast(P)).then_inc(tabs_in, 16)
            sp.dma_start(gain_lat[:, RQ:], k.i["mla_kv_norm"][0, :].partition_broadcast(P)).then_inc(tabs_in, 16)

            def load_x(t):
                sp.wait_ge(xhat_ready, t - 1)
                sp.dma_start(xt[:, t % 2, :], xrow(k, t)).then_inc(x_in[t % 2], 16)

            load_x(2)
            for n in TURNS:
                if n + 3 < NT:
                    load_x(n + 3)
                t = n - 2
                if 0 <= t < NT:
                    sp.wait_ge(h_free, 3 * (t + 1))
                    sp.dma_start(k.va[tcols(t), :], hs[:, t % 2, C_VA:C_QL]).then_inc(out_v[t % 2], 16)
                t = n - 4
                if 0 <= t < NT:
                    sp.wait_ge(kv_free, 2 * (t + 1))
                    sp.dma_start(k.vm[tcols(t), :], kvs[:, t % 2, 1, :]).then_inc(out_vm[t % 2], 16)
                t = n - 3
                if 0 <= t < NT:
                    sp.wait_ge(t_free, number[n, 3] + 1)
                    sp.dma_start(rows(k.qa_t)[:, :, tcols(t)], q_tr[:, :, :]).then_inc(out_q[0], 16)
                    sp.wait_ge(t_free, number[n, 4] + 1)
                    sp.dma_start(k.ka_t[:, tcols(t)], k_tr[:, 0, :]).then_inc(out_k[0], 16)
                    sp.dma_start(k.kr_t[:, tcols(t)], k_tr[0:ROPE, 1, :]).then_inc(out_k[0], 16)
                t = n - 4
                if 0 <= t < NT:
                    sp.wait_ge(t_free, number[n, 6] + 1)
                    sp.dma_start(rows(k.qm_t, DM)[:, :, tcols(t)], qm_tr[:, :, :]).then_inc(out_qm[0], 16)
                    sp.wait_ge(t_free, number[n, 7] + 1)
                    sp.dma_start(rows(k.kn_t)[:, :, tcols(t)], kn_tr[:, :, :]).then_inc(out_kn[0], 16)
            for s in range(2):
                sp.wait_ge(out_v[s], 16 * (NT // 2))
                sp.wait_ge(out_vm[s], 16 * (NT // 2))
            sp.wait_ge(out_q[0], 16 * NT)
            sp.wait_ge(out_k[0], 32 * NT)
            sp.wait_ge(out_qm[0], 16 * NT)
            sp.wait_ge(out_kn[0], 16 * NT)

        @block.tensor
        def _(pe):
            def transposes(n, g, blocks):
                m = number[n, g]
                if m >= 2:
                    pe.wait_ge(t_free, m - 1)
                for q, src in enumerate(blocks):
                    mm = pe.transpose(bank(k, m % 2)[0:cols_of(src), q * P:(q + 1) * P], src, k.ident[:, :])
                mm.then_inc(t_ready, 1)

            def h_bank(t, b):
                lo, hi = BANKS_H[b]
                if t >= 1:
                    pe.wait_ge(h_free, 3 * (t - 1) + b + 1)
                out = bank(k, 2 + b)[:, 0:hi - lo]
                for j in range(KT):
                    mm = three(pe, out, [u[0][:, t % 2, j, :], u[1][:, t % 2, j, :]],
                               [w[:, j, lo:hi] for w in k.win], j == 0, j == KT - 1)
                mm.then_inc(h_ready, 1)

            for n in TURNS:
                a, b, c = n - 1, n - 3, n - 4
                if n < NT:
                    pe.wait_ge(xhat_ready, n + 1)
                    for g in range(2):
                        transposes(n, g, [xh[:, n % 2, (4 * g + q) * P:(4 * g + q + 1) * P] for q in range(4)])
                if 0 <= a < NT:
                    pe.wait_ge(u_ready, a + 1)
                    h_bank(a, 0)
                if 0 <= b < NT:
                    pe.wait_ge(lat_ready, b + 1)
                    transposes(n, 2, [lat[:, b % 2, q * P:(q + 1) * P] for q in range(3)])
                if 0 <= a < NT:
                    h_bank(a, 1)
                if 0 <= b < NT:
                    pe.wait_ge(qk_ready, b + 1)
                    transposes(n, 3, [qkr[:, b % 2, q * P:(q + 1) * P] for q in range(4)])
                    transposes(n, 4, [qkr[:, b % 2, 4 * P:5 * P], qkr[:, b % 2, QK_A:QK_A + ROPE]])
                if 0 <= a < NT:
                    h_bank(a, 2)
                if 0 <= b < NT:
                    pe.wait_ge(lath_ready, b + 1)
                    for half in range(2):
                        if b >= 1:
                            pe.wait_ge(kv_free, 2 * (b - 1) + half + 1)
                        out = bank(k, 6 + half)[:, 0:4 * DM]
                        for j in range(RQ // P):
                            mm = three(pe, out, [w[:, j, :] for w in lath],
                                       [w[:, j, half * 4 * DM:(half + 1) * 4 * DM] for w in k.wuq], j == 0, j == RQ // P - 1)
                        mm.then_inc(qm_ready, 1)
                if 0 <= c < NT:
                    pe.wait_ge(qm_roped, c + 1)
                    for g in range(2):
                        transposes(n, 5 + g, [qms[:, c % 2, (4 * g + q) * DM:(4 * g + q + 1) * DM] for q in range(4)])
                    transposes(n, 7, [kvs[:, c % 2, 0, q * P:(q + 1) * P] for q in range(4)])
                if 0 <= b < NT:
                    for half in range(2):
                        pe.wait_ge(qm_free, 2 * b + half + 1)
                        mm = three(pe, bank(k, 6 + half), [w[:, 2, :] for w in lath],
                                   [w[:, :].rearrange("p (h c) -> p h c", h=HM)[:, :, half * NOPE:(half + 1) * NOPE] for w in k.wukv],
                                   True, True)
                        mm.then_inc(kv_ready, 1)

        @block.scalar
        def _(act):
            def take(n, g):
                act.wait_ge(t_ready, number[n, g] + 1)
                return bank(k, number[n, g] % 2)

            def root_x(t):
                act.wait_ge(var_ready, t + 1)
                act.activation(std[:, t % 2, :], mv[:, t % 2, 1:2], ACT.Sqrt, bias=k.eps[:, 0:1]).then_inc(std_ready, 1)

            def h_copy(t, m):
                lo, hi = BANKS_H[m]
                act.wait_ge(h_ready, 3 * t + m + 1)
                if m == 0 and t >= 2:
                    act.wait_ge(out_v[t % 2], 16 * (t // 2))
                    act.wait_ge(qk_ready, t - 1)
                    act.wait_ge(lat_ready, t - 1)
                act.activation(hs[:, t % 2, lo:hi], bank(k, 2 + m)[:, 0:hi - lo], ACT.Copy).then_inc(h_free, 1)

            root_x(0)
            for n in TURNS:
                a, b, c = n - 1, n - 3, n - 4
                if n < NT:
                    if n == 0:
                        act.wait_ge(modp, 1)
                    if n >= 1:
                        act.wait_ge(u_ready, n)
                    seq = 0 if n < NTP else 1
                    for g in range(2):
                        src = take(n, g)
                        for q in range(4):
                            j = 4 * g + q
                            mm = act.activation(uf[:, j, :], src[:, q * P:(q + 1) * P], ACT.Identity,
                                                bias=modt[:, seq, 1, j:j + 1], scale=modt[:, seq, 0, j:j + 1])
                            if q < 3:
                                mm.then_inc(uf_ready, 1)
                        mm.then_inc(t_free, 1)
                if n + 1 < NT:
                    root_x(n + 1)
                if n < NT:
                    act.wait_ge(t_free, number[n, 1] + 1)
                    if n >= 2:
                        act.wait_ge(h_ready, 3 * (n - 1))
                    act.activation(u[0][:, n % 2, :, :], uf[:, :, :], ACT.Copy).then_inc(u_hi, 1)
                if 0 <= a < NT:
                    h_copy(a, 0)
                if 0 <= n - 2 < NT:
                    act.wait_ge(sums_ready, n - 1)
                    act.activation(rn[:, :], ssq[:, :], ACT.Sqrt, bias=k.eps[:, 0:1]).then_inc(root_ready, 1)
                if 0 <= b < NT:
                    src = take(n, 2)
                    if b >= 1:
                        act.wait_ge(lath_ready, b)
                    act.activation(latf[:, :, :], src[:, 0:3 * P].rearrange("p (q c) -> p q c", c=P), ACT.Copy).then_inc(t_free, 1)
                if 0 <= a < NT:
                    h_copy(a, 1)
                if 0 <= b < NT:
                    src = take(n, 3)
                    if b >= 1:
                        act.wait_ge(out_q[0], 16 * b)
                    act.activation(q_tr[:, :, :], src.rearrange("p (q c) -> p q c", c=P), ACT.Copy).then_inc(t_free, 1)
                    src = take(n, 4)
                    if b >= 1:
                        act.wait_ge(out_k[0], 32 * b)
                    act.activation(k_tr[:, 0, :], src[:, 0:P], ACT.Copy).then_inc(uf_ready, 1)
                    act.activation(k_tr[0:ROPE, 1, :], src[0:ROPE, P:2 * P], ACT.Copy).then_inc(t_free, 1)
                if 0 <= a < NT:
                    h_copy(a, 2)
                if 0 <= b < NT:
                    for half in range(2):
                        act.wait_ge(qm_ready, 2 * b + half + 1)
                        if half == 0 and b >= 2:
                            act.wait_ge(t_ready, number[b - 2 + 4, 6] + 1)
                        act.activation(qms[:, b % 2, half * 4 * DM:(half + 1) * 4 * DM], bank(k, 6 + half)[:, 0:4 * DM], ACT.Copy).then_inc(qm_free, 1)
                if 0 <= c < NT:
                    if c >= 1:
                        act.wait_ge(out_qm[0], 16 * c)
                    for g in range(2):
                        src = take(n, 5 + g)
                        act.activation(qm_tr[:, 4 * g:4 * g + 4, :], src[0:DM, :].rearrange("p (q c) -> p q c", c=P), ACT.Copy).then_inc(t_free, 1)
                    src = take(n, 7)
                    if c >= 1:
                        act.wait_ge(out_kn[0], 16 * c)
                    act.activation(kn_tr[:, :, :], src.rearrange("p (q c) -> p q c", c=P), ACT.Copy).then_inc(t_free, 1)
                if 0 <= b < NT:
                    for half in range(2):
                        act.wait_ge(kv_ready, 2 * b + half + 1)
                        if half == 1 and b >= 2:
                            act.wait_ge(out_vm[b % 2], 16 * (b // 2))
                        act.activation(kvs[:, b % 2, half, :], bank(k, 6 + half)[:, :], ACT.Copy).then_inc(kv_free, 1)

        @block.gpsimd
        def _(pool):
            for t in range(NT):
                pool.wait_ge(h_free, 3 * (t + 1))
                if t >= 1:
                    pool.wait_ge(sums_ready, t)
                pool.tensor_tensor(sq[:, 0:QK_A], hs[:, t % 2, 0:QK_A], hs[:, t % 2, 0:QK_A], ALU.mult).then_inc(pl, 1)
                pool.tensor_tensor(sq[:, C_QL:C_KR], hs[:, t % 2, C_QL:C_KR], hs[:, t % 2, C_QL:C_KR], ALU.mult).then_inc(sq_done, 1)

        @block.vector
        def _(dve):
            link = Link(dve, dv)

            def rope(out, x, cos, sin, heads, w, tmp):
                c2 = cos[:, None, None, :].to_broadcast([P, heads, 2, w])
                s1 = sin[:, None, :].to_broadcast([P, heads, w])
                link(dve.tensor_tensor(tmp[:, :, 0:w], x[:, :, w:2 * w], s1, ALU.mult))
                link(dve.tensor_tensor(tmp[:, :, w:2 * w], x[:, :, 0:w], s1, ALU.mult))
                link(dve.tensor_tensor(x.rearrange("p h (a c) -> p h a c", a=2), x.rearrange("p h (a c) -> p h a c", a=2), c2, ALU.mult))
                link(dve.tensor_tensor(out[:, :, 0:w], x[:, :, 0:w], tmp[:, :, 0:w], ALU.subtract))
                return dve.tensor_tensor(out[:, :, w:2 * w], x[:, :, w:2 * w], tmp[:, :, w:2 * w], ALU.add)

            dve.wait_ge(mod_in, 64)
            for s in range(2):
                m = dve.tensor_scalar(modt[:, s, 0, :], modt[:, s, 0, :], 1.0, None, ALU.add)
                if s == 0:
                    link(m)
            m.then_inc(modp, 1)

            def moments(t):
                dve.wait_ge(x_in[t % 2], 16 * (t // 2 + 1))
                for q in range(2):
                    link(dve.bn_stats(stats[:, t % 2, 6 * q:6 * q + 6], xt[:, t % 2, q * 512:(q + 1) * 512]))
                dve.bn_aggr(mv[:, t % 2, :], stats[:, t % 2, :]).then_inc(var_ready, 1)

            def x_hat(t):
                dve.wait_ge(std_ready, t + 1)
                dve.wait_ge(var_ready, t + 1)
                link(dve.reciprocal(std[:, t % 2, :], std[:, t % 2, :]))
                if t >= 2:
                    dve.wait_ge(t_ready, number[t - 2, 1] + 1)
                dve.tensor_scalar(xh[:, t % 2, :], xt[:, t % 2, :], mv[:, t % 2, 0:1], std[:, t % 2, :], ALU.subtract, ALU.mult).then_inc(xhat_ready, 1)

            def mla_rope(t):
                pos = t if t < NTP else t - NTP
                dve.wait_ge(qm_free, 2 * (t + 1))
                dve.wait_ge(qk_ready, min(t + 2, NT))
                x = qms[:, t % 2, :].rearrange("p (h c) -> p h c", c=DM)[:, :, NOPE:]
                rope(x, x, tab[:, pos, 64:80], tab[:, pos, 80:96], HM, ROPE // 2, mrot[:, :, :]).then_inc(qm_roped, 1)

            def sums(t):
                dve.wait_ge(sq_done, t + 1)
                dve.wait_ge(pl, t + 1)
                if t >= 1:
                    dve.wait_ge(root_ready, t)
                link(dve.reduce_sum(ssq[:, 0:heads], sq[:, 0:QK_A].rearrange("p (h c) -> p h c", c=DA), AX.X))
                link(dve.reduce_sum(ssq[:, heads:heads + 1], sq[:, C_QL:C_KVL], AX.X))
                link(dve.reduce_sum(ssq[:, heads + 1:heads + 2], sq[:, C_KVL:C_KR], AX.X))
                dve.tensor_tensor(ssq[:, :], ssq[:, :], inv_n[:, :], ALU.mult).then_inc(sums_ready, 1)

            def split_latents(t):
                dve.wait_ge(t_free, number[t + 3, 2] + 1)
                if t >= 1:
                    dve.wait_ge(kv_ready, 2 * t)
                link(dve.tensor_copy(lath[0][:, :, :], latf[:, :, :]))
                dve.tensor_tensor(lath[1][:, :, :], latf[:, :, :], lath[0][:, :, :], ALU.subtract).then_inc(lath_ready, 1)

            def norms(t):
                h = hs[:, t % 2, :]
                pos = t if t < NTP else t - NTP
                dve.wait_ge(root_ready, t + 1)
                link(dve.reciprocal(rn[:, :], rn[:, :]))
                if t >= 2:
                    dve.wait_ge(t_ready, number[t - 2 + 3, 2] + 1)
                link(dve.scalar_tensor_tensor(lat[:, t % 2, 0:RQ], h[:, C_QL:C_KVL], rn[:, heads:heads + 1], gain_lat[:, 0:RQ], ALU.mult, ALU.mult))
                dve.scalar_tensor_tensor(lat[:, t % 2, RQ:], h[:, C_KVL:C_KR], rn[:, heads + 1:heads + 2], gain_lat[:, RQ:], ALU.mult, ALU.mult).then_inc(lat_ready, 1)
                qk3 = qk[:, :].rearrange("p (h c) -> p h c", c=DA)
                link(dve.tensor_tensor(qk3, h[:, 0:QK_A].rearrange("p (h c) -> p h c", c=DA), rn[:, 0:heads, None].to_broadcast([P, heads, DA]), ALU.mult))
                link(dve.tensor_tensor(qk3[:, 0:HA, :], qk3[:, 0:HA, :], gain_qk[:, 0:1, :].to_broadcast([P, HA, DA]), ALU.mult))
                link(dve.tensor_tensor(qk3[:, HA:, :], qk3[:, HA:, :], gain_qk[:, 1:2, :].to_broadcast([P, KVA, DA]), ALU.mult))
                if t >= 2:
                    dve.wait_ge(t_ready, number[t - 2 + 3, 4] + 1)
                link(rope(qkr[:, t % 2, 0:QK_A].rearrange("p (h c) -> p h c", c=DA), qk3, tab[:, pos, 0:32], tab[:, pos, 32:64],
                          heads, DA // 2, rot[:, :].rearrange("p (h c) -> p h c", c=DA)))
                if t >= 2:
                    dve.wait_ge(qm_roped, t - 1)
                rope(qkr[:, t % 2, QK_A:].rearrange("p (h c) -> p h c", h=1), h[:, C_KR:].rearrange("p (h c) -> p h c", h=1),
                     tab[:, pos, 64:80], tab[:, pos, 80:96], 1, ROPE // 2, mrot[:, 0:1, :]).then_inc(qk_ready, 1)

            heads = HA + KVA
            moments(0)
            x_hat(0)
            for n in TURNS:
                if n + 1 < NT:
                    moments(n + 1)
                if 0 <= n - 4 < NT:
                    mla_rope(n - 4)
                if n + 1 < NT:
                    x_hat(n + 1)
                if n < NT:
                    dve.wait_ge(u_hi, n + 1)
                    dve.tensor_tensor(u[1][:, n % 2, :, :], uf[:, :, :], u[0][:, n % 2, :, :], ALU.subtract).then_inc(u_ready, 1)
                if n == 2:
                    dve.wait_ge(tabs_in, 96)
                if 0 <= n - 2 < NT:
                    sums(n - 2)
                if 0 <= n - 3 < NT:
                    split_latents(n - 3)
                if 0 <= n - 2 < NT:
                    norms(n - 2)


def cols_of(src):
    n = 1
    for s in src.shape[1:]:
        n *= s
    return n


def attention(k, stage):
    nc = k.nc
    sb = lambda name, shape, dt=F32: k.sb(stage, name, shape, dt)
    H = HA + HM
    RING = 3
    UNITS = 1 + S_SAMPLE // P
    PS = 3
    LAG = 2
    qf = sb("q_f32", [P, TOK])
    kf = sb("k_f32", [P, TOK])
    vf = sb("v_f32", [P, NT, VD])
    qs = [sb(f"q_{s}", [P, RING, TOK], F32R) for s in ("a", "b")]
    ks = [sb(f"k_{s}", [P, RING, TOK], F32R) for s in ("a", "b")]
    VC = VD + 2
    vs = [sb(f"v_{s}", [P, RING, NT, VC], F32R) for s in ("hi", "lo")]
    pf = sb("p_f32", [P, PS, 1024])
    ph = [sb(f"p_{s}", [P, PS, 1024], F32R) for s in ("hi", "lo")]
    mcol = sb("max_col", [P, NT])
    mrow = sb("neg_max_row", [NT, P], F32R)
    oc = sb("o_t", [VD + 1, TOK])
    rec = sb("recip_sum", [P, NT])
    on = sb("o_head", [P, 2, NT, VD])
    wo_raw = sb("w_out_raw", [P, D])
    gain = sb("grp_gain", [P, KT])

    q_in, k_in, v_in = k.sem("q_in"), k.sem("k_in"), k.sem("v_in")
    q_hi, k_hi, v_hi, q_lo, k_lo, v_lo = (k.sem(n) for n in ("q_hi_ready", "k_hi_ready", "v_hi_ready", "q_lo_ready", "k_lo_ready", "v_lo_ready"))
    ones, pool_link = k.sem("ones_rows"), k.sem("at_pool_link")
    s_ready, e_done, p_hi, p_lo, pv_done = (k.sem(n) for n in ("s_ready", "exp_done", "p_hi_ready", "p_lo_ready", "pv_done"))
    a_ready, a_free = k.sem("approx_ready"), k.sem("approx_free")
    m_tr, m_row, m_in = k.sem("max_tr"), k.sem("max_row"), k.sem("max_in")
    o_free, ot_ready, ot_free = k.sem("o_free"), k.sem("ot_ready"), k.sem("ot_free")
    rec_done = k.sem("rec_done")
    gain_in, wo_in, wo_hi, wo_lo = (k.sem(n) for n in ("gain_in", "wo_in", "wo_hi_ready", "wo_lo_ready"))
    o_out = [k.sem(f"o_out{s}") for s in range(2)]

    gqa = lambda g: g < HA
    GROUP = HA // KVA

    def kv(g):
        return g // GROUP if gqa(g) else KVA + g - HA

    def first_head(n):
        return n * GROUP if n < KVA else HA + n - KVA

    def last_head(n):
        return first_head(n) + (GROUP - 1 if n < KVA else 0)

    S_BANKS = [k.bank[0], k.bank[1]]
    A_PAIR, O_PAIR = k.bank[2], k.bank[3]
    ITEMS = UNITS
    SPREAD = {(0, "x"): 0, (0, "y"): 1, (1, "x"): 2, (1, "y"): 3, (2, "x"): 4, (3, "x"): 5, (3, "y"): 6, (4, "x"): 7, (5, "x"): 8}
    ROWS_AT = 6
    OUT_AT = sum(u < 2 or (u, z) == (2, "x") for u, z in SPREAD)

    def first_use(g):
        return (ITEMS + 1) * min(g + 1, 2) + (ITEMS + 2) * max(g - 1, 0)

    def item_use(g, i):
        return i if g == 0 else first_use(g - 1) + (g > 1 and i >= OUT_AT) + i

    def out_use(g):
        return first_use(g + 1) + OUT_AT if g < H - 2 else first_use(H - 1) + g - (H - 2)

    def use_before(eng, m):
        if m >= 1:
            eng.wait_ge(a_free, m)

    with nc.Block() as block:
        @block.sync
        def _(sp):
            for g in range(H):
                sp.wait_ge(m_row, g + 1)
                row = qs[1][DA:DA + 1, g % RING, :] if gqa(g) else qs[0][DM:DM + 1, g % RING, :]
                sp.dma_start(row.bitcast(F32), mrow[:, :].bitcast(F32)).then_inc(m_in, 16)

        @block.gpsimd
        def _(pool):
            def load(g):
                n = kv(g)
                if g >= 1:
                    pool.wait_ge(q_lo, g)
                if gqa(g):
                    for half in range(2):
                        pool.dma_start(qf[64 * half:64 * half + 64, :], k.qa_t[g * DA:(g + 1) * DA, :]).then_inc(q_in, 16)
                else:
                    h = g - HA
                    pool.dma_start(qf[0:48, :], k.qm_t[h * DM:h * DM + 48, :]).then_inc(q_in, 16)
                    pool.dma_start(qf[48:DM, :], k.qm_t[h * DM + 48:(h + 1) * DM, :]).then_inc(q_in, 16)
                if g != first_head(n):
                    return
                if n >= 1:
                    pool.wait_ge(k_lo, n)
                    pool.wait_ge(v_lo, n)
                if gqa(g):
                    for half in range(2):
                        pool.dma_start(kf[64 * half:64 * half + 64, :], k.ka_t[n * DA:(n + 1) * DA, :]).then_inc(k_in, 16)
                    pool.dma_start(vf[:, :, :], rows(k.va)[:, :, n * VD:(n + 1) * VD]).then_inc(v_in, 16)
                else:
                    pool.dma_start(kf[0:NOPE, :], k.kn_t[h * NOPE:(h + 1) * NOPE, :]).then_inc(k_in, 16)
                    pool.dma_start(kf[NOPE:DM, :], k.kr_t[:, :]).then_inc(k_in, 16)
                    pool.dma_start(vf[:, :, :], rows(k.vm)[:, :, h * VD:(h + 1) * VD]).then_inc(v_in, 16)

            def store(g):
                pool.wait_ge(a_free, out_use(g) + 1)
                pool.dma_start(rows(k.o)[:, :, g * VD:(g + 1) * VD], on[:, g % 2, :, :]).then_inc(o_out[g % 2], 16)

            def load_w_out(j):
                if j >= 1:
                    pool.wait_ge(wo_lo, j)
                pool.dma_start(wo_raw[:, :], rows(k.i["w_out"][0])[:, j, :]).then_inc(wo_in, 16)

            load(0)
            link = Link(pool, pool_link)
            for s in range(RING):
                link(pool.memset(vs[0][:, s, :, VD:VC].bitcast(F32), 1.0))
                link(pool.memset(vs[1][:, s, :, VD:VC].bitcast(F32), 0.0))
                ins = pool.memset(ks[1][DA:DA + 1, s, :].bitcast(F32), 1.0)
                if s < RING - 1:
                    link(ins)
            ins.then_inc(ones, 1)
            load(1)
            load(2)
            with nc.allow_non_contiguous_dma(reason="columns of gains, once"):
                for m, name in enumerate(("grp_norm_a", "grp_norm_b")):
                    pool.dma_start(gain[:, 4 * m:4 * m + 4], k.i[name][0, :].rearrange("(j p) -> p j", p=P)).then_inc(gain_in, 16)
            for g in range(H):
                if g + 3 < H:
                    load(g + 3)
                if g < KT:
                    load_w_out(g)
                store(g)
            for s in range(2):
                pool.wait_ge(o_out[s], 16 * (H // 2))

        @block.tensor
        def _(pe):
            def scores(g, u):
                c = g * UNITS + u
                if u == 0:
                    pe.wait_ge(m_in, 16 * (g + 1))
                if c >= 2:
                    pe.wait_ge(e_done, c - 1)
                out = S_BANKS[c % 2]
                s, n = g % RING, kv(g) % RING
                if u == 0:
                    jobs = [(out[:, 0, m * 256:(m + 1) * 256], m * P, slice(0, S_PROMPT)) for m in range(NTP)]
                else:
                    key = S_PROMPT + (u - 1) * P
                    jobs = [(out[:, m, :], key, slice(S_PROMPT + m * 512, S_PROMPT + (m + 1) * 512)) for m in range(2)]
                for dst, key, q in jobs:
                    kk = slice(key, key + P)
                    if gqa(g):
                        pe.matmul(dst, ks[0][:, n, kk], qs[0][:, s, q], start=True, stop=False)
                        mm = pe.matmul(dst, ks[1][0:DA + 1, n, kk], qs[1][0:DA + 1, s, q], start=False, stop=True)
                    else:
                        pe.matmul(dst, ks[0][0:DM + 1, n, kk], qs[0][0:DM + 1, s, q], start=True, stop=False)
                        pe.matmul(dst, ks[1][0:DM, n, kk], qs[0][0:DM, s, q], start=False, stop=False)
                        mm = pe.matmul(dst, ks[0][0:DM, n, kk], qs[1][0:DM, s, q], start=False, stop=True)
                mm.then_inc(s_ready, 1)

            def values(g, u):
                c = g * UNITS + u
                pe.wait_ge(p_lo, c + 1)
                if u == 0:
                    pe.wait_ge(v_lo, kv(g) + 1)
                    if g >= 1:
                        pe.wait_ge(o_free, 2 * g)
                if u == 1:
                    pe.wait_ge(o_free, 2 * g + 1)
                s = kv(g) % RING
                if u == 0:
                    jobs = [(O_PAIR[0:VD + 1, 0, 0:256], m, slice(m * 256, (m + 1) * 256), m == 0, m == NTP - 1) for m in range(NTP)]
                else:
                    jobs = [(O_PAIR[0:VD + 1, m, :], NTP + u - 1, slice(m * 512, (m + 1) * 512), u == 1, u == UNITS - 1) for m in range(2)]
                for dst, t, q, first, last in jobs:
                    v = [x[:, s, t, 0:VD + 1] for x in vs]
                    mm = three(pe, dst, v, [x[:, c % PS, q] for x in ph], first, last)
                mm.then_inc(pv_done, 1)

            def maxima(g, i):
                m = item_use(g, i)
                use_before(pe, m)
                if i == 0:
                    pe.wait_ge(q_lo, g + 1)
                    pe.wait_ge(k_lo, kv(g) + 1)
                    pe.wait_ge(ones, 1 + min(max(g - HA + 1, 0), RING))
                s, n = g % RING, kv(g) % RING
                w = P if gqa(g) else DM
                if i < ITEMS - 1:
                    q = slice(S_PROMPT + i * P, S_PROMPT + (i + 1) * P)
                    jobs = [(A_PAIR[:, c, :], q, slice(S_PROMPT + c * 512, S_PROMPT + (c + 1) * 512)) for c in range(2)]
                else:
                    jobs = [(A_PAIR[:, 0, c * 256:(c + 1) * 256], slice(c * P, (c + 1) * P), slice(0, S_PROMPT)) for c in range(NTP)]
                for dst, q, key in jobs:
                    mm = pe.matmul(dst, qs[0][0:w, s, q], ks[0][0:w, n, key], start=True, stop=True)
                mm.then_inc(a_ready, 1)

            def max_rows(g):
                m = item_use(g, ITEMS)
                use_before(pe, m)
                pe.transpose(A_PAIR[0:NT, 0, 0:P], mcol[:, :], k.ident[:, :]).then_inc(a_ready, 1)

            def outputs(g):
                use_before(pe, out_use(g))
                pe.wait_ge(o_free, 2 * (g + 1))
                for t in range(NT):
                    mm = pe.transpose(A_PAIR[:, t // 5, t % 5 * VC:t % 5 * VC + VD + 1], oc[:, t * P:(t + 1) * P], k.ident[0:VD + 1, 0:VD + 1])
                mm.then_inc(a_ready, 1)

            for i in range(ITEMS):
                maxima(0, i)
            max_rows(0)
            for g in range(H):
                for u in range(UNITS):
                    scores(g, u)
                    if g + 1 < H and (u, "x") in SPREAD:
                        maxima(g + 1, SPREAD[u, "x"])
                    if g + 1 < H and u == ROWS_AT:
                        max_rows(g + 1)
                    c = g * UNITS + u - LAG
                    if c >= 0:
                        values(c // UNITS, c % UNITS)
                    if u == 2 and g >= 1:
                        outputs(g - 1)
                    if g + 1 < H and (u, "y") in SPREAD:
                        maxima(g + 1, SPREAD[u, "y"])
            for u in range(UNITS - LAG, UNITS):
                values(H - 1, u)
            outputs(H - 1)

        @block.scalar
        def _(act):
            def round_q(g):
                act.wait_ge(q_in, 32 * (g + 1))
                if g >= RING:
                    act.wait_ge(s_ready, UNITS * (g - RING + 1))
                s = g % RING
                if gqa(g):
                    act.activation(qs[1][0:DA, s, :], qf[0:DA, :], ACT.Copy)
                    act.activation(qs[0][:, s, :], qf[:, :], ACT.Copy).then_inc(q_hi, 1)
                else:
                    act.activation(qs[0][0:DM, s, :], qf[0:DM, :], ACT.Copy).then_inc(q_hi, 1)

            def round_k(n):
                act.wait_ge(k_in, 32 * (n + 1))
                if n >= RING:
                    act.wait_ge(s_ready, UNITS * (last_head(n - RING) + 1))
                w = P if n < KVA else DM
                act.activation(ks[0][0:w, n % RING, :], kf[0:w, :], ACT.Copy).then_inc(k_hi, 1)

            def round_v(n):
                act.wait_ge(v_in, 16 * (n + 1))
                if n >= RING:
                    act.wait_ge(pv_done, UNITS * (last_head(n - RING) + 1))
                act.activation(vs[0][:, n % RING, :, 0:VD], vf[:, :, :], ACT.Copy).then_inc(v_hi, 1)

            def exp(g, u):
                c = g * UNITS + u
                scale = DA ** -0.5 if gqa(g) else DM ** -0.5
                act.wait_ge(s_ready, c + 1)
                if c >= PS:
                    act.wait_ge(p_lo, c - PS + 1)
                w = 512 if u == 0 else 1024
                src = S_BANKS[c % 2][:, :, :].rearrange("p a b -> p (a b)")[:, 0:w]
                act.activation(pf[:, c % PS, 0:w], src, ACT.Exp, scale=scale).then_inc(e_done, 1)
                act.wait_ge(e_done, c + 1)
                if c >= PS:
                    act.wait_ge(pv_done, c - PS + 1)
                act.activation(ph[0][:, c % PS, 0:w], pf[:, c % PS, 0:w], ACT.Copy).then_inc(p_hi, 1)

            def take_outputs(g, part):
                act.wait_ge(pv_done, g * UNITS + (1 if part == 0 else UNITS))
                if part == 0:
                    if g >= 1:
                        act.wait_ge(a_ready, out_use(g - 1) + 1)
                    act.activation(oc[:, 0:S_PROMPT], O_PAIR[0:VD + 1, 0, 0:S_PROMPT], ACT.Copy).then_inc(o_free, 1)
                else:
                    act.activation(oc[:, S_PROMPT:], O_PAIR[0:VD + 1, :, :].rearrange("p a b -> p (a b)"), ACT.Copy).then_inc(o_free, 1)

            def w_out_hi(j):
                act.wait_ge(gain_in, 32)
                act.wait_ge(wo_in, 16 * (j + 1))
                act.activation(k.wo[0][:, j, :], wo_raw[:, :], ACT.Copy, scale=gain[:, j:j + 1]).then_inc(wo_hi, 1)

            round_q(0)
            round_k(0)
            round_v(0)
            round_q(1)
            for g in range(H):
                for u in range(UNITS):
                    exp(g, u)
                    if u == 1 and g >= 1:
                        take_outputs(g - 1, 1)
                    if g + 2 < H and u == 4:
                        round_q(g + 2)
                    if g + 2 < H and first_head(kv(g + 2)) == g + 2:
                        if u == 5:
                            round_k(kv(g + 2))
                        if u == 6:
                            round_v(kv(g + 2))
                    if u == 2:
                        take_outputs(g, 0)
                    if u == 7 and 1 <= g <= KT:
                        w_out_hi(g - 1)
            take_outputs(H - 1, 1)

        @block.vector
        def _(dve):
            def low_q(g):
                dve.wait_ge(q_hi, g + 1)
                s = g % RING
                if gqa(g):
                    ins = dve.tensor_tensor(qs[0][DA:P, s, :], qf[DA:P, :], qs[0][DA:P, s, :], ALU.subtract)
                else:
                    if g < HA + RING:
                        dve.memset(ks[0][DM:DM + 1, kv(g) % RING, :].bitcast(F32), 1.0).then_inc(ones, 1)
                    ins = dve.tensor_tensor(qs[1][0:DM, s, :], qf[0:DM, :], qs[0][0:DM, s, :], ALU.subtract)
                ins.then_inc(q_lo, 1)

            def low_k(n):
                dve.wait_ge(k_hi, n + 1)
                s, w = n % RING, DA if n < KVA else DM
                dve.tensor_tensor(ks[1][0:w, s, :], kf[0:w, :], ks[0][0:w, s, :], ALU.subtract).then_inc(k_lo, 1)

            def low_v(n):
                dve.wait_ge(v_hi, n + 1)
                dve.tensor_tensor(vs[1][:, n % RING, :, 0:VD], vf[:, :, :], vs[0][:, n % RING, :, 0:VD], ALU.subtract).then_inc(v_lo, 1)

            def p_low(g, u):
                c = g * UNITS + u
                w = 512 if u == 0 else 1024
                dve.wait_ge(p_hi, c + 1)
                dve.tensor_tensor(ph[1][:, c % PS, 0:w], pf[:, c % PS, 0:w], ph[0][:, c % PS, 0:w], ALU.subtract).then_inc(p_lo, 1)

            def maximum(g, i):
                m = item_use(g, i)
                dve.wait_ge(a_ready, m + 1)
                if i == 0 and g >= 1:
                    dve.wait_ge(a_ready, item_use(g - 1, ITEMS) + 1)
                if i < ITEMS - 1:
                    dve.reduce_max(mcol[:, NTP + i:NTP + i + 1], A_PAIR[:, :, :].rearrange("p a b -> p (a b)"), AX.X).then_inc(a_free, 1)
                else:
                    dve.reduce_max(mcol[:, 0:NTP], A_PAIR[:, 0, :].rearrange("p (a b) -> p a b", a=NTP), AX.X).then_inc(a_free, 1)

            def max_row(g):
                dve.wait_ge(a_ready, item_use(g, ITEMS) + 1)
                if g >= 1:
                    dve.wait_ge(m_in, 16 * g)
                dve.tensor_scalar(mrow[:, :], A_PAIR[0:NT, 0, 0:P], -1.0, None, ALU.mult).then_inc(m_row, 1)
                dve.wait_ge(m_row, g + 1)
                dve.engine_nop().then_inc(a_free, 1)

            def normalise(g):
                dve.wait_ge(a_ready, out_use(g) + 1)
                if g >= 2:
                    dve.wait_ge(o_out[g % 2], 16 * (g // 2))
                for m in range(2):
                    tr = A_PAIR[:, m, 0:5 * VC].rearrange("p (t c) -> p t c", c=VC)
                    dve.reciprocal(rec[:, 5 * m:5 * m + 5, None], tr[:, :, VD:VD + 1]).then_inc(rec_done, 1)
                    dve.wait_ge(rec_done, 2 * g + m + 1)
                    ins = dve.tensor_tensor(on[:, g % 2, 5 * m:5 * m + 5, :], tr[:, :, 0:VD],
                                            rec[:, 5 * m:5 * m + 5, None].to_broadcast([P, 5, VD]), ALU.mult)
                ins.then_inc(a_free, 1)

            def w_out_low(j):
                dve.wait_ge(wo_hi, j + 1)
                dve.scalar_tensor_tensor(k.wo[1][:, j, :], wo_raw[:, :], gain[:, j:j + 1], k.wo[0][:, j, :], ALU.mult, ALU.subtract).then_inc(wo_lo, 1)

            low_q(0)
            low_k(0)
            for i in range(ITEMS):
                maximum(0, i)
            max_row(0)
            low_v(0)
            low_q(1)
            for g in range(H):
                for u in range(UNITS):
                    if g + 1 < H and (u, "x") in SPREAD:
                        maximum(g + 1, SPREAD[u, "x"])
                    if g + 1 < H and u == ROWS_AT:
                        max_row(g + 1)
                    c = g * UNITS + u - 1
                    if c >= 0:
                        p_low(c // UNITS, c % UNITS)
                    if u == 2 and g >= 1:
                        normalise(g - 1)
                    if g + 2 < H and u == 5:
                        low_q(g + 2)
                    if g + 2 < H and first_head(kv(g + 2)) == g + 2:
                        if u == 6:
                            low_k(kv(g + 2))
                        if u == 7:
                            low_v(kv(g + 2))
                    if u == 8 and 1 <= g <= KT:
                        w_out_low(g - 1)
                    if g + 1 < H and (u, "y") in SPREAD:
                        maximum(g + 1, SPREAD[u, "y"])
            p_low(H - 1, UNITS - 1)
            normalise(H - 1)


def output(k, stage):
    nc = k.nc
    sb = lambda name, shape, dt=F32: k.sb(stage, name, shape, dt)
    modt = sb("mod_mid_t", [P, 2, 2, KT])
    g1 = sb("gate_1", [P, 2, D])
    ln1 = sb("ln1_gain_bias", [P, 2, D])
    ot = sb("o_tile", [P, 3, D])
    junk = sb("squares_c", [P, 512])
    ss = sb("grp_sums", [P, 3, 2])
    mt = [sb(f"mix_t_{s}", [P, 2, KT, P], F32R) for s in ("hi", "lo")]
    y = sb("y", [P, 2, D])
    r = sb("gated_or_x_hat", [P, D])
    uf = sb("u2_f32", [P, KT, P])
    stats = sb("stats_c", [P, 2, 12])
    mv = sb("mean_var_c", [P, 2, 2])
    std = sb("std_c", [P, 2, 1])

    tabs_in, modp = k.sem("oc_tabs_in"), k.sem("oc_mod_plus_one")
    o_in, x_in = [k.sem(f"oc_o_in{s}") for s in range(3)], [k.sem(f"oc_x_in{s}") for s in range(2)]
    ss_ready, on_ready = k.sem("ss_ready"), k.sem("on_ready")
    mt_tr, mt_hi, mt_lo = k.sem("mt_tr"), k.sem("mt_hi"), k.sem("mt_lo")
    mix_ready, mix_free = k.sem("mix_ready"), k.sem("mix_free")
    var_ready, std_ready = k.sem("oc_var"), k.sem("oc_std")
    x1_ready, x1_out = k.sem("x1_ready"), [k.sem(f"x1_out{s}") for s in range(2)]
    xh_ready, u_tr, uf_ready, u2_hi, u2_ready = (k.sem(n) for n in ("oc_xhat", "oc_u_tr", "oc_uf", "u2_hi_ready", "u2_ready"))
    dv, ac = k.sem("oc_dve_link"), k.sem("oc_act_link")
    TURNS = range(NT + 3)

    with nc.Block() as block:
        @block.sync
        def _(sp):
            def load_o(t):
                sp.dma_start(ot[:, t % 3, :], k.o[t * P:(t + 1) * P, :]).then_inc(o_in[t % 3], 16)

            def load_x(t):
                sp.dma_start(y[:, t % 2, :], xrow(k, t)).then_inc(x_in[t % 2], 16)

            for t in range(3):
                load_o(t)
            with nc.allow_non_contiguous_dma(reason="columns of the modulation, once"):
                for s in range(2):
                    for m, part in enumerate((4, 3)):
                        sp.dma_start(modt[:, s, m, :], k.mod[s, part * D:(part + 1) * D].rearrange("(j p) -> p j", p=P)).then_inc(tabs_in, 16)
            for t in range(2):
                load_x(t)
            for s in range(2):
                sp.dma_start(g1[:, s, :], k.mod[s, 2 * D:3 * D].partition_broadcast(P)).then_inc(tabs_in, 16)
            for m, g in enumerate(("ln1_g", "ln1_b")):
                sp.dma_start(ln1[:, m, :], k.i[g][0, :].partition_broadcast(P)).then_inc(tabs_in, 16)
            for n in TURNS:
                if n + 3 < NT:
                    sp.wait_ge(mt_tr, 2 * (n + 1))
                    load_o(n + 3)
                t = n - 2
                if 0 <= t < NT:
                    sp.wait_ge(x1_ready, t + 1)
                    sp.dma_start(k.x1[t * P:(t + 1) * P, :], y[:, t % 2, :]).then_inc(x1_out[t % 2], 16)
                    if t + 2 < NT:
                        sp.wait_ge(x1_out[t % 2], 16 * (t // 2 + 1))
                        sp.wait_ge(xh_ready, t + 1)
                        load_x(t + 2)
            for s in range(2):
                sp.wait_ge(x1_out[s], 16 * (NT // 2))

        @block.tensor
        def _(pe):
            def mix_t(t):
                pe.wait_ge(on_ready, t + 1)
                for m in range(2):
                    if t >= 1:
                        pe.wait_ge(mt_lo, 2 * (t - 1) + m + 1)
                    for q in range(4):
                        j = 4 * m + q
                        mm = pe.transpose(bank(k, m)[:, q * P:(q + 1) * P], ot[:, t % 3, j * P:(j + 1) * P], k.ident[:, :])
                    mm.then_inc(mt_tr, 1)

            def mix(t):
                pe.wait_ge(mt_lo, 2 * (t + 1))
                if t >= 2:
                    pe.wait_ge(mix_free, t - 1)
                out = k.bank[1 + t % 2]
                for m in range(2):
                    for j in range(KT):
                        mm = three(pe, out[:, m, :], [x[:, t % 2, j, :] for x in mt],
                                   [w[:, j, m * 512:(m + 1) * 512] for w in k.wo], j == 0, j == KT - 1)
                mm.then_inc(mix_ready, 1)

            def u_t(t):
                pe.wait_ge(xh_ready, t + 1)
                if t >= 1:
                    pe.wait_ge(uf_ready, t)
                for j in range(KT):
                    mm = pe.transpose(k.bank[3][:, j // 4, j % 4 * P:(j % 4 + 1) * P], r[:, j * P:(j + 1) * P], k.ident[:, :])
                mm.then_inc(u_tr, 1)

            for n in TURNS:
                if 0 <= n - 3 < NT:
                    u_t(n - 3)
                if n < NT:
                    mix_t(n)
                if 0 <= n - 1 < NT:
                    mix(n - 1)

        @block.scalar
        def _(act):
            def squares(t):
                act.wait_ge(o_in[t % 3], 16 * (t // 3 + 1))
                for m in range(2):
                    ins = act.activation(junk[:, :], ot[:, t % 3, m * 512:(m + 1) * 512], ACT.Square, accum_out=ss[:, t % 3, m:m + 1])
                    ins.then_inc(ac, 1)
                    act.wait_ge(ac, 2 * t + m + 1)
                act.activation(ss[:, t % 3, :], ss[:, t % 3, :], ACT.Sqrt, scale=1.0 / 512, bias=k.eps[:, 0:1]).then_inc(ss_ready, 1)

            def mix_hi(t):
                for m in range(2):
                    act.wait_ge(mt_tr, 2 * t + m + 1)
                    if m == 0 and t >= 2:
                        act.wait_ge(mix_ready, t - 1)
                    act.activation(mt[0][:, t % 2, 4 * m:4 * m + 4, :], bank(k, m).rearrange("p (q c) -> p q c", c=P), ACT.Copy).then_inc(mt_hi, 1)

            def root(t, which):
                act.wait_ge(var_ready, 2 * t + which + 1)
                act.activation(std[:, which, :], mv[:, which, 1:2], ACT.Sqrt, bias=k.eps[:, 0:1]).then_inc(std_ready, 1)

            def modulate(t):
                act.wait_ge(u_tr, t + 1)
                if t == 0:
                    act.wait_ge(modp, 1)
                if t >= 1:
                    act.wait_ge(u2_ready, t)
                seq = 0 if t < NTP else 1
                for j in range(KT):
                    ins = act.activation(uf[:, j, :], k.bank[3][:, j // 4, j % 4 * P:(j % 4 + 1) * P], ACT.Identity,
                                         bias=modt[:, seq, 1, j:j + 1], scale=modt[:, seq, 0, j:j + 1])
                ins.then_inc(uf_ready, 1)
                act.wait_ge(uf_ready, t + 1)
                act.activation(k.u2[0][:, :, t * P:(t + 1) * P], uf[:, :, :], ACT.Copy).then_inc(u2_hi, 1)

            squares(0)
            squares(1)
            for n in TURNS:
                if 0 <= n - 3 < NT:
                    modulate(n - 3)
                if n < NT:
                    mix_hi(n)
                if 0 <= n - 2 < NT:
                    root(n - 2, 0)
                if n + 2 < NT:
                    squares(n + 2)
                if 0 <= n - 2 < NT:
                    root(n - 2, 1)

        @block.vector
        def _(dve):
            link = Link(dve, dv)

            def group_norm(t):
                dve.wait_ge(ss_ready, t + 1)
                link(dve.reciprocal(ss[:, t % 3, :], ss[:, t % 3, :]))
                for m in range(2):
                    ins = dve.tensor_scalar(ot[:, t % 3, m * 512:(m + 1) * 512], ot[:, t % 3, m * 512:(m + 1) * 512],
                                            ss[:, t % 3, m:m + 1], None, ALU.mult)
                ins.then_inc(on_ready, 1)

            def mix_lo(t):
                for m in range(2):
                    dve.wait_ge(mt_hi, 2 * t + m + 1)
                    dve.tensor_tensor(mt[1][:, t % 2, 4 * m:4 * m + 4, :], bank(k, m).rearrange("p (q c) -> p q c", c=P),
                                      mt[0][:, t % 2, 4 * m:4 * m + 4, :], ALU.subtract).then_inc(mt_lo, 1)

            def moments(t, which):
                for m in range(2):
                    link(dve.bn_stats(stats[:, which, 6 * m:6 * m + 6], y[:, t % 2, m * 512:(m + 1) * 512]))
                dve.bn_aggr(mv[:, which, :], stats[:, which, :]).then_inc(var_ready, 1)

            def norm(t, which, out):
                dve.wait_ge(var_ready, 2 * t + which + 1)
                dve.wait_ge(std_ready, 2 * t + which + 1)
                link(dve.reciprocal(std[:, which, :], std[:, which, :]))
                return dve.tensor_scalar(out, y[:, t % 2, :], mv[:, which, 0:1], std[:, which, :], ALU.subtract, ALU.mult)

            def residual(t):
                seq = 0 if t < NTP else 1
                dve.wait_ge(mix_ready, t + 1)
                if t >= 1:
                    dve.wait_ge(u_tr, t)
                dve.tensor_tensor(r[:, :], k.bank[1 + t % 2][:, :, :].rearrange("p a b -> p (a b)"), g1[:, seq, :], ALU.mult).then_inc(mix_free, 1)
                dve.wait_ge(mix_free, t + 1)
                dve.wait_ge(x_in[t % 2], 16 * (t // 2 + 1))
                link(dve.scalar_tensor_tensor(y[:, t % 2, :], y[:, t % 2, :], ALPHA, r[:, :], ALU.mult, ALU.add))
                moments(t, 0)

            def first_norm(t):
                yt = y[:, t % 2, :]
                link(norm(t, 0, yt))
                link(dve.tensor_tensor(yt, yt, ln1[:, 0, :], ALU.mult))
                dve.tensor_tensor(yt, yt, ln1[:, 1, :], ALU.add).then_inc(x1_ready, 1)
                dve.wait_ge(x1_ready, t + 1)
                moments(t, 1)

            def u_low(t):
                cols = slice(t * P, (t + 1) * P)
                dve.wait_ge(u2_hi, t + 1)
                dve.tensor_tensor(k.u2[1][:, :, cols], uf[:, :, :], k.u2[0][:, :, cols], ALU.subtract).then_inc(u2_ready, 1)

            group_norm(0)
            for n in TURNS:
                if n + 1 < NT:
                    group_norm(n + 1)
                if n == 0:
                    dve.wait_ge(tabs_in, 128)
                    for s in range(2):
                        ins = dve.tensor_scalar(modt[:, s, 0, :], modt[:, s, 0, :], 1.0, None, ALU.add)
                    ins.then_inc(modp, 1)
                if 0 <= n - 2 < NT:
                    residual(n - 2)
                if n < NT:
                    mix_lo(n)
                if 0 <= n - 2 < NT:
                    first_norm(n - 2)
                if 0 <= n - 3 < NT:
                    u_low(n - 3)
                if 0 <= n - 2 < NT:
                    norm(n - 2, 1, r[:, :]).then_inc(xh_ready, 1)


def channel(k, stage):
    nc = k.nc
    sumf = k.sb(stage, "sum_f", [P, NT, D])
    with ExitStack() as inner:
        sb = lambda name, shape, dt=F32: k.sb(inner, name, shape, dt)
        raw_gu = sb("gate_up_raw", [P, 2, KT, P])
        raw_d = sb("down_raw", [P, D])
        wgu = [sb(f"gate_up_{s}", [P, 2, 2, KT, P], F32R) for s in ("hi", "lo")]
        wd = [sb(f"down_{s}", [P, 2, D], F32R) for s in ("hi", "lo")]
        sg = sb("silu_gate", [P, 512])
        hf = sb("hidden_f32", [P, 512])
        hid = [sb(f"hidden_{s}", [P, TOK], F32R) for s in ("hi", "lo")]
        gu_in, d_in = k.sem("gu_in"), k.sem("down_in")
        gu_hi, gu_lo, d_hi, d_lo = (k.sem(n) for n in ("gu_hi", "gu_lo", "down_hi", "down_lo"))
        gu_ready, silu_done, h_ready, hid_hi, hid_lo = (k.sem(n) for n in ("gu_ready", "silu_done", "ff_h", "hid_hi", "hid_lo"))
        dn_ready, dn_added = k.sem("down_ready"), k.sem("down_added")
        TILES = [range(c[0] // P, c[1] // P) for c in CHUNKS]
        NCH = len(CHUNKS)

        def run(eng, body):
            body(0, 0, True)
            body(1, 1, False)
            with eng.Fori(2, NF, 2) as i:
                body(i, 0, False)
                body(i + 1, 1, False)
            body(NF, 0, False, last=True)

        def prev(f, c):
            return (c - 1) % NCH, NCH * f + c

        with nc.Block() as block:
            @block.sync
            def _(sp):
                wg, wu, w_dn = rows(k.i["w_gate"][0]), rows(k.i["w_up"][0]), rows(k.i["w_down"][0])

                def load(f, wait=True):
                    if wait:
                        sp.wait_ge(gu_lo, f)
                    for m, w in enumerate((k.i["w_gate"][0], k.i["w_up"][0])):
                        sp.dma_start(raw_gu[:, m, :, :], rows(w)[:, :, bass.ds(f * P, P)]).then_inc(gu_in, 16)
                    if wait:
                        sp.wait_ge(d_lo, f)
                    sp.dma_start(raw_d[:, :], k.i["w_down"][0][bass.ds(f * P, P), :]).then_inc(d_in, 16)

                load(0, wait=False)
                load(1)
                with sp.Fori(2, NF) as f:
                    load(f)

            @block.tensor
            def _(pe):
                def down(f, t, slot):
                    if t < 2 and isinstance(f, int) and f == 1:
                        pass
                    else:
                        pe.wait_ge(dn_added, NT * (f - 1) + t - 1)
                    for m in range(2):
                        mm = three(pe, k.bank[2 + t % 2][:, m, :], [x[:, t * P:(t + 1) * P] for x in hid],
                                   [w[:, 1 - slot, m * 512:(m + 1) * 512] for w in wd], True, True)
                    mm.then_inc(dn_ready, 1)

                def body(f, slot, first, last=False):
                    for c, (lo, hi) in enumerate(CHUNKS):
                        if not first:
                            pe.wait_ge(hid_lo, NCH * (f - 1) + c + 1)
                            if c == 0:
                                pe.wait_ge(d_lo, f)
                            for t in TILES[c]:
                                down(f, t, slot)
                        if last:
                            continue
                        if c == 0:
                            pe.wait_ge(gu_lo, f + 1)
                        out = k.bank[(slot + c) % 2]
                        if not (first and c < 2):
                            pe.wait_ge(h_ready, NCH * f + c - 1)
                        for m in range(2):
                            for j in range(KT):
                                mm = three(pe, out[:, m, 0:hi - lo], [w[:, slot, m, j, :] for w in wgu],
                                           [x[:, j, lo:hi] for x in k.u2], j == 0, j == KT - 1)
                        mm.then_inc(gu_ready, 1)

                run(pe, body)

            @block.scalar
            def _(act):
                def gu_round(f, slot, first):
                    act.wait_ge(gu_in, 32 * (f + 1))
                    if not first:
                        act.wait_ge(gu_ready, NCH * (f - 1))
                    act.activation(wgu[0][:, slot, :, :, :], raw_gu[:, :, :, :], ACT.Copy).then_inc(gu_hi, 1)

                def d_round(f, slot, first):
                    act.wait_ge(d_in, 16 * (f + 1))
                    if not first:
                        act.wait_ge(dn_ready, NT * (f - 1))
                    act.activation(wd[0][:, slot, :], raw_d[:, :], ACT.Copy).then_inc(d_hi, 1)

                def silu(f, c, slot):
                    pc, m = prev(f, c)
                    lo, hi = CHUNKS[pc]
                    act.wait_ge(gu_ready, m)
                    if not (isinstance(m, int) and m == 1):
                        act.wait_ge(h_ready, m - 1)
                    act.activation(sg[:, 0:hi - lo], k.bank[(slot + c + 1) % 2][:, 0, 0:hi - lo], ACT.Silu).then_inc(silu_done, 1)
                    act.wait_ge(h_ready, m)
                    if not (isinstance(f, int) and (f == 0 or (f == 1 and c == 0))):
                        act.wait_ge(dn_ready, NT * (f - 1 - (c == 0)) + TILES[pc][-1] + 1)
                    act.activation(hid[0][:, lo:hi], hf[:, 0:hi - lo], ACT.Copy).then_inc(hid_hi, 1)

                gu_round(0, 0, True)

                def body(f, slot, first, last=False):
                    for c in range(NCH):
                        if not (first and c == 0) and not (last and c > 0):
                            silu(f, c, slot)
                        if last:
                            continue
                        if c == 1:
                            d_round(f, slot, isinstance(f, int) and f < 2)
                        if c == 2:
                            if isinstance(f, int):
                                gu_round(f + 1, 1 - slot, f == 0)
                            elif slot == 0:
                                gu_round(f + 1, 1, False)
                            else:
                                with act.If(f + 1 < NF):
                                    gu_round(f + 1, 0, False)

                run(act, body)

            @block.vector
            def _(dve):
                def gu_low(f, slot):
                    dve.wait_ge(gu_hi, f + 1)
                    dve.tensor_tensor(wgu[1][:, slot, :, :, :], raw_gu[:, :, :, :], wgu[0][:, slot, :, :, :], ALU.subtract).then_inc(gu_lo, 1)

                def d_low(f, slot):
                    dve.wait_ge(d_hi, f + 1)
                    dve.tensor_tensor(wd[1][:, slot, :], raw_d[:, :], wd[0][:, slot, :], ALU.subtract).then_inc(d_lo, 1)

                def product(f, c, slot):
                    pc, m = prev(f, c)
                    lo, hi = CHUNKS[pc]
                    dve.wait_ge(silu_done, m)
                    if not (isinstance(m, int) and m == 1):
                        dve.wait_ge(hid_lo, m - 1)
                    dve.tensor_tensor(hf[:, 0:hi - lo], k.bank[(slot + c + 1) % 2][:, 1, 0:hi - lo], sg[:, 0:hi - lo], ALU.mult).then_inc(h_ready, 1)

                def hidden_low(f, c):
                    pc, m = prev(f, c)
                    lo, hi = CHUNKS[pc]
                    dve.wait_ge(hid_hi, m)
                    dve.tensor_tensor(hid[1][:, lo:hi], hf[:, 0:hi - lo], hid[0][:, lo:hi], ALU.subtract).then_inc(hid_lo, 1)

                def add(f, t):
                    dve.wait_ge(dn_ready, NT * (f - 1) + t + 1)
                    src = k.bank[2 + t % 2][:, :, :].rearrange("p a b -> p (a b)")
                    if isinstance(f, int) and f == 1:
                        dve.tensor_copy(sumf[:, t, :], src).then_inc(dn_added, 1)
                    else:
                        dve.wait_ge(dn_added, NT * (f - 2) + t + 1)
                        dve.tensor_tensor(sumf[:, t, :], src, sumf[:, t, :], ALU.add).then_inc(dn_added, 1)

                gu_low(0, 0)

                def body(f, slot, first, last=False):
                    for c in range(NCH):
                        before = not (first and c == 0) and not (last and c > 0)
                        tiles = [] if first else list(TILES[c])
                        for q in range(max(len(tiles), 2)):
                            if q < len(tiles):
                                add(f, tiles[q])
                            if before and q == 0:
                                product(f, c, slot)
                            if before and q == 1:
                                hidden_low(f, c)
                        if last:
                            continue
                        if c == 1:
                            d_low(f, slot)
                        if c == 2:
                            if isinstance(f, int) or slot == 0:
                                gu_low(f + 1, 1 - slot)
                            else:
                                with dve.If(f + 1 < NF):
                                    gu_low(f + 1, 0)

                run(dve, body)

    with ExitStack() as inner:
        last_norm(k, inner, sumf)


def last_norm(k, stage, sumf):
    nc = k.nc
    sb = lambda name, shape, dt=F32: k.sb(stage, name, shape, dt)
    g2 = sb("gate_2", [P, 2, D])
    ln2 = sb("ln2_gain_bias", [P, 2, D])
    xt = sb("x1_tile", [P, 2, D])
    z = sb("z", [P, 3, D])
    stats = sb("stats_e", [P, 2, 12])
    mv = sb("mean_var_e", [P, 2, 2])
    std = sb("std_e", [P, 2, 1])
    tabs_in, x_in = k.sem("e_tabs_in"), [k.sem(f"e_x_in{s}") for s in range(2)]
    y_ready, var_ready, std_ready, hat_ready, gained, out_ready = (k.sem(n) for n in ("e_y", "e_var", "e_std", "e_hat", "e_gained", "e_out"))
    y_out = [k.sem(f"e_stored{s}") for s in range(3)]
    dv = k.sem("e_dve_link")

    with nc.Block() as block:
        @block.sync
        def _(sp):
            for s in range(2):
                sp.dma_start(g2[:, s, :], k.mod[s, 5 * D:6 * D].partition_broadcast(P)).then_inc(tabs_in, 16)
            for t in range(2):
                sp.dma_start(xt[:, t, :], k.x1[t * P:(t + 1) * P, :]).then_inc(x_in[t], 16)
            for m, g in enumerate(("ln2_g", "ln2_b")):
                sp.dma_start(ln2[:, m, :], k.i[g][0, :].partition_broadcast(P)).then_inc(tabs_in, 16)
            for t in range(NT):
                if t + 2 < NT:
                    sp.wait_ge(y_ready, t + 1)
                    sp.dma_start(xt[:, t % 2, :], k.x1[(t + 2) * P:(t + 3) * P, :]).then_inc(x_in[t % 2], 16)
                sp.wait_ge(out_ready, t + 1)
                dst = k.o_prompt(t) if t < NTP else k.o_sample(t - NTP)
                sp.dma_start(dst, z[:, t % 3, :]).then_inc(y_out[t % 3], 16)
            for s in range(3):
                sp.wait_ge(y_out[s], 16 * len(range(s, NT, 3)))

        @block.scalar
        def _(act):
            for t in range(NT):
                act.wait_ge(var_ready, t + 1)
                act.activation(std[:, t % 2, :], mv[:, t % 2, 1:2], ACT.Sqrt, bias=k.eps[:, 0:1]).then_inc(std_ready, 1)

        @block.gpsimd
        def _(pool):
            for t in range(NT):
                pool.wait_ge(gained, t + 1)
                pool.tensor_tensor(z[:, t % 3, :], z[:, t % 3, :], ln2[:, 1, :], ALU.add).then_inc(out_ready, 1)

        @block.vector
        def _(dve):
            link = Link(dve, dv)
            dve.wait_ge(tabs_in, 64)
            for n in range(NT + 1):
                if n < NT:
                    zt, seq = z[:, n % 3, :], 0 if n < NTP else 1
                    dve.wait_ge(x_in[n % 2], 16 * (n // 2 + 1))
                    if n >= 3:
                        dve.wait_ge(y_out[n % 3], 16 * (n // 3))
                    link(dve.tensor_tensor(zt, sumf[:, n, :], g2[:, seq, :], ALU.mult))
                    dve.scalar_tensor_tensor(zt, xt[:, n % 2, :], ALPHA, zt, ALU.mult, ALU.add).then_inc(y_ready, 1)
                    dve.wait_ge(y_ready, n + 1)
                    for m in range(2):
                        link(dve.bn_stats(stats[:, n % 2, 6 * m:6 * m + 6], zt[:, m * 512:(m + 1) * 512]))
                    dve.bn_aggr(mv[:, n % 2, :], stats[:, n % 2, :]).then_inc(var_ready, 1)
                t = n - 1
                if t >= 0:
                    zt = z[:, t % 3, :]
                    dve.wait_ge(std_ready, t + 1)
                    dve.wait_ge(var_ready, t + 1)
                    link(dve.reciprocal(std[:, t % 2, :], std[:, t % 2, :]))
                    link(dve.tensor_scalar(zt, zt, mv[:, t % 2, 0:1], std[:, t % 2, :], ALU.subtract, ALU.mult))
                    dve.tensor_tensor(zt, zt, ln2[:, 0, :], ALU.mult).then_inc(gained, 1)


_INS = ["x_prompt", "x_sample", "c_prompt", "c_sample", "w_ada", "b_ada", "w_in", "gqa_q_norm", "gqa_k_norm",
        "mla_q_norm", "w_uq", "mla_kv_norm", "w_ukv", "grp_norm_a", "grp_norm_b", "w_out", "ln1_g", "ln1_b",
        "w_gate", "w_up", "w_down", "ln2_g", "ln2_b"]
_OUTS = [("y_prompt", (1, 256, 1024)), ("y_sample", (1, 1024, 1024))]


def _tables():
    import numpy as np

    row = np.repeat(np.arange(1024 // 64, dtype=np.float32), 64)
    col = np.tile(np.arange(64, dtype=np.float32), 1024 // 64)
    parts = []
    for dim in (64, 32):
        n = dim // 4
        freq = (1.0 / np.power(np.float32(10000.0), np.arange(n, dtype=np.float32) / np.float32(n))).astype(np.float32)
        ang = np.concatenate([row[:, None] * freq, col[:, None] * freq], axis=-1).astype(np.float32)
        parts += [np.cos(ang), np.sin(ang)]
    inv_n = np.array([1 / 64] * 10 + [1 / 256, 1 / 128], np.float32)
    return {"ident": np.eye(128, dtype=np.float32), "rope": np.concatenate(parts, 1).astype(np.float32), "inv_n": inv_n}


def kernel(**inputs):
    import numpy as _np
    import concourse.bacc as _bacc
    from concourse import mybir as _mybir
    from concourse.bass_utils import run_bass_kernel_spmd as _run

    nc = _bacc.Bacc("TRN2", target_bir_lowering=False, num_devices=1)
    arrays = {name: _np.ascontiguousarray(inputs[name]) for name in _INS}
    arrays.update(_tables())
    ins = {n: nc.dram_tensor(f"in_{n}", a.shape, _mybir.dt.from_np(a.dtype), kind="ExternalInput").ap() for n, a in arrays.items()}
    outs = {n: nc.dram_tensor(f"out_{n}", s, _mybir.dt.float32, kind="ExternalOutput").ap() for n, s in _OUTS}
    encoder_layer(nc, ins, outs)
    r = _run(nc, [{f"in_{n}": a for n, a in arrays.items()}], core_ids=[0])
    return tuple(r.results[0][f"out_{n}"] for n, _ in _OUTS)
```

```python
import concourse.bass as bass
from concourse import mybir
from contextlib import ExitStack

F32 = mybir.dt.float32
F32R = mybir.dt.float32r
ALU = mybir.AluOpType
ACT = mybir.ActivationFunctionType
AX = mybir.AxisListType

P = 128
D = 1024
KT = D // P
S_PROMPT, S_SAMPLE = 256, 1024
TOK = S_PROMPT + S_SAMPLE
NT = TOK // P
NTP = S_PROMPT // P
EPS = 1e-6
HA, KVA, DA = 8, 2, 64
HM, NOPE, ROPE, VD = 8, 64, 32, 64
DM = NOPE + ROPE
RQ, RKV = 256, 128
QK_A = (HA + KVA) * DA
C_VA = QK_A
C_QL = C_VA + KVA * DA
C_KVL = C_QL + RQ
C_KR = C_KVL + RKV
W_IN = C_KR + ROPE
BANKS_H = [(0, 384), (384, 768), (768, W_IN)]
FF = 2816
NF = FF // P
ALPHA = 2.0 ** 0.25
CHUNKS = [(0, 256), (256, 768), (768, 1280)]


def rows(ap, n=P):
    return ap.rearrange("(t p) m -> p t m", p=n)


class Link:

    def __init__(self, eng, sem, start=0):
        self.eng, self.sem, self.n = eng, sem, start

    def __call__(self, ins):
        self.n += 1
        ins.then_inc(self.sem, 1)
        self.eng.wait_ge(self.sem, self.n)


class Kernel:
    def __init__(self, nc, ctx, ins, outs):
        self.nc, self.ctx = nc, ctx
        self.i, self.o = ins, outs
        self.names = set()

    def sem(self, name):
        return self.ctx.enter_context(self.nc.semaphore(name))

    def sb(self, stage, name, shape, dt=F32, side=None):
        return stage.enter_context(self.nc.sbuf_tensor(name, shape, dt, side=side))

    def dram(self, name, shape):
        return self.nc.dram_tensor(name, shape, F32, kind="Internal").ap()


def encoder_layer(nc, ins, outs):
    ctx = ExitStack()
    with ctx:
        k = Kernel(nc, ctx, ins, outs)
        k.bank = [ctx.enter_context(nc.psum_tensor(f"pair{b}", [P, 2, 512], F32)) for b in range(4)]
        k.ident = k.sb(ctx, "ident", [P, P])
        k.eps = k.sb(ctx, "eps", [P, 1])
        k.mod = k.dram("mod_rows", [2, 6 * D])
        parts = lambda name, shape: [k.dram(f"{name}_{s}_rows", shape) for s in ("hi", "lo")]
        k.qa_t = parts("qa_t", [HA * DA, TOK])
        k.ka_t = parts("ka_t", [KVA * DA, TOK])
        k.va = parts("va", [TOK, KVA * DA])
        k.qm_t = parts("qm_t", [HM * DM, TOK])
        k.kn_t = parts("kn_t", [HM * NOPE, TOK])
        k.kr_t = parts("kr_t", [ROPE, TOK])
        k.vm = parts("vm", [TOK, HM * VD])
        k.o = k.dram("o", [TOK, D])
        k.x1 = k.dram("x1", [TOK, D])
        k.o_prompt = lambda t: outs["y_prompt"][0, t * P:(t + 1) * P, :]
        k.o_sample = lambda t: outs["y_sample"][0, t * P:(t + 1) * P, :]
        with ExitStack() as weights:
            k.win = [k.sb(weights, f"w_in_{s}", [P, KT, W_IN], F32R) for s in ("hi", "lo")]
            k.wuq = [k.sb(weights, f"w_uq_{s}", [P, RQ // P, HM * DM], F32R) for s in ("hi", "lo")]
            k.wukv = [k.sb(weights, f"w_ukv_{s}", [P, HM * (NOPE + VD)], F32R) for s in ("hi", "lo")]
            with nc.Block() as block, ExitStack() as early:
                k.early = early
                with ExitStack() as stage:
                    modulation(k, stage, block)
                with ExitStack() as stage:
                    projections(k, stage, block)
        k.u2_memory = ctx.enter_context(ExitStack())
        with ExitStack() as weights:
            w_out_lo_memory = weights.enter_context(ExitStack())
            k.wo = [k.sb(weights, "w_out_hi", [P, KT, D], F32R), k.sb(w_out_lo_memory, "w_out_lo", [P, KT, D], F32R)]
            with ExitStack() as stage:
                attention(k, stage)
            k.u2 = [k.sb(k.u2_memory, f"u2_{s}", [P, KT, TOK], F32R, side="right") for s in ("hi", "lo")]
            flat = k.wo[0][:, :, :].rearrange("p a b -> p (a b)")
            k.wgu = [flat[:, m * 4 * D:(m + 1) * 4 * D].rearrange("p (s m j c) -> p s m j c", s=2, m=2, c=P) for m in range(2)]
            w_out_lo_memory.close()
            k.raw_gu = k.sb(weights, "gate_up_raw", [P, 2, KT, P])
            k.raw_d = k.sb(weights, "down_raw", [P, D])
            k.wd = [k.sb(weights, f"down_{s}", [P, 2, D], F32R) for s in ("hi", "lo")]
            k.sg = k.sb(weights, "silu_gate", [P, 512])
            k.hf = k.sb(weights, "hidden_f32", [P, 512])
            k.gu_in, k.down_in, k.gu_hi, k.gu_lo = (k.sem(n) for n in ("gu_in", "down_in", "gu_hi", "gu_lo"))
            with nc.Block() as block:
                with ExitStack() as stage:
                    output(k, stage, block)
                with ExitStack() as stage:
                    channel(k, stage, block)


def bank(k, n):
    return k.bank[n // 2][:, n % 2, :]


def xrow(k, t):
    if t < NTP:
        return k.i["x_prompt"][0, t * P:(t + 1) * P, :]
    return k.i["x_sample"][0, (t - NTP) * P:(t - NTP + 1) * P, :]


def three(pe, out, a, b, start, stop):
    pe.matmul(out, a[0], b[0], start=start, stop=False)
    pe.matmul(out, a[0], b[1], start=False, stop=False)
    return pe.matmul(out, a[1], b[0], start=False, stop=stop)


def modulation(k, stage, block):
    nc = k.nc
    NC = 6 * D // 512
    RING = 3
    right = lambda name, shape: k.sb(stage, name, shape, side="right")
    c_t = right("c_t", [P, KT, 2])
    silu_c = right("silu_c", [P, KT, 2])
    wa = right("w_ada_ring", [P, RING, KT, 512])
    bias = right("b_ada_rows", [2, 6 * D])
    mrow = right("mod_chunk", [2, 2, 512])
    raw = right("w_raw", [P, 2, W_IN])
    c_in, ident_in = k.sem("c_in"), k.sem("ident_in")
    wa_in = [k.sem(f"wa_in{s}") for s in range(RING)]
    b_in = k.sem("b_ada_in")
    raw_in = [k.sem(f"raw_in{s}") for s in range(2)]
    c_ready, mod_done, mod_sum = k.sem("c_ready"), k.sem("mod_done"), k.sem("mod_sum")
    mod_out = [k.sem(f"mod_out{s}") for s in range(2)]
    hi_done, lo_done = k.sem("w_hi_done"), k.sem("w_lo_done")

    pieces = [(rows(k.i["w_in"][0])[:, j, :], k.win[0][:, j, :], k.win[1][:, j, :]) for j in range(KT)]
    pieces += [(rows(k.i["w_uq"][0])[:, j, :], k.wuq[0][:, j, :], k.wuq[1][:, j, :]) for j in range(RQ // P)]
    pieces += [(k.i["w_ukv"][0], k.wukv[0][:, :], k.wukv[1][:, :])]

    k.mod_out, k.lo_done, k.pieces = mod_out, lo_done, len(pieces)
    k.ident_in, k.eps_ready = ident_in, k.sem("eps_ready")

    @block.sync
    def _(sp):
        for s, c in enumerate(("c_prompt", "c_sample")):
            with nc.allow_non_contiguous_dma(reason="two short vectors"):
                sp.dma_start(c_t[:, :, s:s + 1], k.i[c][0:1, :].rearrange("a (p j) -> p j a", j=KT)).then_inc(c_in, 16)
        wsrc = k.i["w_ada"][0].rearrange("(p j) n -> p j n", j=KT)
        for n in range(NC):
            if n >= RING:
                sp.wait_ge(mod_done, n - RING + 1)
            sp.dma_start(wa[:, n % RING, :, :], wsrc[:, :, n * 512:(n + 1) * 512]).then_inc(wa_in[n % RING], 16)

    @block.gpsimd
    def _(pool):
        pool.memset(k.eps[:, :], EPS).then_inc(k.eps_ready, 1)
        pool.dma_start(k.ident[:, :], k.i["ident"]).then_inc(ident_in, 16)
        for m, (src, hi, lo) in enumerate(pieces):
            if m >= 2:
                pool.wait_ge(lo_done, m - 1)
            pool.dma_start(raw[:, m % 2, :hi.shape[-1]], src).then_inc(raw_in[m % 2], 16)
        pool.wait_ge(ident_in, 16)

    @block.tensor
    def _(pe):
        pe.wait_ge(c_ready, 1)
        for n in range(NC):
            pe.wait_ge(wa_in[n % RING], 16 * (n // RING + 1))
            if n >= 8:
                pe.wait_ge(mod_sum, n - 7)
            for j in range(KT):
                mm = pe.matmul(bank(k, n % 8)[0:2, :], silu_c[:, j, :], wa[:, n % RING, j, :],
                               start=j == 0, stop=j == KT - 1)
            mm.then_inc(mod_done, 1)

    @block.scalar
    def _(act):
        act.dma_start(bias[:, :], k.i["b_ada"][0, :].partition_broadcast(2)).then_inc(b_in, 16)
        act.wait_ge(c_in, 32)
        act.activation(silu_c[:, :, :], c_t[:, :, :], ACT.Silu).then_inc(c_ready, 1)
        assert len(pieces) <= NC
        for n in range(NC):
            if n < len(pieces):
                act.wait_ge(raw_in[n % 2], 16 * (n // 2 + 1))
                hi = pieces[n][1]
                act.activation(hi, raw[:, n % 2, :hi.shape[-1]], ACT.Copy).then_inc(hi_done, 1)
            if n >= 1:
                act.wait_ge(mod_sum, n)
                act.dma_start(k.mod[:, (n - 1) * 512:n * 512], mrow[:, (n - 1) % 2, :]).then_inc(mod_out[(n - 1) % 2], 16)
        act.wait_ge(mod_sum, NC)
        act.dma_start(k.mod[:, (NC - 1) * 512:], mrow[:, (NC - 1) % 2, :]).then_inc(mod_out[(NC - 1) % 2], 16)

    @block.vector
    def _(dve):
        def split(m):
            src, hi, lo = pieces[m]
            dve.wait_ge(hi_done, m + 1)
            dve.tensor_tensor(lo, raw[:, m % 2, :hi.shape[-1]], hi, ALU.subtract).then_inc(lo_done, 1)

        for n in range(NC):
            if n < len(pieces):
                split(n)
            dve.wait_ge(mod_done, n + 1)
            if n == 0:
                dve.wait_ge(b_in, 16)
            if n >= 2:
                dve.wait_ge(mod_out[n % 2], 16 * (n // 2))
            dve.tensor_tensor(mrow[:, n % 2, :], bank(k, n % 8)[0:2, :], bias[:, n * 512:(n + 1) * 512], ALU.add).then_inc(mod_sum, 1)
        for m in range(NC, len(pieces)):
            split(m)


def projections(k, stage, block):
    nc = k.nc
    early = lambda name, shape: k.sb(k.early, name, shape)
    xt = early("x_tile", [P, 2, D])
    stats = early("x_stats", [P, 2, 12])
    mv = early("x_mean_var", [P, 2, 2])
    std = early("x_std", [P, 2, 1])
    xh = early("x_hat", [P, 2, D])
    modt = early("mod_in_t", [P, 2, 2, KT])
    inv_n = early("inv_n", [P, 12])
    gain_qk = early("gain_qk", [P, 2, DA])
    gain_lat = early("gain_lat", [P, RQ + RKV])
    tab = early("rope_tables", [P, S_SAMPLE // P, 96])
    sb = lambda name, shape, dt=F32: k.sb(stage, name, shape, dt)
    uf = sb("u_t", [P, KT, P])
    u = [sb(f"u_{s}", [P, 2, KT, P], F32R) for s in ("hi", "lo")]
    hs = sb("h", [P, 2, W_IN])
    sq = sb("squares", [P, C_KR])
    ssq = sb("norm_sums", [P, 12])
    rn = sb("norm_factors", [P, 12])
    qk = sb("qk", [P, QK_A])
    rot = sb("qk_rotated", [P, QK_A])
    qkr = sb("qk_out", [P, 2, QK_A + ROPE])
    lat = sb("latents", [P, 2, RQ + RKV])
    latf = sb("latents_t", [P, 3, P])
    lath = [sb(f"latents_t_{s}", [P, 3, P], F32R) for s in ("hi", "lo")]
    qms = sb("q_mla", [P, 2, HM * DM])
    mrot = sb("q_mla_rotated", [P, HM, ROPE])
    kvs = sb("kv_mla", [P, 2, 2, HM * NOPE])
    q_tr, q_trh = sb("qa_tr", [P, 4, P]), sb("qa_tr_hi", [P, 4, P], F32R)
    k_tr, k_trh = sb("ka_tr", [P, 2, P]), sb("ka_tr_hi", [P, 2, P], F32R)
    qm_tr, qm_trh = sb("qm_tr", [DM, HM, P]), sb("qm_tr_hi", [DM, HM, P], F32R)
    kn_tr, kn_trh = sb("kn_tr", [P, 4, P]), sb("kn_tr_hi", [P, 4, P], F32R)
    va_s = [sb(f"va_{s}", [P, KVA * DA], F32R) for s in ("hi", "lo")]
    vm_s = [sb(f"vm_{s}", [P, HM * VD], F32R) for s in ("hi", "lo")]

    def mla_tr(t):
        if t < NT - 1:
            return qm_tr[:, :, :], qm_trh[:, :, :], kn_tr[:, :, :], kn_trh[:, :, :]
        return (xt[0:DM, 0, :].rearrange("p (h c) -> p h c", h=HM), xt[0:DM, 1, :].rearrange("p (h c) -> p h c", h=HM).bitcast(F32R),
                xh[:, 0, 0:512].rearrange("p (h c) -> p h c", h=4), xh[:, 0, 512:].rearrange("p (h c) -> p h c", h=4).bitcast(F32R))

    x_in = [k.sem(f"pj_x_in{s}") for s in range(2)]
    tabs_in, mod_in, modp = k.sem("tabs_in"), k.sem("mod_in"), k.sem("mod_plus_one")
    var_ready, std_ready, xhat_ready = k.sem("pj_var"), k.sem("pj_std"), k.sem("pj_xhat")
    t_ready, t_free = k.sem("pj_t_ready"), k.sem("pj_t_free")
    uf_ready, u_hi, u_ready = k.sem("uf_ready"), k.sem("pj_u_hi"), k.sem("pj_u_ready")
    h_ready, h_free = k.sem("h_ready"), k.sem("h_free")
    qm_ready, qm_free, kv_ready, kv_free = (k.sem(n) for n in ("qm_ready", "qm_free", "kv_ready", "kv_free"))
    sums_ready, root_ready = k.sem("sums_ready"), k.sem("root_ready")
    qk_ready, lat_ready, latf_ready, lath_ready = (k.sem(n) for n in ("qk_ready", "lat_ready", "latf_ready", "lath_ready"))
    qm_roped = k.sem("qm_roped")
    sq_done = k.sem("sq_done")
    out_v, out_q, out_k, out_qm, out_kn, out_vm = (k.sem(n) for n in ("out_va", "out_qa", "out_ka", "out_qm", "out_kn", "out_vm"))
    va_hi, q_hi, k_hi, qm_hi, kn_hi, vm_hi = (k.sem(n) for n in ("va_hi_done", "qa_hi_done", "ka_hi_done", "qm_hi_done", "kn_hi_done", "vm_hi_done"))
    va_lo, q_lo, k_lo, qm_lo, kn_lo, vm_lo = (k.sem(n) for n in ("va_lo_done", "qa_lo_done", "ka_lo_done", "qm_lo_done", "kn_lo_done", "vm_lo_done"))
    dv, pl = k.sem("pj_dve_link"), k.sem("pj_pool_link")

    def tcols(t):
        return slice(t * P, (t + 1) * P)

    def after_modulation(eng):
        eng.wait_ge(k.lo_done, k.pieces)
        for s in range(2):
            eng.wait_ge(k.mod_out[s], 16 * (6 * D // 512 // 2))

    def groups(n):
        return ([0, 1] if n < NT else []) + ([2, 3, 4] if 0 <= n - 3 < NT else []) + ([5, 6, 7] if 0 <= n - 4 < NT else [])

    TURNS = range(NT + 5)
    DVE_LOWS = 2
    order = [(n, g) for n in TURNS for g in groups(n)]
    number = {ng: m for m, ng in enumerate(order)}

    @block.sync
    def _(sp):
        for s in range(2):
            sp.wait_ge(k.mod_out[s], 32)
        with nc.allow_non_contiguous_dma(reason="modulation columns, once"):
            for s in range(2):
                for m, part in enumerate((1, 0)):
                    sp.dma_start(modt[:, s, m, :], k.mod[s, part * D:(part + 1) * D].rearrange("(j p) -> p j", p=P)).then_inc(mod_in, 16)
        for t in range(2):
            sp.dma_start(xt[:, t, :], xrow(k, t)).then_inc(x_in[t], 16)
        sp.dma_start(tab[:, :, :], rows(k.i["rope"])).then_inc(tabs_in, 16)
        sp.dma_start(inv_n[:, :], k.i["inv_n"].partition_broadcast(P)).then_inc(tabs_in, 16)
        for m, g in enumerate(("gqa_q_norm", "gqa_k_norm")):
            sp.dma_start(gain_qk[:, m, :], k.i[g][0, :].partition_broadcast(P)).then_inc(tabs_in, 16)
        sp.dma_start(gain_lat[:, 0:RQ], k.i["mla_q_norm"][0, :].partition_broadcast(P)).then_inc(tabs_in, 16)
        sp.dma_start(gain_lat[:, RQ:], k.i["mla_kv_norm"][0, :].partition_broadcast(P)).then_inc(tabs_in, 16)

        def load_x(t):
            sp.wait_ge(xhat_ready, t - 1)
            sp.dma_start(xt[:, t % 2, :], xrow(k, t)).then_inc(x_in[t % 2], 16)

        load_x(2)
        for n in TURNS:
            if n + 3 < NT:
                load_x(n + 3)
            def store(dst, src, done):
                for d, x in zip(dst, src):
                    sp.dma_start(d, x).then_inc(done, 16)

            t = n - 2
            if 0 <= t < NT:
                sp.wait_ge(va_lo, t + 1)
                store([d[tcols(t), :] for d in k.va], [x[:, :].bitcast(F32) for x in va_s], out_v)
            t = n - 4
            if 0 <= t < NT:
                sp.wait_ge(q_lo, t + 1)
                store([rows(d)[:, :, tcols(t)] for d in k.qa_t], [q_trh[:, :, :].bitcast(F32), q_tr[:, :, :]], out_q)
                sp.wait_ge(k_lo, t + 1)
                store([d[:, tcols(t)] for d in k.ka_t], [k_trh[:, 0, :].bitcast(F32), k_tr[:, 0, :]], out_k)
                store([d[:, tcols(t)] for d in k.kr_t], [k_trh[0:ROPE, 1, :].bitcast(F32), k_tr[0:ROPE, 1, :]], out_k)
            t = n - 5
            if 0 <= t < NT:
                sp.wait_ge(qm_lo, t + 1)
                q, qh, kn, knh = mla_tr(t)
                store([rows(d, DM)[:, :, tcols(t)] for d in k.qm_t], [qh.bitcast(F32), q], out_qm)
                sp.wait_ge(kn_lo, t + 1)
                store([rows(d)[:, :, tcols(t)] for d in k.kn_t], [knh.bitcast(F32), kn], out_kn)
            t = n - 4
            if 0 <= t < NT:
                sp.wait_ge(vm_lo, t + 1)
                store([d[tcols(t), :] for d in k.vm], [x[:, :].bitcast(F32) for x in vm_s], out_vm)
        for done in (out_v, out_q, out_qm, out_kn, out_vm):
            sp.wait_ge(done, 32 * NT)
        sp.wait_ge(out_k, 64 * NT)

    @block.tensor
    def _(pe):
        def transposes(n, g, blocks):
            m = number[n, g]
            if m >= 2:
                pe.wait_ge(t_free, m - 1)
            for q, src in enumerate(blocks):
                mm = pe.transpose(bank(k, m % 2)[0:cols_of(src), q * P:(q + 1) * P], src, k.ident[:, :])
            mm.then_inc(t_ready, 1)

        def h_bank(t, b):
            lo, hi = BANKS_H[b]
            if t >= 1:
                pe.wait_ge(h_free, 3 * (t - 1) + b + 1)
            out = bank(k, 2 + b)[:, 0:hi - lo]
            if t == 0:
                pe.wait_ge(k.lo_done, k.pieces)
            for j in range(KT):
                mm = three(pe, out, [u[0][:, t % 2, j, :], u[1][:, t % 2, j, :]],
                           [w[:, j, lo:hi] for w in k.win], j == 0, j == KT - 1)
            mm.then_inc(h_ready, 1)

        pe.wait_ge(k.ident_in, 16)
        for n in TURNS:
            a, b, c = n - 1, n - 3, n - 4
            if n < NT:
                pe.wait_ge(xhat_ready, n + 1)
                for g in range(2):
                    transposes(n, g, [xh[:, n % 2, (4 * g + q) * P:(4 * g + q + 1) * P] for q in range(4)])
            if 0 <= a < NT:
                pe.wait_ge(u_ready, a + 1)
                h_bank(a, 0)
            if 0 <= b < NT:
                pe.wait_ge(lat_ready, b + 1)
                transposes(n, 2, [lat[:, b % 2, q * P:(q + 1) * P] for q in range(3)])
            if 0 <= a < NT:
                h_bank(a, 1)
            if 0 <= b < NT:
                pe.wait_ge(qk_ready, b + 1)
                transposes(n, 3, [qkr[:, b % 2, q * P:(q + 1) * P] for q in range(4)])
                transposes(n, 4, [qkr[:, b % 2, 4 * P:5 * P], qkr[:, b % 2, QK_A:QK_A + ROPE]])
            if 0 <= a < NT:
                h_bank(a, 2)
            if 0 <= b < NT:
                pe.wait_ge(lath_ready, b + 1)
                for half in range(2):
                    if b >= 1:
                        pe.wait_ge(kv_free, 2 * (b - 1) + half + 1)
                    out = bank(k, 6 + half)[:, 0:4 * DM]
                    for j in range(RQ // P):
                        mm = three(pe, out, [w[:, j, :] for w in lath],
                                   [w[:, j, half * 4 * DM:(half + 1) * 4 * DM] for w in k.wuq], j == 0, j == RQ // P - 1)
                    mm.then_inc(qm_ready, 1)
            if 0 <= c < NT:
                pe.wait_ge(qm_roped, c + 1)
                for g in range(2):
                    transposes(n, 5 + g, [qms[:, c % 2, (4 * g + q) * DM:(4 * g + q + 1) * DM] for q in range(4)])
                transposes(n, 7, [kvs[:, c % 2, 0, q * P:(q + 1) * P] for q in range(4)])
            if 0 <= b < NT:
                for half in range(2):
                    pe.wait_ge(qm_free, 2 * b + half + 1)
                    mm = three(pe, bank(k, 6 + half), [w[:, 2, :] for w in lath],
                               [w[:, :].rearrange("p (h c) -> p h c", h=HM)[:, :, half * NOPE:(half + 1) * NOPE] for w in k.wukv],
                               True, True)
                    mm.then_inc(kv_ready, 1)

    @block.scalar
    def _(act):
        def take(n, g):
            act.wait_ge(t_ready, number[n, g] + 1)
            return bank(k, number[n, g] % 2)

        def root_x(t):
            act.wait_ge(var_ready, t + 1)
            act.activation(std[:, t % 2, :], mv[:, t % 2, 1:2], ACT.Sqrt, bias=k.eps[:, 0:1]).then_inc(std_ready, 1)

        def h_copy(t, m):
            lo, hi = BANKS_H[m]
            act.wait_ge(h_ready, 3 * t + m + 1)
            if m == 0 and t >= 2:
                act.wait_ge(va_lo, t - 1)
                act.wait_ge(qk_ready, t - 1)
                act.wait_ge(lat_ready, t - 1)
            act.activation(hs[:, t % 2, lo:hi], bank(k, 2 + m)[:, 0:hi - lo], ACT.Copy).then_inc(h_free, 1)

        act.wait_ge(k.eps_ready, 1)
        root_x(0)
        root_x(1)
        after_modulation(act)
        for n in TURNS:
            a, b, c = n - 1, n - 3, n - 4
            if n < NT:
                if n == 0:
                    act.wait_ge(modp, 1)
                if n >= 1:
                    act.wait_ge(u_ready, n)
                seq = 0 if n < NTP else 1
                for g in range(2):
                    src = take(n, g)
                    for q in range(4):
                        j = 4 * g + q
                        mm = act.activation(uf[:, j, :], src[:, q * P:(q + 1) * P], ACT.Identity,
                                            bias=modt[:, seq, 1, j:j + 1], scale=modt[:, seq, 0, j:j + 1])
                        if q < 3:
                            mm.then_inc(uf_ready, 1)
                    mm.then_inc(t_free, 1)
            if 0 <= n - 2 < NT:
                act.wait_ge(sums_ready, n - 1)
                act.activation(rn[:, :], ssq[:, :], ACT.Sqrt, bias=k.eps[:, 0:1]).then_inc(root_ready, 1)
            if n < NT:
                act.wait_ge(t_free, number[n, 1] + 1)
                if n >= 2:
                    act.wait_ge(h_ready, 3 * (n - 1))
                act.activation(u[0][:, n % 2, :, :], uf[:, :, :], ACT.Copy).then_inc(u_hi, 1)
            if 0 <= n - 5 < NT:
                act.wait_ge(t_free, number[n - 1, 7] + 1)
                q, qh, kn, knh = mla_tr(n - 5)
                act.activation(qh, q, ACT.Copy).then_inc(qm_hi, 1)
                act.activation(knh, kn, ACT.Copy).then_inc(kn_hi, 1)
            if 0 <= n - 4 < NT:
                act.wait_ge(kv_free, 2 * (n - 3))
                if n >= 5:
                    act.wait_ge(out_vm, 32 * (n - 4))
                act.activation(vm_s[0][:, :], kvs[:, n % 2, 1, :], ACT.Copy).then_inc(vm_hi, 1)
            if 0 <= n - 2 < NT:
                act.wait_ge(h_free, 3 * (n - 1))
                if n >= 3:
                    act.wait_ge(out_v, 32 * (n - 2))
                act.activation(va_s[0][:, :], hs[:, n % 2, C_VA:C_QL], ACT.Copy).then_inc(va_hi, 1)
            if 0 <= a < NT:
                h_copy(a, 0)
            if n + 2 < NT:
                root_x(n + 2)
            if 0 <= b < NT:
                src = take(n, 2)
                if b >= 1:
                    act.wait_ge(lath_ready, b)
                act.activation(latf[:, :, :], src[:, 0:3 * P].rearrange("p (q c) -> p q c", c=P), ACT.Copy).then_inc(t_free, 1)
            if 0 <= a < NT:
                h_copy(a, 1)
            if 0 <= b < NT:
                src = take(n, 3)
                if b >= 1:
                    act.wait_ge(out_q, 32 * b)
                act.activation(q_tr[:, :, :], src.rearrange("p (q c) -> p q c", c=P), ACT.Copy).then_inc(t_free, 1)
                src = take(n, 4)
                if b >= 1:
                    act.wait_ge(out_k, 64 * b)
                act.activation(k_tr[:, 0, :], src[:, 0:P], ACT.Copy).then_inc(uf_ready, 1)
                act.activation(k_tr[0:ROPE, 1, :], src[0:ROPE, P:2 * P], ACT.Copy).then_inc(t_free, 1)
                act.wait_ge(t_free, number[n, 4] + 1)
                act.activation(q_trh[:, :, :], q_tr[:, :, :], ACT.Copy).then_inc(q_hi, 1)
                act.activation(k_trh[:, 0, :], k_tr[:, 0, :], ACT.Copy).then_inc(uf_ready, 1)
                act.activation(k_trh[0:ROPE, 1, :], k_tr[0:ROPE, 1, :], ACT.Copy).then_inc(k_hi, 1)
            if 0 <= a < NT:
                h_copy(a, 2)
            if 0 <= b < NT:
                for half in range(2):
                    act.wait_ge(qm_ready, 2 * b + half + 1)
                    if half == 0 and b >= 2:
                        act.wait_ge(t_ready, number[b - 2 + 4, 6] + 1)
                    act.activation(qms[:, b % 2, half * 4 * DM:(half + 1) * 4 * DM], bank(k, 6 + half)[:, 0:4 * DM], ACT.Copy).then_inc(qm_free, 1)
            if 0 <= c < NT:
                q_out, _, k_out, _ = mla_tr(c)
                if 1 <= c < NT - 1:
                    act.wait_ge(out_qm, 32 * c)
                for g in range(2):
                    src = take(n, 5 + g)
                    act.activation(q_out[:, 4 * g:4 * g + 4, :], src[0:DM, :].rearrange("p (q c) -> p q c", c=P), ACT.Copy).then_inc(t_free, 1)
                src = take(n, 7)
                if 1 <= c < NT - 1:
                    act.wait_ge(out_kn, 32 * c)
                act.activation(k_out, src.rearrange("p (q c) -> p q c", c=P), ACT.Copy).then_inc(t_free, 1)
            if 0 <= b < NT:
                for half in range(2):
                    act.wait_ge(kv_ready, 2 * b + half + 1)
                    if half == 1 and b >= 2:
                        act.wait_ge(vm_lo, b - 1)
                    act.activation(kvs[:, b % 2, half, :], bank(k, 6 + half)[:, :], ACT.Copy).then_inc(kv_free, 1)

    @block.gpsimd
    def _(pool):
        for n in TURNS:
            t = n - 2
            if 0 <= t < NT:
                pool.wait_ge(h_free, 3 * (t + 1))
                if t >= 1:
                    pool.wait_ge(sums_ready, t)
                pool.tensor_tensor(sq[:, 0:QK_A], hs[:, t % 2, 0:QK_A], hs[:, t % 2, 0:QK_A], ALU.mult).then_inc(pl, 1)
                pool.tensor_tensor(sq[:, C_QL:C_KR], hs[:, t % 2, C_QL:C_KR], hs[:, t % 2, C_QL:C_KR], ALU.mult).then_inc(sq_done, 1)
                pool.wait_ge(va_hi, t + 1)
                if t >= 1:
                    pool.wait_ge(out_v, 32 * t)
                pool.tensor_tensor(va_s[1][:, :], hs[:, t % 2, C_VA:C_QL], va_s[0][:, :], ALU.subtract).then_inc(va_lo, 1)
            t = n - 4
            if 0 <= t < NT:
                pool.wait_ge(vm_hi, t + 1)
                if t >= 1:
                    pool.wait_ge(out_vm, 32 * t)
                pool.tensor_tensor(vm_s[1][:, :], kvs[:, t % 2, 1, :], vm_s[0][:, :], ALU.subtract).then_inc(vm_lo, 1)
            t = n - 5
            if 0 <= t < NT - DVE_LOWS:
                q, qh, kn, knh = mla_tr(t)
                pool.wait_ge(qm_hi, t + 1)
                pool.tensor_tensor(q.bitcast(F32R), q, qh, ALU.subtract).then_inc(qm_lo, 1)
                pool.wait_ge(kn_hi, t + 1)
                pool.tensor_tensor(kn.bitcast(F32R), kn, knh, ALU.subtract).then_inc(kn_lo, 1)

    @block.vector
    def _(dve):
        link = Link(dve, dv)

        def rope(out, x, cos, sin, heads, w, tmp):
            c2 = cos[:, None, None, :].to_broadcast([P, heads, 2, w])
            s1 = sin[:, None, :].to_broadcast([P, heads, w])
            link(dve.tensor_tensor(tmp[:, :, 0:w], x[:, :, w:2 * w], s1, ALU.mult))
            link(dve.tensor_tensor(tmp[:, :, w:2 * w], x[:, :, 0:w], s1, ALU.mult))
            link(dve.tensor_tensor(x.rearrange("p h (a c) -> p h a c", a=2), x.rearrange("p h (a c) -> p h a c", a=2), c2, ALU.mult))
            link(dve.tensor_tensor(out[:, :, 0:w], x[:, :, 0:w], tmp[:, :, 0:w], ALU.subtract))
            return dve.tensor_tensor(out[:, :, w:2 * w], x[:, :, w:2 * w], tmp[:, :, w:2 * w], ALU.add)

        def moments(t):
            dve.wait_ge(x_in[t % 2], 16 * (t // 2 + 1))
            for q in range(2):
                link(dve.bn_stats(stats[:, t % 2, 6 * q:6 * q + 6], xt[:, t % 2, q * 512:(q + 1) * 512]))
            dve.bn_aggr(mv[:, t % 2, :], stats[:, t % 2, :]).then_inc(var_ready, 1)

        moments(0)
        moments(1)
        dve.wait_ge(mod_in, 64)
        for s in range(2):
            m = dve.tensor_scalar(modt[:, s, 0, :], modt[:, s, 0, :], 1.0, None, ALU.add)
            if s == 0:
                link(m)
        m.then_inc(modp, 1)

        def x_hat(t):
            dve.wait_ge(std_ready, t + 1)
            dve.wait_ge(var_ready, t + 1)
            link(dve.reciprocal(std[:, t % 2, :], std[:, t % 2, :]))
            if t >= 2:
                dve.wait_ge(t_ready, number[t - 2, 1] + 1)
            dve.tensor_scalar(xh[:, t % 2, :], xt[:, t % 2, :], mv[:, t % 2, 0:1], std[:, t % 2, :], ALU.subtract, ALU.mult).then_inc(xhat_ready, 1)

        def mla_rope(t):
            pos = t if t < NTP else t - NTP
            dve.wait_ge(qm_free, 2 * (t + 1))
            dve.wait_ge(qk_ready, min(t + 2, NT))
            x = qms[:, t % 2, :].rearrange("p (h c) -> p h c", c=DM)[:, :, NOPE:]
            rope(x, x, tab[:, pos, 64:80], tab[:, pos, 80:96], HM, ROPE // 2, mrot[:, :, :]).then_inc(qm_roped, 1)

        def sums(t):
            dve.wait_ge(sq_done, t + 1)
            dve.wait_ge(pl, t + 1)
            if t >= 1:
                dve.wait_ge(root_ready, t)
            link(dve.reduce_sum(ssq[:, 0:heads], sq[:, 0:QK_A].rearrange("p (h c) -> p h c", c=DA), AX.X))
            link(dve.reduce_sum(ssq[:, heads:heads + 1], sq[:, C_QL:C_KVL], AX.X))
            link(dve.reduce_sum(ssq[:, heads + 1:heads + 2], sq[:, C_KVL:C_KR], AX.X))
            dve.tensor_tensor(ssq[:, :], ssq[:, :], inv_n[:, :], ALU.mult).then_inc(sums_ready, 1)

        def split_latents(t):
            dve.wait_ge(t_free, number[t + 3, 2] + 1)
            if t >= 1:
                dve.wait_ge(kv_ready, 2 * t)
            link(dve.tensor_copy(lath[0][:, :, :], latf[:, :, :]))
            dve.tensor_tensor(lath[1][:, :, :], latf[:, :, :], lath[0][:, :, :], ALU.subtract).then_inc(lath_ready, 1)

        def norms(t):
            h = hs[:, t % 2, :]
            pos = t if t < NTP else t - NTP
            dve.wait_ge(root_ready, t + 1)
            link(dve.reciprocal(rn[:, :], rn[:, :]))
            if t >= 2:
                dve.wait_ge(t_ready, number[t - 2 + 3, 2] + 1)
            link(dve.scalar_tensor_tensor(lat[:, t % 2, 0:RQ], h[:, C_QL:C_KVL], rn[:, heads:heads + 1], gain_lat[:, 0:RQ], ALU.mult, ALU.mult))
            dve.scalar_tensor_tensor(lat[:, t % 2, RQ:], h[:, C_KVL:C_KR], rn[:, heads + 1:heads + 2], gain_lat[:, RQ:], ALU.mult, ALU.mult).then_inc(lat_ready, 1)
            qk3 = qk[:, :].rearrange("p (h c) -> p h c", c=DA)
            link(dve.tensor_tensor(qk3, h[:, 0:QK_A].rearrange("p (h c) -> p h c", c=DA), rn[:, 0:heads, None].to_broadcast([P, heads, DA]), ALU.mult))
            link(dve.tensor_tensor(qk3[:, 0:HA, :], qk3[:, 0:HA, :], gain_qk[:, 0:1, :].to_broadcast([P, HA, DA]), ALU.mult))
            link(dve.tensor_tensor(qk3[:, HA:, :], qk3[:, HA:, :], gain_qk[:, 1:2, :].to_broadcast([P, KVA, DA]), ALU.mult))
            if t >= 2:
                dve.wait_ge(t_ready, number[t - 2 + 3, 4] + 1)
            link(rope(qkr[:, t % 2, 0:QK_A].rearrange("p (h c) -> p h c", c=DA), qk3, tab[:, pos, 0:32], tab[:, pos, 32:64],
                      heads, DA // 2, rot[:, :].rearrange("p (h c) -> p h c", c=DA)))
            if t >= 2:
                dve.wait_ge(qm_roped, t - 1)
            rope(qkr[:, t % 2, QK_A:].rearrange("p (h c) -> p h c", h=1), h[:, C_KR:].rearrange("p (h c) -> p h c", h=1),
                 tab[:, pos, 64:80], tab[:, pos, 80:96], 1, ROPE // 2, mrot[:, 0:1, :]).then_inc(qk_ready, 1)

        def low(x, hi):
            return dve.tensor_tensor(x.bitcast(F32R), x, hi, ALU.subtract)

        def gqa_low(t):
            dve.wait_ge(q_hi, t + 1)
            low(q_tr[:, :, :], q_trh[:, :, :]).then_inc(q_lo, 1)
            dve.wait_ge(k_hi, t + 1)
            link(low(k_tr[:, 0, :], k_trh[:, 0, :]))
            low(k_tr[0:ROPE, 1, :], k_trh[0:ROPE, 1, :]).then_inc(k_lo, 1)

        def mla_low(t):
            q, qh, kn, knh = mla_tr(t)
            if t == NT - DVE_LOWS:
                dve.wait_ge(qm_lo, t)
                dve.wait_ge(kn_lo, t)
            dve.wait_ge(qm_hi, t + 1)
            low(q, qh).then_inc(qm_lo, 1)
            dve.wait_ge(kn_hi, t + 1)
            low(kn, knh).then_inc(kn_lo, 1)

        heads = HA + KVA
        x_hat(0)
        after_modulation(dve)
        for n in TURNS:
            if 0 <= n - 4 < NT:
                mla_rope(n - 4)
            if n + 1 < NT:
                x_hat(n + 1)
            if 0 <= n - 4 < NT:
                gqa_low(n - 4)
            if n == 2:
                dve.wait_ge(tabs_in, 96)
            if 0 <= n - 2 < NT:
                sums(n - 2)
            if n < NT:
                dve.wait_ge(u_hi, n + 1)
                dve.tensor_tensor(u[1][:, n % 2, :, :], uf[:, :, :], u[0][:, n % 2, :, :], ALU.subtract).then_inc(u_ready, 1)
            if n + 2 < NT:
                moments(n + 2)
            if 0 <= n - 3 < NT:
                split_latents(n - 3)
            if 0 <= n - 2 < NT:
                norms(n - 2)
            if NT - DVE_LOWS <= n - 5 < NT:
                mla_low(n - 5)


def cols_of(src):
    n = 1
    for s in src.shape[1:]:
        n *= s
    return n


def attention(k, stage):
    nc = k.nc
    sb = lambda name, shape, dt=F32: k.sb(stage, name, shape, dt)
    H = HA + HM
    RING = 3
    UNITS = 1 + S_SAMPLE // P
    PS = 3
    LAG = 2
    qs = [sb(f"q_{s}", [P, RING, TOK], F32R) for s in ("a", "b")]
    ks = [sb(f"k_{s}", [P, RING, TOK], F32R) for s in ("a", "b")]
    VC = VD + 2
    vs = [sb(f"v_{s}", [P, RING, NT, VC], F32R) for s in ("hi", "lo")]
    pf = sb("p_f32", [P, PS, 1024])
    ph = [sb(f"p_{s}", [P, PS, 1024], F32R) for s in ("hi", "lo")]
    mcol = sb("max_col", [P, NT])
    mrow = sb("neg_max_row", [NT, P], F32R)
    oc = sb("o_t", [VD + 1, 2, TOK])
    rec = sb("recip_sum", [P, NT])
    on = sb("o_head", [P, 2, NT, VD])
    wo_raw = sb("w_out_raw", [P, D])
    gain = sb("grp_gain", [P, KT])

    q_in, k_in, v_in = ([k.sem(f"{n}{s}") for s in range(RING)] for n in ("q_in", "k_in", "v_in"))
    first_in = [k.sem(f"first_{n}_in") for n in ("approx", "exact", "values")]
    ones, pool_link = k.sem("ones_rows"), k.sem("at_pool_link")
    s_ready, e_done, p_hi, p_lo, pv_done = (k.sem(n) for n in ("s_ready", "exp_done", "p_hi_ready", "p_lo_ready", "pv_done"))
    a_ready, a_free = k.sem("approx_ready"), k.sem("approx_free")
    m_tr, m_row, m_in = k.sem("max_tr"), k.sem("max_row"), k.sem("max_in")
    o_free, ot_ready, ot_free = k.sem("o_free"), k.sem("ot_ready"), k.sem("ot_free")
    rec_done = k.sem("rec_done")
    gain_in, wo_in, wo_hi, wo_lo = (k.sem(n) for n in ("gain_in", "wo_in", "wo_hi_ready", "wo_lo_ready"))
    o_out = [k.sem(f"o_out{s}") for s in range(2)]

    gqa = lambda g: g < HA
    GROUP = HA // KVA

    def kv(g):
        return g // GROUP if gqa(g) else KVA + g - HA

    def first_head(n):
        return n * GROUP if n < KVA else HA + n - KVA

    def last_head(n):
        return first_head(n) + (GROUP - 1 if n < KVA else 0)

    def arrived(n, loads):
        return 16 * sum(loads(i) for i in range(n % RING, n + 1, RING) if i > 0)

    S_BANKS = [k.bank[0], k.bank[1]]
    A_PAIR, O_PAIR = k.bank[2], k.bank[3]
    ITEMS, EARLY = UNITS, 3
    ROWS_AT = UNITS - EARLY
    OUT_AT = 5

    def beside(g, u):
        h, i = (g + 1, EARLY + u) if u < ROWS_AT else (g + 2, u - ROWS_AT)
        return (h, i) if h < H else None

    uses = [("item", 0, i) for i in range(ITEMS)] + [("rows", 0)] + [("item", 1, i) for i in range(EARLY)]
    for g in range(H):
        for u in range(UNITS):
            if u == ROWS_AT and g + 1 < H:
                uses.append(("rows", g + 1))
            if u == OUT_AT and g >= 1:
                uses.append(("outputs", g - 1))
            if beside(g, u):
                uses.append(("item", *beside(g, u)))
    uses.append(("outputs", H - 1))
    number = {use: m for m, use in enumerate(uses)}

    def item_use(g, i):
        return number["item", g, i]

    def rows_use(g):
        return number["rows", g]

    def out_use(g):
        return number["outputs", g]

    def a_pair(m):
        return [k.bank[2], k.bank[0], k.bank[1]][m % 3] if m < ITEMS else k.bank[2]

    def use_before(eng, m):
        before = m - 3 if m < ITEMS else m - 1
        if before >= 0:
            eng.wait_ge(a_free, before + 1)

    def load(eng, g):
        s = g % RING
        if g >= RING:
            eng.wait_ge(s_ready, UNITS * (g - RING + 1))
        if gqa(g):
            hi, lo = (x[g * DA:(g + 1) * DA, :] for x in k.qa_t)
            jobs = [(qs[0][0:DA], hi), (qs[0][DA:P], lo), (qs[1][0:DA], hi)]
        else:
            h = g - HA
            jobs = [(q[0:DM], x[h * DM:(h + 1) * DM, :]) for q, x in zip(qs, k.qm_t)]
        for dst, src in jobs:
            eng.dma_start(dst[:, s, :].bitcast(F32), src).then_inc(q_in[s], 16)
        n = kv(g)
        if g != first_head(n):
            return
        s = n % RING
        if n >= RING:
            eng.wait_ge(s_ready, UNITS * (last_head(n - RING) + 1))
        if gqa(g):
            hi, lo = (x[n * DA:(n + 1) * DA, :] for x in k.ka_t)
            jobs = [(ks[0][0:DA], hi), (ks[0][DA:P], hi), (ks[1][0:DA], lo)]
            values = [x[:, n * VD:(n + 1) * VD] for x in k.va]
        else:
            if g < HA + RING:
                eng.memset(ks[0][DM:DM + 1, s, :].bitcast(F32), 1.0).then_inc(ones, 1)
            jobs = [(x[0:NOPE], n_t[h * NOPE:(h + 1) * NOPE, :]) for x, n_t in zip(ks, k.kn_t)]
            jobs += [(x[NOPE:DM], r_t) for x, r_t in zip(ks, k.kr_t)]
            values = [x[:, h * VD:(h + 1) * VD] for x in k.vm]
        for dst, src in jobs:
            eng.dma_start(dst[:, s, :].bitcast(F32), src).then_inc(k_in[s], 16)
        if n >= RING:
            eng.wait_ge(pv_done, UNITS * (last_head(n - RING) + 1))
        for dst, src in zip(vs, values):
            eng.dma_start(dst[:, s, :, 0:VD].bitcast(F32), rows(src)).then_inc(v_in[s], 16)

    def load_first(eng):
        (q_hi, q_lo), (k_hi, k_lo) = ((x[0:DA, :] for x in parts) for parts in (k.qa_t, k.ka_t))
        first = [(qs[0][0:DA], q_hi), (qs[0][DA:P], q_lo), (ks[0][0:DA], k_hi), (ks[0][DA:P], k_hi)]
        for jobs, done in ((first, first_in[0]), ([(qs[1][0:DA], q_hi), (ks[1][0:DA], k_lo)], first_in[1])):
            for dst, src in jobs:
                eng.dma_start(dst[:, 0, :].bitcast(F32), src).then_inc(done, 16)
        for dst, src in zip(vs, k.va):
            eng.dma_start(dst[:, 0, :, 0:VD].bitcast(F32), rows(src[:, 0:VD])).then_inc(first_in[2], 16)

    with nc.Block() as block:
        @block.sync
        def _(sp):
            load_first(sp)
            for g in range(H):
                sp.wait_ge(m_row, g + 1)
                row = qs[1][DA:DA + 1, g % RING, :] if gqa(g) else qs[0][DM:DM + 1, g % RING, :]
                sp.dma_start(row.bitcast(F32), mrow[:, :].bitcast(F32)).then_inc(m_in, 16)

        @block.gpsimd
        def _(pool):
            def store(g):
                pool.wait_ge(a_free, out_use(g) + 1)
                pool.dma_start(rows(k.o)[:, :, g * VD:(g + 1) * VD], on[:, g % 2, :, :]).then_inc(o_out[g % 2], 16)

            def load_w_out(j):
                if j >= 1:
                    pool.wait_ge(wo_lo, j)
                pool.dma_start(wo_raw[:, :], rows(k.i["w_out"][0])[:, j, :]).then_inc(wo_in, 16)

            link = Link(pool, pool_link)
            for s in range(KVA):
                link(pool.memset(ks[1][DA:DA + 1, s, :].bitcast(F32), 1.0))
            for s in range(RING):
                link(pool.memset(vs[0][:, s, :, VD:VC].bitcast(F32), 1.0))
                ins = pool.memset(vs[1][:, s, :, VD:VC].bitcast(F32), 0.0)
                if s < RING - 1:
                    link(ins)
            ins.then_inc(ones, 1)
            load(pool, 1)
            load(pool, 2)
            with nc.allow_non_contiguous_dma(reason="columns of gains, once"):
                for m, name in enumerate(("grp_norm_a", "grp_norm_b")):
                    pool.dma_start(gain[:, 4 * m:4 * m + 4], k.i[name][0, :].rearrange("(j p) -> p j", p=P)).then_inc(gain_in, 16)
            for g in range(H):
                if g + 3 < H:
                    load(pool, g + 3)
                if HA - 1 <= g < H - 1:
                    load_w_out(g - HA + 1)
                store(g)
            for s in range(2):
                pool.wait_ge(o_out[s], 16 * (H // 2))

        @block.tensor
        def _(pe):
            def scores(g, u):
                c = g * UNITS + u
                if u == 0:
                    if g == 0:
                        pe.wait_ge(first_in[1], 32)
                    pe.wait_ge(m_in, 16 * (g + 1))
                    pe.wait_ge(ones, 1 + min(max(g - HA + 1, 0), RING))
                if c >= 2:
                    pe.wait_ge(e_done, c - 1)
                out = S_BANKS[c % 2]
                s, n = g % RING, kv(g) % RING
                if u == 0:
                    jobs = [(out[:, 0, m * 256:(m + 1) * 256], m * P, slice(0, S_PROMPT)) for m in range(NTP)]
                else:
                    key = S_PROMPT + (u - 1) * P
                    jobs = [(out[:, m, :], key, slice(S_PROMPT + m * 512, S_PROMPT + (m + 1) * 512)) for m in range(2)]
                for dst, key, q in jobs:
                    kk = slice(key, key + P)
                    if gqa(g):
                        pe.matmul(dst, ks[0][:, n, kk], qs[0][:, s, q], start=True, stop=False)
                        mm = pe.matmul(dst, ks[1][0:DA + 1, n, kk], qs[1][0:DA + 1, s, q], start=False, stop=True)
                    else:
                        pe.matmul(dst, ks[0][0:DM + 1, n, kk], qs[0][0:DM + 1, s, q], start=True, stop=False)
                        pe.matmul(dst, ks[1][0:DM, n, kk], qs[0][0:DM, s, q], start=False, stop=False)
                        mm = pe.matmul(dst, ks[0][0:DM, n, kk], qs[1][0:DM, s, q], start=False, stop=True)
                mm.then_inc(s_ready, 1)

            def values(g, u):
                c = g * UNITS + u
                pe.wait_ge(p_lo, c + 1)
                if u == 0:
                    if kv(g) == 0:
                        pe.wait_ge(first_in[2], 32)
                    else:
                        pe.wait_ge(v_in[kv(g) % RING], arrived(kv(g), lambda n: 2))
                    if g >= 1:
                        pe.wait_ge(o_free, 3 * g - 1)
                if u == 1:
                    pe.wait_ge(o_free, 3 * g + 1)
                s = kv(g) % RING
                if u == 0:
                    jobs = [(O_PAIR[0:VD + 1, 0, 0:256], m, slice(m * 256, (m + 1) * 256), m == 0, m == NTP - 1) for m in range(NTP)]
                else:
                    jobs = [(O_PAIR[0:VD + 1, m, :], NTP + u - 1, slice(m * 512, (m + 1) * 512), u == 1, u == UNITS - 1) for m in range(2)]
                for dst, t, q, first, last in jobs:
                    v = [x[:, s, t, 0:VD + 1] for x in vs]
                    mm = three(pe, dst, v, [x[:, c % PS, q] for x in ph], first, last)
                mm.then_inc(pv_done, 1)

            def maxima(g, i):
                m = item_use(g, i)
                use_before(pe, m)
                if i == 0:
                    if g == 0:
                        pe.wait_ge(first_in[0], 64)
                    else:
                        pe.wait_ge(q_in[g % RING], arrived(g, lambda h: 3 if gqa(h) else 2))
                    if kv(g) > 0:
                        pe.wait_ge(k_in[kv(g) % RING], arrived(kv(g), lambda n: 3 if n < KVA else 4))
                s, n = g % RING, kv(g) % RING
                w = P if gqa(g) else DM
                if i < ITEMS - 1:
                    q = slice(S_PROMPT + i * P, S_PROMPT + (i + 1) * P)
                    jobs = [(a_pair(m)[:, c, :], q, slice(S_PROMPT + c * 512, S_PROMPT + (c + 1) * 512)) for c in range(2)]
                else:
                    jobs = [(a_pair(m)[:, 0, c * 256:(c + 1) * 256], slice(c * P, (c + 1) * P), slice(0, S_PROMPT)) for c in range(NTP)]
                for dst, q, key in jobs:
                    mm = pe.matmul(dst, qs[0][0:w, s, q], ks[0][0:w, n, key], start=True, stop=True)
                mm.then_inc(a_ready, 1)

            def max_rows(g):
                m = rows_use(g)
                use_before(pe, m)
                pe.transpose(A_PAIR[0:NT, 0, 0:P], mcol[:, :], k.ident[:, :]).then_inc(a_ready, 1)

            def outputs(g):
                use_before(pe, out_use(g))
                pe.wait_ge(o_free, 3 * (g + 1))
                for t in range(NT):
                    mm = pe.transpose(A_PAIR[:, t // 5, t % 5 * VC:t % 5 * VC + VD + 1], oc[:, g % 2, t * P:(t + 1) * P], k.ident[0:VD + 1, 0:VD + 1])
                mm.then_inc(a_ready, 1)

            for i in range(ITEMS):
                maxima(0, i)
            max_rows(0)
            for i in range(EARLY):
                maxima(1, i)
            for g in range(H):
                for u in range(UNITS):
                    scores(g, u)
                    twice = True
                    if g + 1 < H and u == ROWS_AT:
                        max_rows(g + 1)
                    elif g >= 1 and u == OUT_AT:
                        outputs(g - 1)
                    else:
                        twice = False
                    if beside(g, u) and not twice:
                        maxima(*beside(g, u))
                    c = g * UNITS + u - LAG
                    if c >= 0:
                        values(c // UNITS, c % UNITS)
                    if beside(g, u) and twice:
                        maxima(*beside(g, u))
            for u in range(UNITS - LAG, UNITS):
                values(H - 1, u)
            outputs(H - 1)

        @block.scalar
        def _(act):
            def exp(g, u):
                c = g * UNITS + u
                scale = DA ** -0.5 if gqa(g) else DM ** -0.5
                act.wait_ge(s_ready, c + 1)
                if c >= PS:
                    act.wait_ge(p_lo, c - PS + 1)
                w = 512 if u == 0 else 1024
                src = S_BANKS[c % 2][:, :, :].rearrange("p a b -> p (a b)")[:, 0:w]
                act.activation(pf[:, c % PS, 0:w], src, ACT.Exp, scale=scale).then_inc(e_done, 1)
                act.wait_ge(e_done, c + 1)
                if c >= PS:
                    act.wait_ge(pv_done, c - PS + 1)
                act.activation(ph[0][:, c % PS, 0:w], pf[:, c % PS, 0:w], ACT.Copy).then_inc(p_hi, 1)

            def take_outputs(g, part):
                act.wait_ge(pv_done, g * UNITS + (1 if part == 0 else UNITS))
                if part == 0:
                    if g >= 2:
                        act.wait_ge(a_ready, out_use(g - 2) + 1)
                    act.activation(oc[:, g % 2, 0:S_PROMPT], O_PAIR[0:VD + 1, 0, 0:S_PROMPT], ACT.Copy).then_inc(o_free, 1)
                else:
                    for m in range(2):
                        act.activation(oc[:, g % 2, S_PROMPT + m * 512:S_PROMPT + (m + 1) * 512], O_PAIR[0:VD + 1, m, :], ACT.Copy).then_inc(o_free, 1)

            def w_out_hi(j):
                act.wait_ge(gain_in, 32)
                act.wait_ge(wo_in, 16 * (j + 1))
                act.activation(k.wo[0][:, j, :], wo_raw[:, :], ACT.Copy, scale=gain[:, j:j + 1]).then_inc(wo_hi, 1)

            for g in range(H):
                for u in range(UNITS):
                    exp(g, u)
                    if u == 1 and g >= 1:
                        take_outputs(g - 1, 1)
                    if u == 2:
                        take_outputs(g, 0)
                    if u == 7 and g >= HA:
                        w_out_hi(g - HA)
            take_outputs(H - 1, 1)

        @block.vector
        def _(dve):
            def p_low(g, u):
                c = g * UNITS + u
                w = 512 if u == 0 else 1024
                dve.wait_ge(p_hi, c + 1)
                dve.tensor_tensor(ph[1][:, c % PS, 0:w], pf[:, c % PS, 0:w], ph[0][:, c % PS, 0:w], ALU.subtract).then_inc(p_lo, 1)

            def maximum(g, i):
                m = item_use(g, i)
                dve.wait_ge(a_ready, m + 1)
                if i == 0 and g >= 1:
                    dve.wait_ge(a_ready, rows_use(g - 1) + 1)
                if i < ITEMS - 1:
                    dve.reduce_max(mcol[:, NTP + i:NTP + i + 1], a_pair(m)[:, :, :].rearrange("p a b -> p (a b)"), AX.X).then_inc(a_free, 1)
                else:
                    dve.reduce_max(mcol[:, 0:NTP], a_pair(m)[:, 0, :].rearrange("p (a b) -> p a b", a=NTP), AX.X).then_inc(a_free, 1)

            def max_row(g):
                dve.wait_ge(a_ready, rows_use(g) + 1)
                if g >= 1:
                    dve.wait_ge(m_in, 16 * g)
                dve.tensor_scalar(mrow[:, :], A_PAIR[0:NT, 0, 0:P], -1.0, None, ALU.mult).then_inc(m_row, 1)
                dve.wait_ge(m_row, g + 1)
                dve.engine_nop().then_inc(a_free, 1)

            def normalise(g):
                dve.wait_ge(a_ready, out_use(g) + 1)
                if g >= 2:
                    dve.wait_ge(o_out[g % 2], 16 * (g // 2))
                for m in range(2):
                    tr = A_PAIR[:, m, 0:5 * VC].rearrange("p (t c) -> p t c", c=VC)
                    dve.reciprocal(rec[:, 5 * m:5 * m + 5, None], tr[:, :, VD:VD + 1]).then_inc(rec_done, 1)
                    dve.wait_ge(rec_done, 2 * g + m + 1)
                    ins = dve.tensor_tensor(on[:, g % 2, 5 * m:5 * m + 5, :], tr[:, :, 0:VD],
                                            rec[:, 5 * m:5 * m + 5, None].to_broadcast([P, 5, VD]), ALU.mult)
                ins.then_inc(a_free, 1)

            def w_out_low(j):
                dve.wait_ge(wo_hi, j + 1)
                dve.scalar_tensor_tensor(k.wo[1][:, j, :], wo_raw[:, :], gain[:, j:j + 1], k.wo[0][:, j, :], ALU.mult, ALU.subtract).then_inc(wo_lo, 1)

            for i in range(ITEMS):
                maximum(0, i)
            max_row(0)
            for i in range(EARLY):
                maximum(1, i)
            for g in range(H):
                for u in range(UNITS):
                    c = g * UNITS + u - 1
                    if c >= 0:
                        p_low(c // UNITS, c % UNITS)
                    if g + 1 < H and u == ROWS_AT:
                        max_row(g + 1)
                    if g >= 1 and u == OUT_AT:
                        normalise(g - 1)
                    if beside(g, u):
                        maximum(*beside(g, u))
                    if u == 8 and g >= HA:
                        w_out_low(g - HA)
            p_low(H - 1, UNITS - 1)
            normalise(H - 1)


def output(k, stage, block):
    nc = k.nc
    sb = lambda name, shape, dt=F32: k.sb(stage, name, shape, dt)
    modt = sb("mod_mid_t", [P, 2, 2, KT])
    g1 = sb("gate_1", [P, 2, D])
    ln1 = sb("ln1_gain_bias", [P, 2, D])
    ot = sb("o_tile", [P, 3, D])
    junk = sb("squares_c", [P, 512])
    ss = sb("grp_sums", [P, 3, 2])
    mt = [sb(f"mix_t_{s}", [P, 2, KT, P], F32R) for s in ("hi", "lo")]
    y = sb("y", [P, 2, D])
    r = sb("gated_or_x_hat", [P, D])
    uf = sb("u2_f32", [P, KT, P])
    stats = sb("stats_c", [P, 2, 12])
    mv = sb("mean_var_c", [P, 2, 2])
    std = sb("std_c", [P, 2, 1])

    tabs_in, modp = k.sem("oc_tabs_in"), k.sem("oc_mod_plus_one")
    o_in, x_in = [k.sem(f"oc_o_in{s}") for s in range(3)], [k.sem(f"oc_x_in{s}") for s in range(2)]
    ss_ready, on_ready = k.sem("ss_ready"), k.sem("on_ready")
    mt_tr, mt_hi, mt_lo = k.sem("mt_tr"), k.sem("mt_hi"), k.sem("mt_lo")
    mix_ready, mix_free = k.sem("mix_ready"), k.sem("mix_free")
    var_ready, std_ready = k.sem("oc_var"), k.sem("oc_std")
    x1_ready, x1_out = k.sem("x1_ready"), [k.sem(f"x1_out{s}") for s in range(2)]
    xh_ready, u_tr, uf_ready, u2_hi, u2_ready = (k.sem(n) for n in ("oc_xhat", "oc_u_tr", "oc_uf", "u2_hi_ready", "u2_ready"))
    dv, ac = k.sem("oc_dve_link"), k.sem("oc_act_link")
    TURNS = range(NT + 3)
    k.mix_ready, k.mix_free, k.uf_ready, k.u2_ready, k.x1_out = mix_ready, mix_free, uf_ready, u2_ready, x1_out

    @block.sync
    def _(sp):
        def load_o(t):
            sp.dma_start(ot[:, t % 3, :], k.o[t * P:(t + 1) * P, :]).then_inc(o_in[t % 3], 16)

        def load_x(t):
            sp.dma_start(y[:, t % 2, :], xrow(k, t)).then_inc(x_in[t % 2], 16)

        for t in range(3):
            load_o(t)
        with nc.allow_non_contiguous_dma(reason="columns of the modulation, once"):
            for s in range(2):
                for m, part in enumerate((4, 3)):
                    sp.dma_start(modt[:, s, m, :], k.mod[s, part * D:(part + 1) * D].rearrange("(j p) -> p j", p=P)).then_inc(tabs_in, 16)
        for t in range(2):
            load_x(t)
        for s in range(2):
            sp.dma_start(g1[:, s, :], k.mod[s, 2 * D:3 * D].partition_broadcast(P)).then_inc(tabs_in, 16)
        for m, g in enumerate(("ln1_g", "ln1_b")):
            sp.dma_start(ln1[:, m, :], k.i[g][0, :].partition_broadcast(P)).then_inc(tabs_in, 16)
        for n in TURNS:
            if n + 3 < NT:
                sp.wait_ge(mt_tr, 2 * (n + 1))
                load_o(n + 3)
            t = n - 2
            if 0 <= t < NT:
                sp.wait_ge(x1_ready, t + 1)
                sp.dma_start(k.x1[t * P:(t + 1) * P, :], y[:, t % 2, :]).then_inc(x1_out[t % 2], 16)
                if t + 2 < NT:
                    sp.wait_ge(x1_out[t % 2], 16 * (t // 2 + 1))
                    sp.wait_ge(xh_ready, t + 1)
                    load_x(t + 2)
        for s in range(2):
            sp.wait_ge(x1_out[s], 16 * (NT // 2))

    @block.tensor
    def _(pe):
        def mix_t(t):
            pe.wait_ge(on_ready, t + 1)
            for m in range(2):
                if t >= 1:
                    pe.wait_ge(mt_lo, 2 * (t - 1) + m + 1)
                for q in range(4):
                    j = 4 * m + q
                    mm = pe.transpose(bank(k, m)[:, q * P:(q + 1) * P], ot[:, t % 3, j * P:(j + 1) * P], k.ident[:, :])
                mm.then_inc(mt_tr, 1)

        def mix(t):
            pe.wait_ge(mt_lo, 2 * (t + 1))
            if t >= 2:
                pe.wait_ge(mix_free, t - 1)
            out = k.bank[1 + t % 2]
            for m in range(2):
                for j in range(KT):
                    mm = three(pe, out[:, m, :], [x[:, t % 2, j, :] for x in mt],
                               [w[:, j, m * 512:(m + 1) * 512] for w in k.wo], j == 0, j == KT - 1)
            mm.then_inc(mix_ready, 1)

        def u_t(t):
            pe.wait_ge(xh_ready, t + 1)
            if t >= 1:
                pe.wait_ge(uf_ready, t)
            for j in range(KT):
                mm = pe.transpose(k.bank[3][:, j // 4, j % 4 * P:(j % 4 + 1) * P], r[:, j * P:(j + 1) * P], k.ident[:, :])
            mm.then_inc(u_tr, 1)

        k.last_u_t = lambda: u_t(NT - 1)
        for n in TURNS:
            if 0 <= n - 3 < NT - 1:
                u_t(n - 3)
            if n < NT:
                mix_t(n)
            if 0 <= n - 1 < NT:
                mix(n - 1)

    @block.scalar
    def _(act):
        def squares(t):
            act.wait_ge(o_in[t % 3], 16 * (t // 3 + 1))
            for m in range(2):
                ins = act.activation(junk[:, :], ot[:, t % 3, m * 512:(m + 1) * 512], ACT.Square, accum_out=ss[:, t % 3, m:m + 1])
                ins.then_inc(ac, 1)
                act.wait_ge(ac, 2 * t + m + 1)
            act.activation(ss[:, t % 3, :], ss[:, t % 3, :], ACT.Sqrt, scale=1.0 / 512, bias=k.eps[:, 0:1]).then_inc(ss_ready, 1)

        def mix_hi(t):
            for m in range(2):
                act.wait_ge(mt_tr, 2 * t + m + 1)
                if m == 0 and t >= 2:
                    act.wait_ge(mix_ready, t - 1)
                act.activation(mt[0][:, t % 2, 4 * m:4 * m + 4, :], bank(k, m).rearrange("p (q c) -> p q c", c=P), ACT.Copy).then_inc(mt_hi, 1)

        def root(t, which):
            act.wait_ge(var_ready, 2 * t + which + 1)
            act.activation(std[:, which, :], mv[:, which, 1:2], ACT.Sqrt, bias=k.eps[:, 0:1]).then_inc(std_ready, 1)

        def modulate(t):
            act.wait_ge(u_tr, t + 1)
            if t == 0:
                act.wait_ge(modp, 1)
            if t >= 1:
                act.wait_ge(u2_ready, t)
            seq = 0 if t < NTP else 1
            for j in range(KT):
                ins = act.activation(uf[:, j, :], k.bank[3][:, j // 4, j % 4 * P:(j % 4 + 1) * P], ACT.Identity,
                                     bias=modt[:, seq, 1, j:j + 1], scale=modt[:, seq, 0, j:j + 1])
            ins.then_inc(uf_ready, 1)
            act.wait_ge(uf_ready, t + 1)
            act.activation(k.u2[0][:, :, t * P:(t + 1) * P], uf[:, :, :], ACT.Copy).then_inc(u2_hi, 1)

        squares(0)
        squares(1)
        for n in TURNS:
            if n == NT + 1:
                act.wait_ge(mix_ready, NT)
                for m, name in enumerate(("w_gate", "w_up")):
                    act.dma_start(k.raw_gu[:, m, :, :], rows(k.i[name][0])[:, :, 0:P]).then_inc(k.gu_in, 16)
                act.dma_start(k.raw_d[:, :], k.i["w_down"][0][0:P, :]).then_inc(k.down_in, 16)
            if 0 <= n - 3 < NT:
                modulate(n - 3)
            if n < NT:
                mix_hi(n)
            if 0 <= n - 2 < NT:
                root(n - 2, 0)
            if n + 2 < NT:
                squares(n + 2)
            if n == NT + 1:
                act.wait_ge(k.gu_in, 32)
                act.activation(k.wgu[0][:, 0, :, :, :], k.raw_gu[:, :, :, :], ACT.Copy).then_inc(k.gu_hi, 1)
            if 0 <= n - 2 < NT:
                root(n - 2, 1)

    @block.vector
    def _(dve):
        link = Link(dve, dv)

        def group_norm(t):
            dve.wait_ge(ss_ready, t + 1)
            link(dve.reciprocal(ss[:, t % 3, :], ss[:, t % 3, :]))
            for m in range(2):
                ins = dve.tensor_scalar(ot[:, t % 3, m * 512:(m + 1) * 512], ot[:, t % 3, m * 512:(m + 1) * 512],
                                        ss[:, t % 3, m:m + 1], None, ALU.mult)
            ins.then_inc(on_ready, 1)

        def mix_lo(t):
            for m in range(2):
                dve.wait_ge(mt_hi, 2 * t + m + 1)
                dve.tensor_tensor(mt[1][:, t % 2, 4 * m:4 * m + 4, :], bank(k, m).rearrange("p (q c) -> p q c", c=P),
                                  mt[0][:, t % 2, 4 * m:4 * m + 4, :], ALU.subtract).then_inc(mt_lo, 1)

        def moments(t, which):
            for m in range(2):
                link(dve.bn_stats(stats[:, which, 6 * m:6 * m + 6], y[:, t % 2, m * 512:(m + 1) * 512]))
            dve.bn_aggr(mv[:, which, :], stats[:, which, :]).then_inc(var_ready, 1)

        def norm(t, which, out):
            dve.wait_ge(var_ready, 2 * t + which + 1)
            dve.wait_ge(std_ready, 2 * t + which + 1)
            link(dve.reciprocal(std[:, which, :], std[:, which, :]))
            return dve.tensor_scalar(out, y[:, t % 2, :], mv[:, which, 0:1], std[:, which, :], ALU.subtract, ALU.mult)

        def residual(t):
            seq = 0 if t < NTP else 1
            dve.wait_ge(mix_ready, t + 1)
            if t >= 1:
                dve.wait_ge(u_tr, t)
            dve.tensor_tensor(r[:, :], k.bank[1 + t % 2][:, :, :].rearrange("p a b -> p (a b)"), g1[:, seq, :], ALU.mult).then_inc(mix_free, 1)
            dve.wait_ge(mix_free, t + 1)
            dve.wait_ge(x_in[t % 2], 16 * (t // 2 + 1))
            link(dve.scalar_tensor_tensor(y[:, t % 2, :], y[:, t % 2, :], ALPHA, r[:, :], ALU.mult, ALU.add))
            moments(t, 0)

        def first_norm(t):
            yt = y[:, t % 2, :]
            link(norm(t, 0, yt))
            link(dve.tensor_tensor(yt, yt, ln1[:, 0, :], ALU.mult))
            dve.tensor_tensor(yt, yt, ln1[:, 1, :], ALU.add).then_inc(x1_ready, 1)
            dve.wait_ge(x1_ready, t + 1)
            moments(t, 1)

        def u_low(t):
            cols = slice(t * P, (t + 1) * P)
            dve.wait_ge(u2_hi, t + 1)
            dve.tensor_tensor(k.u2[1][:, :, cols], uf[:, :, :], k.u2[0][:, :, cols], ALU.subtract).then_inc(u2_ready, 1)

        group_norm(0)
        for n in TURNS:
            if n + 1 < NT:
                group_norm(n + 1)
            if n == 0:
                dve.wait_ge(tabs_in, 128)
                for s in range(2):
                    ins = dve.tensor_scalar(modt[:, s, 0, :], modt[:, s, 0, :], 1.0, None, ALU.add)
                ins.then_inc(modp, 1)
            if 0 <= n - 2 < NT:
                residual(n - 2)
            if n < NT:
                mix_lo(n)
            if 0 <= n - 2 < NT:
                first_norm(n - 2)
            if n == NT + 1:
                dve.wait_ge(k.gu_hi, 1)
                dve.tensor_tensor(k.wgu[1][:, 0, :, :, :], k.raw_gu[:, :, :, :], k.wgu[0][:, 0, :, :, :], ALU.subtract).then_inc(k.gu_lo, 1)
            if 0 <= n - 3 < NT:
                u_low(n - 3)
            if 0 <= n - 2 < NT:
                norm(n - 2, 1, r[:, :]).then_inc(xh_ready, 1)


def channel(k, stage, block):
    nc = k.nc
    sb = lambda name, shape, dt=F32: k.sb(stage, name, shape, dt)
    sumf = sb("sum_f", [P, NT, D])
    raw_gu, raw_d, wgu, wd, sg, hf = k.raw_gu, k.raw_d, k.wgu, k.wd, k.sg, k.hf
    hid = [sb(f"hidden_{s}", [P, TOK], F32R) for s in ("hi", "lo")]
    g2 = sb("gate_2", [P, 2, D])
    row_sum = sb("row_sum", [P, NT])
    neg_mean = sb("neg_mean", [P, NT])
    sq_sum = sb("square_sum", [P, NT])
    std = sb("std_e", [P, NT])
    k.u2_memory.close()
    right = lambda name, shape: k.sb(k.u2_memory, name, shape, side="right")
    z = right("z", [P, NT, D])
    ln2 = right("ln2_gain_bias", [P, 2, D])
    junk = right("stats_scratch", [P, D])
    x1 = [raw_gu[:, m, :, :].rearrange("p a b -> p (a b)") for m in range(2)]
    gu_in, d_in, gu_hi, gu_lo = k.gu_in, k.down_in, k.gu_hi, k.gu_lo
    d_hi, d_lo = k.sem("down_hi"), k.sem("down_lo")
    gu_ready, silu_done, h_ready, hid_hi, hid_lo = (k.sem(n) for n in ("gu_ready", "silu_done", "ff_h", "hid_hi", "hid_lo"))
    dn_ready, dn_added = k.sem("down_ready"), k.sem("down_added")
    g2_in, ln2_in, merged = (k.sem(n) for n in ("gate_2_in", "ln2_in", "x1_merged"))
    x1_in = [k.sem(f"x1_in{s}") for s in range(2)]
    y_ready, std_ready, centred, scaled, out_ready, stored = (k.sem(n) for n in ("e_y", "e_std", "e_centred", "e_scaled", "e_out", "e_stored"))
    ac, x1_scaled, gated = k.sem("e_act_link"), k.sem("x1_scaled"), k.sem("sum_gated")
    TILES = [range(c[0] // P, c[1] // P) for c in CHUNKS]
    NCH = len(CHUNKS)
    assert NF % 2 == 0 and NF >= 6

    def run(eng, body):
        body(0, 0, True)
        body(1, 1, False)
        with eng.Fori(2, NF - 2, 2) as i:
            body(i, 0, False)
            body(i + 1, 1, False)
        body(NF - 2, 0, False)
        body(NF - 1, 1, False)
        body(NF, 0, False, last=True)

    def prev(f, c):
        return (c - 1) % NCH, NCH * f + c

    def after_output(eng):
        eng.wait_ge(k.u2_ready, NT)
        for s in range(2):
            eng.wait_ge(k.x1_out[s], 16 * (NT // 2))

    @block.sync
    def _(sp):
        wg, wu, w_dn = rows(k.i["w_gate"][0]), rows(k.i["w_up"][0]), rows(k.i["w_down"][0])

        def load(f):
            sp.wait_ge(gu_lo, f)
            for m, w in enumerate((k.i["w_gate"][0], k.i["w_up"][0])):
                sp.dma_start(raw_gu[:, m, :, :], rows(w)[:, :, bass.ds(f * P, P)]).then_inc(gu_in, 16)
            sp.wait_ge(d_lo, f)
            sp.dma_start(raw_d[:, :], k.i["w_down"][0][bass.ds(f * P, P), :]).then_inc(d_in, 16)

        load(1)
        with sp.Fori(2, NF) as f:
            load(f)
        sp.wait_ge(gu_lo, NF)
        for t in range(NT):
            if t >= 2:
                sp.wait_ge(merged, t - 1)
            sp.dma_start(x1[t % 2], k.x1[t * P:(t + 1) * P, :]).then_inc(x1_in[t % 2], 16)
        for t in range(NT):
            sp.wait_ge(out_ready, t + 1)
            sp.dma_start(k.o_prompt(t) if t < NTP else k.o_sample(t - NTP), z[:, t, :]).then_inc(stored, 16)
        sp.wait_ge(stored, 16 * NT)

    @block.gpsimd
    def _(pool):
        after_output(pool)
        for s in range(2):
            pool.dma_start(g2[:, s, :], k.mod[s, 5 * D:6 * D].partition_broadcast(P)).then_inc(g2_in, 16)
        for t in range(NT):
            pool.wait_ge(x1_in[t % 2], 16 * (t // 2 + 1))
            pool.tensor_scalar(x1[t % 2], x1[t % 2], ALPHA, None, ALU.mult).then_inc(x1_scaled, 1)
            pool.wait_ge(x1_scaled, t + 1)
            pool.wait_ge(gated, t + 1)
            pool.tensor_tensor(sumf[:, t, :], sumf[:, t, :], x1[t % 2], ALU.add).then_inc(merged, 1)
        pool.wait_ge(ln2_in, 32)
        for t in range(NT):
            pool.wait_ge(scaled, t + 1)
            pool.tensor_tensor(z[:, t, :], z[:, t, :], ln2[:, 1, :], ALU.add).then_inc(out_ready, 1)

    @block.tensor
    def _(pe):
        def down(f, t, slot):
            if not (isinstance(f, int) and f == 1 and t < 2):
                pe.wait_ge(dn_added, NT * (f - 1) + t - 1)
            for m in range(2):
                mm = three(pe, k.bank[2 + t % 2][:, m, :], [x[:, t * P:(t + 1) * P] for x in hid],
                           [w[:, 1 - slot, m * 512:(m + 1) * 512] for w in wd], True, True)
            mm.then_inc(dn_ready, 1)

        def body(f, slot, first, last=False):
            for c, (lo, hi) in enumerate(CHUNKS):
                if not first:
                    pe.wait_ge(hid_lo, NCH * (f - 1) + c + 1)
                    if c == 0:
                        pe.wait_ge(d_lo, f)
                    for t in TILES[c]:
                        down(f, t, slot)
                if last:
                    continue
                if c == 0:
                    pe.wait_ge(gu_lo, f + 1)
                out = k.bank[(slot + c) % 2]
                if not (first and c < 2):
                    pe.wait_ge(h_ready, NCH * f + c - 1)
                if first:
                    pe.wait_ge(k.u2_ready, TILES[c][-1] + 1)
                    if c == 1:
                        pe.wait_ge(k.mix_free, NT)
                for m in range(2):
                    for j in range(KT):
                        mm = three(pe, out[:, m, 0:hi - lo], [w[:, slot, m, j, :] for w in wgu],
                                   [x[:, j, lo:hi] for x in k.u2], j == 0, j == KT - 1)
                mm.then_inc(gu_ready, 1)
                if first and c == 0:
                    k.last_u_t()
                if first and c == NCH - 1:
                    pe.wait_ge(k.uf_ready, NT)

        run(pe, body)

    @block.scalar
    def _(act):
        def gu_round(f, slot, first):
            act.wait_ge(gu_in, 32 * (f + 1))
            if not first:
                act.wait_ge(gu_ready, NCH * (f - 1))
            act.activation(wgu[0][:, slot, :, :, :], raw_gu[:, :, :, :], ACT.Copy).then_inc(gu_hi, 1)

        def d_round(f, slot, first):
            act.wait_ge(d_in, 16 * (f + 1))
            if not first:
                act.wait_ge(dn_ready, NT * (f - 1))
            act.activation(wd[0][:, slot, :], raw_d[:, :], ACT.Copy).then_inc(d_hi, 1)

        def silu(f, c, slot):
            pc, m = prev(f, c)
            lo, hi = CHUNKS[pc]
            act.wait_ge(gu_ready, m)
            if not (isinstance(m, int) and m == 1):
                act.wait_ge(h_ready, m - 1)
            act.activation(sg[:, 0:hi - lo], k.bank[(slot + c + 1) % 2][:, 0, 0:hi - lo], ACT.Silu).then_inc(silu_done, 1)
            act.wait_ge(h_ready, m)
            if not (isinstance(f, int) and (f == 0 or (f == 1 and c == 0))):
                act.wait_ge(dn_ready, NT * (f - 1 - (c == 0)) + TILES[pc][-1] + 1)
            act.activation(hid[0][:, lo:hi], hf[:, 0:hi - lo], ACT.Copy).then_inc(hid_hi, 1)

        after_output(act)

        def body(f, slot, first, last=False):
            for c in range(NCH):
                if not (first and c == 0) and not (last and c > 0):
                    silu(f, c, slot)
                if last and c == 0:
                    for m, g in enumerate(("ln2_g", "ln2_b")):
                        act.dma_start(ln2[:, m, :], k.i[g][0, :].partition_broadcast(P)).then_inc(ln2_in, 16)
                if last:
                    continue
                if c == 1:
                    d_round(f, slot, isinstance(f, int) and f < 2)
                if c == 2:
                    if not (isinstance(f, int) and f == NF - 1):
                        gu_round(f + 1, 1 - slot, isinstance(f, int) and f == 0)

        def statistics(t):
            act.wait_ge(y_ready, t + 1)
            act.activation(junk[:, :], z[:, t, :], ACT.Copy, accum_out=row_sum[:, t:t + 1]).then_inc(ac, 1)
            act.wait_ge(ac, 3 * t + 1)
            act.activation(neg_mean[:, t:t + 1], row_sum[:, t:t + 1], ACT.Copy, scale=-1.0 / D).then_inc(ac, 1)
            act.wait_ge(ac, 3 * t + 2)
            act.activation(junk[:, :], z[:, t, :], ACT.Square, bias=neg_mean[:, t:t + 1], accum_out=sq_sum[:, t:t + 1]).then_inc(ac, 1)
            act.wait_ge(ac, 3 * t + 3)
            act.activation(std[:, t:t + 1], sq_sum[:, t:t + 1], ACT.Sqrt, scale=1.0 / D, bias=k.eps[:, 0:1]).then_inc(std_ready, 1)

        run(act, body)
        for n in range(NT + 1):
            if n < NT:
                statistics(n)
            if n >= 1:
                t = n - 1
                act.wait_ge(centred, t + 1)
                act.activation(z[:, t, :], z[:, t, :], ACT.Copy, scale=std[:, t:t + 1]).then_inc(scaled, 1)

    @block.vector
    def _(dve):
        def gu_low(f, slot):
            dve.wait_ge(gu_hi, f + 1)
            dve.tensor_tensor(wgu[1][:, slot, :, :, :], raw_gu[:, :, :, :], wgu[0][:, slot, :, :, :], ALU.subtract).then_inc(gu_lo, 1)

        def d_low(f, slot):
            dve.wait_ge(d_hi, f + 1)
            dve.tensor_tensor(wd[1][:, slot, :], raw_d[:, :], wd[0][:, slot, :], ALU.subtract).then_inc(d_lo, 1)

        def product(f, c, slot):
            pc, m = prev(f, c)
            lo, hi = CHUNKS[pc]
            dve.wait_ge(silu_done, m)
            if not (isinstance(m, int) and m == 1):
                dve.wait_ge(hid_lo, m - 1)
            dve.tensor_tensor(hf[:, 0:hi - lo], k.bank[(slot + c + 1) % 2][:, 1, 0:hi - lo], sg[:, 0:hi - lo], ALU.mult).then_inc(h_ready, 1)

        def hidden_low(f, c):
            pc, m = prev(f, c)
            lo, hi = CHUNKS[pc]
            dve.wait_ge(hid_hi, m)
            dve.tensor_tensor(hid[1][:, lo:hi], hf[:, 0:hi - lo], hid[0][:, lo:hi], ALU.subtract).then_inc(hid_lo, 1)

        def gate(t):
            if t == 0:
                dve.wait_ge(g2_in, 32)
            dve.wait_ge(dn_added, NT * (NF - 2) + t + 1)
            dve.tensor_tensor(sumf[:, t, :], sumf[:, t, :], g2[:, int(t >= NTP), :], ALU.mult).then_inc(gated, 1)

        def last_add(t):
            dve.wait_ge(dn_ready, NT * (NF - 1) + t + 1)
            dve.tensor_tensor(z[:, t, :], k.bank[2 + t % 2][:, :, :].rearrange("p a b -> p (a b)"), g2[:, int(t >= NTP), :], ALU.mult).then_inc(dn_added, 1)
            dve.wait_ge(dn_added, NT * (NF - 1) + t + 1)
            dve.wait_ge(merged, t + 1)
            dve.tensor_tensor(z[:, t, :], z[:, t, :], sumf[:, t, :], ALU.add).then_inc(y_ready, 1)

        def centre(t):
            dve.wait_ge(std_ready, t + 1)
            dve.reciprocal(std[:, t:t + 1], std[:, t:t + 1])
            if t == 0:
                dve.wait_ge(ln2_in, 32)
            dve.wait_ge(y_ready, t + 1)
            dve.scalar_tensor_tensor(z[:, t, :], z[:, t, :], neg_mean[:, t:t + 1], ln2[:, 0, :], ALU.add, ALU.mult).then_inc(centred, 1)

        def add(f, t):
            dve.wait_ge(dn_ready, NT * (f - 1) + t + 1)
            src = k.bank[2 + t % 2][:, :, :].rearrange("p a b -> p (a b)")
            if isinstance(f, int) and f == 1:
                dve.tensor_copy(sumf[:, t, :], src).then_inc(dn_added, 1)
            else:
                dve.wait_ge(dn_added, NT * (f - 2) + t + 1)
                dve.tensor_tensor(sumf[:, t, :], src, sumf[:, t, :], ALU.add).then_inc(dn_added, 1)

        after_output(dve)

        def body(f, slot, first, last=False):
            for c in range(NCH):
                before = not (first and c == 0) and not (last and c > 0)
                tiles = [] if first else list(TILES[c])
                for q in range(max(len(tiles), 2)):
                    if q < len(tiles):
                        t = tiles[q]
                        if last:
                            last_add(t)
                        else:
                            add(f, t)
                        if isinstance(f, int) and f == NF - 1:
                            gate(t)
                    if before and q == 0:
                        product(f, c, slot)
                    if before and q == 1:
                        hidden_low(f, c)
                    if last and q < len(tiles) and t >= 1:
                        centre(t - 1)
                if last:
                    continue
                if c == 1:
                    d_low(f, slot)
                if c == 2:
                    if not (isinstance(f, int) and f == NF - 1):
                        gu_low(f + 1, 1 - slot)

        run(dve, body)
        centre(NT - 1)


_INS = ["x_prompt", "x_sample", "c_prompt", "c_sample", "w_ada", "b_ada", "w_in", "gqa_q_norm", "gqa_k_norm",
        "mla_q_norm", "w_uq", "mla_kv_norm", "w_ukv", "grp_norm_a", "grp_norm_b", "w_out", "ln1_g", "ln1_b",
        "w_gate", "w_up", "w_down", "ln2_g", "ln2_b"]
_OUTS = [("y_prompt", (1, 256, 1024)), ("y_sample", (1, 1024, 1024))]


def _tables():
    import numpy as np

    row = np.repeat(np.arange(1024 // 64, dtype=np.float32), 64)
    col = np.tile(np.arange(64, dtype=np.float32), 1024 // 64)
    parts = []
    for dim in (64, 32):
        n = dim // 4
        freq = (1.0 / np.power(np.float32(10000.0), np.arange(n, dtype=np.float32) / np.float32(n))).astype(np.float32)
        ang = np.concatenate([row[:, None] * freq, col[:, None] * freq], axis=-1).astype(np.float32)
        parts += [np.cos(ang), np.sin(ang)]
    inv_n = np.array([1 / 64] * 10 + [1 / 256, 1 / 128], np.float32)
    return {"ident": np.eye(128, dtype=np.float32), "rope": np.concatenate(parts, 1).astype(np.float32), "inv_n": inv_n}


def kernel(**inputs):
    import numpy as _np
    import concourse.bacc as _bacc
    from concourse import mybir as _mybir
    from concourse.bass_utils import run_bass_kernel_spmd as _run

    nc = _bacc.Bacc("TRN2", target_bir_lowering=False, num_devices=1)
    arrays = {name: _np.ascontiguousarray(inputs[name]) for name in _INS}
    arrays.update(_tables())
    ins = {n: nc.dram_tensor(f"in_{n}", a.shape, _mybir.dt.from_np(a.dtype), kind="ExternalInput").ap() for n, a in arrays.items()}
    outs = {n: nc.dram_tensor(f"out_{n}", s, _mybir.dt.float32, kind="ExternalOutput").ap() for n, s in _OUTS}
    encoder_layer(nc, ins, outs)
    r = _run(nc, [{f"in_{n}": a for n, a in arrays.items()}], core_ids=[0])
    return tuple(r.results[0][f"out_{n}"] for n, _ in _OUTS)
```
